# Optimizing a Trainium2 kernel written in Bass

```python
import jax, jax.numpy as jnp
from jax import lax
import numpy as np

D_MODEL = 1024
BATCH = 1
SEQ = 256
DEPTH = 2

GRID_W = 64
CTX_LEN = 256
N_HEADS = 16
QK_NOPE = 64
QK_ROPE = 32
ROPE_FREQS = QK_ROPE // 4
V_HEAD = 64
Q_LORA = 256
KV_LORA = 128
ROPE_THETA = 10000.0
ATTN_DIM = N_HEADS * V_HEAD
SM_SCALE = (QK_NOPE + QK_ROPE) ** -0.5
Q_BLOCK = 128
F_GROUPS = 4
F_GROUP_DIM = 128
FOURIER_DIM = F_GROUPS * F_GROUP_DIM
OFF_KV = Q_LORA
OFF_KR = OFF_KV + KV_LORA
OFF_F = OFF_KR + QK_ROPE
OFF_G = OFF_F + FOURIER_DIM
IN_COLS = OFF_G + 2 * D_MODEL
D_FF = 2816
N_EXPERTS = 8
TOP_K = 2
D_FF_EXPERT = 3584
N_DENSE = (DEPTH + 1) // 2
N_MOE = DEPTH // 2
ALPHA = (2 * DEPTH) ** 0.25
BETA = (8 * DEPTH) ** -0.25
LN_EPS = 1e-6
RMS_EPS = 1e-6

kernel_name = "hybrid_mla_fnet_moe_diffusion_block"

def _layer_norm_f32(x):
    xf = x.astype(jnp.float32)
    mu = jnp.mean(xf, axis=-1, keepdims=True)
    var = jnp.mean(jnp.square(xf - mu), axis=-1, keepdims=True)
    return (xf - mu) * lax.rsqrt(var + LN_EPS)

def ln_affine(x, g, b):
    return (_layer_norm_f32(x) * g + b).astype(x.dtype)

def ln_modulate(x, shift, scale):
    return (_layer_norm_f32(x) * (1.0 + scale) + shift).astype(x.dtype)

def rms_norm(x, g):
    xf = x.astype(jnp.float32)
    y = xf * lax.rsqrt(jnp.mean(jnp.square(xf), axis=-1, keepdims=True) + RMS_EPS)
    return (y * g).astype(x.dtype)

def axial_rope_tables(n_tokens):
    n_rows = n_tokens // GRID_W
    rows = jnp.repeat(jnp.arange(n_rows), GRID_W)
    cols = jnp.tile(jnp.arange(GRID_W), n_rows)
    pos = jnp.stack([rows, cols], axis=-1).astype(jnp.float32)
    inv_freq = 1.0 / (ROPE_THETA ** (jnp.arange(ROPE_FREQS, dtype=jnp.float32) / ROPE_FREQS))
    ang = pos[..., None] * inv_freq
    return jnp.cos(ang), jnp.sin(ang)

def rope_2d(x, cos, sin):
    xs = x.reshape(x.shape[:-1] + (2, 2, ROPE_FREQS))
    x1, x2 = xs[..., 0, :], xs[..., 1, :]
    c, s = cos.astype(x.dtype), sin.astype(x.dtype)
    out = jnp.stack([x1 * c - x2 * s, x2 * c + x1 * s], axis=-2)
    return out.reshape(x.shape)

def mla_queries(proj, g_q, w_uq, rope):
    lead = proj.shape[:-1]
    q = (rms_norm(proj[..., :Q_LORA], g_q) @ w_uq).reshape(lead + (N_HEADS, QK_NOPE + QK_ROPE))
    qn, qr = q[..., :QK_NOPE], q[..., QK_NOPE:]
    if rope is not None:
        cos, sin = rope
        qr = rope_2d(qr, cos[:, None], sin[:, None])
    return qn, qr

def mla_keys(kv_proj, g_kv, w_uk, w_uv, rope):
    lead = kv_proj.shape[:-1]
    ckv = rms_norm(kv_proj[..., :KV_LORA], g_kv)
    kr = kv_proj[..., KV_LORA:]
    kn = (ckv @ w_uk).reshape(lead + (N_HEADS, QK_NOPE))
    v = (ckv @ w_uv).reshape(lead + (N_HEADS, V_HEAD))
    if rope is not None:
        cos, sin = rope
        kr = rope_2d(kr, cos, sin)
    return kn, kr, v

def attend(qn, qr, kn, kr, v):
    s = jnp.einsum('bqhd,bkhd->bhqk', qn, kn) + jnp.einsum('bqhr,bkr->bhqk', qr, kr)
    p = jax.nn.softmax(s.astype(jnp.float32) * SM_SCALE, axis=-1).astype(v.dtype)
    return jnp.einsum('bhqk,bkhd->bqhd', p, v)

def latent_attention(qn, qr, kn_all, kr_all, v_all):
    b, n = qn.shape[:2]
    nb = n // Q_BLOCK

    def to_blocks(t):
        return jnp.moveaxis(t.reshape((b, nb, Q_BLOCK) + t.shape[2:]), 1, 0)

    out = lax.map(lambda qs: attend(qs[0], qs[1], kn_all, kr_all, v_all), (to_blocks(qn), to_blocks(qr)))
    return jnp.moveaxis(out, 0, 1).reshape(b, n, ATTN_DIM)

def fourier_mix(u):
    b, n, _ = u.shape
    ug = u.reshape(b, n, F_GROUPS, F_GROUP_DIM).astype(jnp.float32)
    z = jnp.fft.fft2(ug, axes=(1, 3), norm="ortho")
    return jnp.real(z).astype(u.dtype).reshape(b, n, FOURIER_DIM)

def mixer_out(proj, attn, w_ao, w_fo, w_out):
    four = fourier_mix(proj[..., OFF_F:OFF_G])
    g_a = jax.nn.sigmoid(proj[..., OFF_G:OFF_G + D_MODEL])
    g_f = jax.nn.sigmoid(proj[..., OFF_G + D_MODEL:])
    merged = g_a * (attn @ w_ao) + g_f * (four @ w_fo)
    return merged @ w_out

def swiglu(h, wg, wu, wd):
    return (jax.nn.silu(h @ wg) * (h @ wu)) @ wd

def moe_ffn(h, w_router, b_router, wg, wu, wd):
    shape = h.shape
    t = h.reshape(-1, shape[-1])
    logits = (t @ w_router).astype(jnp.float32) + b_router.astype(jnp.float32)
    top_v, top_i = lax.top_k(logits, TOP_K)
    w = jax.nn.softmax(top_v, axis=-1)
    combine = jnp.sum(jax.nn.one_hot(top_i, N_EXPERTS, dtype=jnp.float32) * w[..., None], axis=1).astype(h.dtype)
    out = jnp.zeros_like(t)
    for e in range(N_EXPERTS):
        out = out + combine[:, e:e + 1] * swiglu(t, wg[e], wu[e], wd[e])
    return out.reshape(shape)

def setup_inputs(seed: int = 0) -> dict:
    key = jax.random.key(seed)
    ks = jax.random.split(key, 32)

    def nrm(k, shape, scale):
        return jax.random.normal(k, shape, jnp.float32) * scale

    D = D_MODEL
    return {
        "x": nrm(ks[0], (BATCH, SEQ, D), 1.0),
        "c": nrm(ks[1], (BATCH, D), 1.0),
        "ctx": nrm(ks[2], (BATCH, CTX_LEN, D), 1.0),
        "c_ctx": nrm(ks[3], (D,), 1.0),
        "w_mod": nrm(ks[4], (DEPTH, D, 6 * D), 0.5 * D ** -0.5),
        "b_mod": nrm(ks[5], (DEPTH, 6 * D), 0.02),
        "w_in": nrm(ks[6], (DEPTH, D, IN_COLS), D ** -0.5),
        "g_q": 1.0 + nrm(ks[7], (DEPTH, Q_LORA), 0.02),
        "w_uq": nrm(ks[8], (DEPTH, Q_LORA, N_HEADS * (QK_NOPE + QK_ROPE)), Q_LORA ** -0.5),
        "g_kv": 1.0 + nrm(ks[9], (DEPTH, KV_LORA), 0.02),
        "w_uk": nrm(ks[10], (DEPTH, KV_LORA, N_HEADS * QK_NOPE), KV_LORA ** -0.5),
        "w_uv": nrm(ks[11], (DEPTH, KV_LORA, N_HEADS * V_HEAD), BETA * KV_LORA ** -0.5),
        "w_ao": nrm(ks[12], (DEPTH, ATTN_DIM, D), ATTN_DIM ** -0.5),
        "w_fo": nrm(ks[13], (DEPTH, FOURIER_DIM, D), BETA * FOURIER_DIM ** -0.5),
        "w_out": nrm(ks[14], (DEPTH, D, D), BETA * D ** -0.5),
        "ln1_g": 1.0 + nrm(ks[15], (DEPTH, D), 0.02),
        "ln1_b": nrm(ks[16], (DEPTH, D), 0.02),
        "ln2_g": 1.0 + nrm(ks[17], (DEPTH, D), 0.02),
        "ln2_b": nrm(ks[18], (DEPTH, D), 0.02),
        "w_ff_gate": nrm(ks[19], (N_DENSE, D, D_FF), D ** -0.5),
        "w_ff_up": nrm(ks[20], (N_DENSE, D, D_FF), BETA * D ** -0.5),
        "w_ff_down": nrm(ks[21], (N_DENSE, D_FF, D), BETA * D_FF ** -0.5),
        "w_router": nrm(ks[22], (N_MOE, D, N_EXPERTS), D ** -0.5),
        "b_router": nrm(ks[23], (N_MOE, N_EXPERTS), 0.01),
        "w_e_gate": nrm(ks[24], (N_MOE, N_EXPERTS, D, D_FF_EXPERT), D ** -0.5),
        "w_e_up": nrm(ks[25], (N_MOE, N_EXPERTS, D, D_FF_EXPERT), BETA * D ** -0.5),
        "w_e_down": nrm(ks[26], (N_MOE, N_EXPERTS, D_FF_EXPERT, D), BETA * D_FF_EXPERT ** -0.5),
    }

def reference(x, c, ctx, c_ctx, w_mod, b_mod, w_in, g_q, w_uq, g_kv, w_uk, w_uv, w_ao, w_fo, w_out,
              ln1_g, ln1_b, ln2_g, ln2_b, w_ff_gate, w_ff_up, w_ff_down,
              w_router, b_router, w_e_gate, w_e_up, w_e_down):
    n_lat = x.shape[1]
    rope = axial_rope_tables(n_lat)

    def channel_mixer(h, l):
        i = l // 2
        if l % 2 == 0:
            return swiglu(h, w_ff_gate[i], w_ff_up[i], w_ff_down[i])
        return moe_ffn(h, w_router[i], b_router[i], w_e_gate[i], w_e_up[i], w_e_down[i])

    for l in range(DEPTH):
        last = l == DEPTH - 1
        mod_x = jnp.split(jax.nn.silu(c) @ w_mod[l] + b_mod[l], 6, axis=-1)
        mod_x = [m[:, None, :] for m in mod_x]
        mod_c = jnp.split(jax.nn.silu(c_ctx) @ w_mod[l] + b_mod[l], 6, axis=-1)
        sh1x, sc1x, gt1x, sh2x, sc2x, gt2x = mod_x
        sh1c, sc1c, gt1c, sh2c, sc2c, gt2c = mod_c

        h_x = ln_modulate(x, sh1x, sc1x)
        h_c = ln_modulate(ctx, sh1c, sc1c)
        proj_x = h_x @ w_in[l]
        qn_x, qr_x = mla_queries(proj_x, g_q[l], w_uq[l], rope)
        kn_x, kr_x, v_x = mla_keys(proj_x[..., OFF_KV:OFF_F], g_kv[l], w_uk[l], w_uv[l], rope)
        if last:
            kv_c = h_c @ w_in[l][:, OFF_KV:OFF_F]
        else:
            proj_c = h_c @ w_in[l]
            kv_c = proj_c[..., OFF_KV:OFF_F]
        kn_c, kr_c, v_c = mla_keys(kv_c, g_kv[l], w_uk[l], w_uv[l], None)

        attn_x = latent_attention(qn_x, qr_x,
                                  jnp.concatenate([kn_c, kn_x], axis=1),
                                  jnp.concatenate([kr_c, kr_x], axis=1),
                                  jnp.concatenate([v_c, v_x], axis=1))
        y_x = mixer_out(proj_x, attn_x, w_ao[l], w_fo[l], w_out[l])
        x = ln_affine(ALPHA * x + gt1x * y_x, ln1_g[l], ln1_b[l])

        if not last:
            qn_c, qr_c = mla_queries(proj_c, g_q[l], w_uq[l], None)
            attn_c = attend(qn_c, qr_c, kn_c, kr_c, v_c).reshape(ctx.shape[0], ctx.shape[1], ATTN_DIM)
            y_c = mixer_out(proj_c, attn_c, w_ao[l], w_fo[l], w_out[l])
            ctx = ln_affine(ALPHA * ctx + gt1c * y_c, ln1_g[l], ln1_b[l])

        f_x = channel_mixer(ln_modulate(x, sh2x, sc2x), l)
        x = ln_affine(ALPHA * x + gt2x * f_x, ln2_g[l], ln2_b[l])
        if not last:
            f_c = channel_mixer(ln_modulate(ctx, sh2c, sc2c), l)
            ctx = ln_affine(ALPHA * ctx + gt2c * f_c, ln2_g[l], ln2_b[l])

    return x


_drawn_inputs = setup_inputs


def setup_inputs(seed=0):
    import zlib

    import numpy as np

    out = dict(_drawn_inputs(seed))
    spreads = {}
    factors = {'ctx': 8.0,
     'c_ctx': 8.0,
     'b_mod': 8.0,
     'g_q': 8.0,
     'w_uq': 8.0,
     'g_kv': 8.0,
     'w_uk': 8.0,
     'w_uv': 6.343,
     'w_ao': 6.248,
     'b_router': 57.254}
    for name, (base, spread) in spreads.items():
        noise = np.random.default_rng([zlib.crc32(name.encode()), seed]).standard_normal(out[name].shape)
        drawn = base * np.exp(spread * noise) if base else spread * noise
        out[name] = __import__('jax').numpy.asarray(drawn.astype(out[name].dtype))
    for name, factor in factors.items():
        out[name] = (out[name] * factor).astype(out[name].dtype)
    return out
```

```python
from contextlib import ExitStack

import numpy as np

import concourse.bass as bass
from concourse import mybir

ALU = mybir.AluOpType
ACT = mybir.ActivationFunctionType
AX = mybir.AxisListType
F32 = mybir.dt.float32
I32 = mybir.dt.int32
U32 = mybir.dt.uint32

P = 128
D = 1024
KD = D // P
SEQ = 256
CTX = 256
NTOK = SEQ + CTX
TT = NTOK // P
DEPTH = 2
HEADS = 16
NOPE = 64
ROPE = 32
QK = NOPE + ROPE
VH = 64
Q_LORA = 256
KV_LORA = 128
FG = 4
FC = 128
OFF_KV = Q_LORA
OFF_KR = OFF_KV + KV_LORA
OFF_F = OFF_KR + ROPE
OFF_G = OFF_F + FG * FC
D_FF = 2816
FT = D_FF // P
NE = 8
D_FE = 3584
SM_SCALE = float(QK) ** -0.5
ALPHA = float((2 * DEPTH) ** 0.25)
EPS = 1e-6

SLOTS = 7
SLOT = 2048
NFC = D_FE // 512
JOB_CHUNKS = 6 * NFC
assert JOB_CHUNKS % SLOTS == 0
SLOT_TURNS = JOB_CHUNKS // SLOTS
JOBS = 16

C_ID = 0
C_DFTC = C_ID + P
C_DFTT = C_DFTC + 2 * FC
C_COS = C_DFTT + 4 * SEQ
C_SIN = C_COS + NTOK
C_PERM = C_SIN + NTOK
C_SEL = C_PERM + P
C_ONE = C_SEL + 2
C_EPS = C_ONE + 1
C_END = C_EPS + 1
S_C = 0
S_GQ = S_C + 2 * KD
S_GKV = S_GQ + 2 * DEPTH
S_ROUTER = S_GKV + DEPTH
S_END = S_ROUTER + KD * NE
R_IOTA = 0
R_TRI = R_IOTA + P
R_E = R_TRI + P
R_END = R_E + NE


def ring_chunks(w):
    chunks = []

    def mod(l, cb):
        v = w["w_mod"][l].rearrange("(h k p) n -> h p k n", h=2, p=P)
        for h in range(2):
            chunks.append((("mod", l, cb, h), [(0, (4, 512), v[h, :, :, cb * 512:(cb + 1) * 512])]))

    def rows(name, v, k, c0, n):
        chunks.append((name, [(0, (k, n), v.rearrange("(k p) n -> p k n", p=P)[:, :, c0:c0 + n])]))

    for cb in range(6):
        mod(0, cb)
    for l in range(DEPTH):
        w_in = w["w_in"][l]
        rows(("in", l, 0), w_in, KD, 0, Q_LORA)
        rows(("in", l, 1), w_in, KD, OFF_KV, KV_LORA + ROPE)
        rows(("in", l, 2), w_in, KD, OFF_F, 2 * FC)
        rows(("in", l, 3), w_in, KD, OFF_F + 2 * FC, 2 * FC)
        for g in range(4):
            uq = w["w_uq"][l].rearrange("(k p) n -> p k n", p=P)[:, :, g * 4 * QK:(g + 1) * 4 * QK]
            uk = w["w_uk"][l][:, g * 4 * NOPE:(g + 1) * 4 * NOPE]
            uv = w["w_uv"][l][:, g * 4 * VH:(g + 1) * 4 * VH]
            chunks.append((("heads", l, g), [(0, (2, 4 * QK), uq), (2 * 4 * QK, (256,), uk),
                                             (2 * 4 * QK + 256, (256,), uv)]))
        for jj in range(4):
            rows(("ga", l, jj), w_in, KD, OFF_G + jj * 256, 256)
            rows(("gf", l, jj), w_in, KD, OFF_G + D + jj * 256, 256)
            rows(("ao", l, jj), w["w_ao"][l], KD, jj * 256, 256)
            rows(("fo", l, jj), w["w_fo"][l], FG, jj * 256, 256)
            for cb in MERGE_MOD[jj]:
                mod(l, cb)
        for kk in range(4):
            v = w["w_out"][l].rearrange("(g k p) n -> g p k n", k=2, p=P)
            chunks.append((("out", l, kk), [(0, (2, D), v[kk])]))
        if l == 0:
            for fp in range(FT // 2):
                rows(("fg", fp), w["w_ff_gate"][0], KD, fp * 256, 256)
                rows(("fu", fp), w["w_ff_up"][0], KD, fp * 256, 256)
                if 2 <= fp < 8:
                    mod(1, fp - 2)
            down = w["w_ff_down"][0].rearrange("(f p) n -> p f n", p=P)
            for dh in range(2):
                for fg in range(0, FT, 4):
                    n = min(4, FT - fg)
                    chunks.append((("fd", dh, fg), [(0, (n, 512), down[:, fg:fg + n, dh * 512:(dh + 1) * 512])]))
    return chunks


MERGE_MOD = ((6,), (7, 10), (8, 11), (9,))


def merged_plan(l):
    streams = (0, 1) if l == 0 else (1,)
    tiles, units = [], []
    for g in range(4):
        for pair in range(2):
            for s in streams:
                u = len(units)
                units.append((g, pair, s))
                tiles += [(u, g, 2 * pair + h, h, s, qt) for h in range(2) for qt in range(2)]
    per_group = len(tiles) // 4
    plan = [("fill", 0, i) for i in range(8)]
    for i in range(len(tiles) + 4):
        if i < len(tiles):
            plan.append(("score", i))
        if 1 <= i <= len(tiles):
            plan.append(("norm", i - 1))
        if 2 <= i < len(tiles) + 2:
            plan.append(("turn", i - 2))
        if i >= 6 and i % 4 == 2:
            plan.append(("pv", i // 4 - 1))
        if i >= 7 and i % 4 == 3:
            plan.append(("take", i // 4 - 1))
        g, at = divmod(i, per_group)
        if g < 3:
            step = per_group // 8
            if at % step == step - 1:
                plan.append(("fill", g + 1, at // step))
    return plan, tiles, units


def build(nc, w, out):
    ctx = ExitStack()
    with ctx:
        def sem(name):
            return ctx.enter_context(nc.semaphore(name))

        ring = ctx.enter_context(nc.sbuf_tensor("ring", [P, SLOTS, SLOT], F32))
        const = ctx.enter_context(nc.sbuf_tensor("const", [P, C_END], F32))
        small = ctx.enter_context(nc.sbuf_tensor("small", [P, S_END], F32))
        bmod = ctx.enter_context(nc.sbuf_tensor("bmod", [DEPTH * 12, 512], F32))
        x_res = ctx.enter_context(nc.sbuf_tensor("x_res", [P, TT, D], F32))
        h_t = ctx.enter_context(nc.sbuf_tensor("h_t", [P, KD, NTOK], F32))
        reg_q = ctx.enter_context(nc.sbuf_tensor("reg_q", [P, 12288], F32))
        reg_v = ctx.enter_context(nc.sbuf_tensor("reg_v", [P, 2048], F32))
        reg_a = ctx.enter_context(nc.sbuf_tensor("reg_a", [P, 4096], F32))
        reg_f = ctx.enter_context(nc.sbuf_tensor("reg_f", [P, 2048], F32))
        lat_kv = ctx.enter_context(nc.sbuf_tensor("lat_kv", [P, NTOK], F32))
        lat_q = ctx.enter_context(nc.sbuf_tensor("lat_q", [P, 2, NTOK], F32))
        reg_p = ctx.enter_context(nc.sbuf_tensor("reg_p", [P, 3, 512], F32))
        reg_r = ctx.enter_context(nc.sbuf_tensor("reg_r", [P, 3, NTOK], F32))
        gate1 = ctx.enter_context(nc.sbuf_tensor("gate1", [P, 2, D], F32))
        gate2 = ctx.enter_context(nc.sbuf_tensor("gate2", [P, 2, D], F32))
        c_act = ctx.enter_context(nc.sbuf_tensor("c_act", [P, KD, 32], F32))
        modcol = ctx.enter_context(nc.sbuf_tensor("modcol", [P, DEPTH, 4, KD, 2], F32))
        stat = ctx.enter_context(nc.sbuf_tensor("stat", [P, 80], F32))
        bn = stat[:, 0:12].rearrange("p (a b) -> p a b", a=2)
        ln_mv = stat[:, 12:20].rearrange("p (n a) -> p n a", a=2)
        ln_std = stat[:, 20:24]
        ln_rstd = stat[:, 24:28]
        s_top, s_neg, s_sum, s_inv = (stat[:, 28 + 4 * i:32 + 4 * i] for i in range(4))
        c_sigm = stat[:, 48:48 + 2 * KD]
        psum = ctx.enter_context(nc.psum_tensor("psum", [P, 8, 512], F32))

        ident = const[:, C_ID:C_ID + P]
        dft_c = const[:, C_DFTC:C_DFTC + 2 * FC]
        dft_t = const[:, C_DFTT:C_DFTT + 4 * SEQ].rearrange("p (t a n) -> p t a n", t=2, a=2)
        cos = const[:, C_COS:C_COS + NTOK]
        sin = const[:, C_SIN:C_SIN + NTOK]
        perm = const[:, C_PERM:C_PERM + P]
        sel = const[:, C_SEL:C_SEL + 2]
        one = const[:, C_ONE:C_ONE + 1]
        eps = const[:, C_EPS:C_EPS + 1]
        c_raw = small[:, S_C:S_C + 2 * KD].rearrange("p (k s) -> p k s", s=2)
        w_router = small[:, S_ROUTER:S_END].rearrange("p (k e) -> p k e", e=NE)

        q_t = reg_q[:, 0:4096].rearrange("p (b h n) -> p b h n", b=2, h=4)
        k_t = reg_q[:, 4096:8192].rearrange("p (b h n) -> p b h n", b=2, h=4)
        p_t = reg_q[:, 8192:12288].rearrange("p (b h k n) -> p b h k n", b=2, h=2, k=4)
        u_t = reg_q[:, 0:2048].rearrange("p (g n) -> p g n", g=FG)
        squares = reg_q[:, 8192:8192 + 3 * NTOK].rearrange("p (m n) -> p m n", m=3)
        rms = reg_q[:, 8192 + 3 * NTOK:8192 + 5 * NTOK].rearrange("p (m n) -> p m n", m=2)
        dft_1 = reg_q[:, 8192 + 5 * NTOK:8192 + 7 * NTOK].rearrange("p (b t n) -> p b t n", b=2, t=2)
        merged = reg_q[:, 0:4096].rearrange("p (k n) -> p k n", k=KD)
        sig_b = reg_q[:, 4096:4096 + 4 * NTOK].rearrange("p (m n) -> p m n", m=4)
        mrg_b = reg_q[:, 4096 + 4 * NTOK:4096 + 8 * NTOK].rearrange("p (m n) -> p m n", m=4)
        a_t = reg_q[:, 0:FT * NTOK].rearrange("p (f n) -> p f n", f=FT)
        v_sb = reg_v[:, :].rearrange("p (b k n) -> p b k n", b=2, k=4)
        ln_rows = reg_v[:, :].rearrange("p (a n) -> p a n", a=2)
        attn_t = reg_a[:, :].rearrange("p (k n) -> p k n", k=KD)
        z_sb = reg_a[:, 0:2048].rearrange("p (b n) -> p b n", b=2)
        xn = reg_a[:, 2048:4096].rearrange("p (b n) -> p b n", b=2)
        four_t = reg_f[:, :].rearrange("p (g n) -> p g n", g=FG)
        ff_b = reg_f[:, :].rearrange("p (m n) -> p m n", m=4)
        k_rope = reg_r[:, 0, :]
        q_rope = reg_r[:, 0, :]
        rope_a = reg_r[:, 1, :]
        rope_b = reg_r[:, 2, :]
        mod_pm = reg_p

        at = [0]

        def part(n):
            at[0] += n
            return reg_q[:, at[0] - n:at[0]]

        xg_t = part(KD * P).rearrange("p (k n) -> p k n", k=KD)
        e_sig = part(1024).rearrange("p (b n) -> p b n", b=2)
        e_tmp = part(512)
        e_a = part(1024).rearrange("p (b n) -> p b n", b=2)
        e_at = part(1024).rearrange("p (b f n) -> p b f n", b=2, f=4)
        y_sb = part(D)
        f_acc = part(2 * D).rearrange("p (t n) -> p t n", t=2)
        sel_tok = part(2 * P).rearrange("p (t n) -> p t n", t=2)
        sel_slot = part(2 * P).rearrange("p (t n) -> p t n", t=2)
        route_c = part(R_END)
        iota = route_c[:, R_IOTA:R_IOTA + P]
        tri = route_c[:, R_TRI:R_TRI + P]
        e_num = route_c[:, R_E:R_E + NE]
        rt = part(1024)
        assert at[0] <= 12288
        rt_at = [0]

        def rpart(n):
            rt_at[0] += n
            return rt[:, rt_at[0] - n:rt_at[0]]

        b_rout = rpart(NE)
        logits = rpart(2 * NE).rearrange("p (t e) -> p t e", t=2)
        top = rpart(2 * 8).rearrange("p (t e) -> p t e", t=2)
        top_i = rpart(2 * 8).rearrange("p (t e) -> p t e", t=2)
        top_if = rpart(2 * 8).rearrange("p (t e) -> p t e", t=2)
        pair_w = rpart(2 * 4).rearrange("p (t e) -> p t e", t=2)
        hot = rpart(4 * NE).rearrange("p (t k e) -> p t k e", t=2, k=2)
        taken = rpart(2 * NE).rearrange("p (t e) -> p t e", t=2)
        comb = rpart(2 * NE).rearrange("p (t e) -> p t e", t=2)
        tmp8 = rpart(2 * NE).rearrange("p (t e) -> p t e", t=2)
        place = rpart(2 * NE).rearrange("p (t e) -> p t e", t=2)
        count = rpart(NE)
        over = rpart(NE)
        rank = rpart(NE)
        hit = rpart(NE)
        job_at = rpart(2 * (JOBS + 1)).rearrange("p (t j) -> p t j", t=2)
        job_w = rpart(2 * (JOBS + 1)).rearrange("p (t j) -> p t j", t=2)
        job_e = rpart(JOBS)
        job_ei = rpart(JOBS).bitcast(I32)
        n_jobs = rpart(1)
        n_jobs_i = rpart(1).bitcast(I32)

        landed = [sem(f"landed{i}") for i in range(SLOTS)]
        slot_free = sem("slot_free")
        consts_in = sem("consts_in")
        x_in = [sem(f"x_in{t}") for t in range(TT)]
        ln_in = [sem(f"ln_in{i}") for i in range(4)]
        route_in = sem("route_in")
        out_done = sem("out_done")
        c_sig = sem("c_sig")
        c_ready = sem("c_ready")
        mod_acc = sem("mod_acc")
        mod_copied = sem("mod_copied")
        mod_sum = sem("mod_sum")
        mod_done = sem("mod_done")
        dve_own = sem("dve_own")
        act_own = sem("act_own")
        pool_own = sem("pool_own")

        def layered(name):
            return [sem(f"{name}_{l}") for l in range(DEPTH)]

        var_ready, std_ready = sem("var_ready"), sem("std_ready")
        xn_ready = sem("xn_ready")
        xn_turned = [sem("xn_turned0"), sem("xn_turned1")]
        ht_act, ht_dve = sem("ht_act"), sem("ht_dve")
        z_scaled = sem("z_scaled")
        x_new = sem("x_new")
        in_mm, in_act, in_dve = layered("in_mm"), layered("in_act"), layered("in_dve")
        rms_mm, rms_act, lat_done = layered("rms_mm"), layered("rms_act"), layered("lat_done")
        kr_perm, kr_sum = layered("kr_perm"), layered("kr_sum")
        kr_done, kr_copied = layered("kr_done"), layered("kr_copied")
        f1_mm, f1_act, f2_mm, f2_dve = layered("f1_mm"), layered("f1_act"), layered("f2_mm"), layered("f2_dve")
        fill_mm, fill_act, fill_dve = layered("fill_mm"), layered("fill_act"), layered("fill_dve")
        rope_cos = layered("rope_cos")
        s_mm, s_max, s_exp, s_rec, s_nrm = (layered(n) for n in ("s_mm", "s_max", "s_exp", "s_rec", "s_nrm"))
        t_mm, t_out = layered("t_mm"), layered("t_out")
        pv_mm, pv_out = layered("pv_mm"), layered("pv_out")
        g_mm, g_sig, g_mul = layered("g_mm"), layered("g_sig"), layered("g_mul")
        m_done = layered("m_done")
        y_mm, y_used = layered("y_mm"), layered("y_used")
        fg_mm, fg_sig, fa_done = sem("fg_mm"), sem("fg_sig"), sem("fa_done")
        fd_mm, fd_used = sem("fd_mm"), sem("fd_used")
        r_mm, r_taken, route_ready = sem("r_mm"), sem("r_taken"), sem("route_ready")
        r_diff, r_exp = sem("r_diff"), sem("r_exp")
        sel_ready = sem("sel_ready")
        xg_mm, xg_act, xg_dve = sem("xg_mm"), sem("xg_act"), sem("xg_dve")
        gu_mm, e_sig_ok, a_ok = sem("gu_mm"), sem("e_sig_ok"), sem("a_ok")
        at_mm, at_ok = sem("at_mm"), sem("at_ok")
        st_mm, st_ok = sem("st_mm"), sem("st_ok")
        ye_mm, y_dve = sem("ye_mm"), sem("y_dve")
        sc_mm, sc_ok = sem("sc_mm"), sem("sc_ok")
        e_tmp_ok = sem("e_tmp_ok")

        chunks = ring_chunks(w)
        n_static = len(chunks)
        index_of = {name: n for n, (name, _) in enumerate(chunks)}
        arrive = []
        per_slot = [0] * SLOTS
        for n, (_, dmas) in enumerate(chunks):
            per_slot[n % SLOTS] += 16 * len(dmas)
            arrive.append(per_slot[n % SLOTS])

        def slot_view(n, c0, shape):
            size = int(np.prod(shape))
            v = ring[:, n % SLOTS, c0:c0 + size]
            return v.rearrange("p (k n) -> p k n", k=shape[0]) if len(shape) == 2 else v

        q0 = [0, CTX]
        t0 = [0, 2]
        nq = [NTOK, SEQ]
        plans = [merged_plan(l) for l in range(DEPTH)]

        ln_uses = [(0, 1, range(TT)), (0, 2, range(TT)), (1, 1, range(TT)), (1, 2, range(2, TT))]
        tiles_before = [0, 4, 8, 12, 14]
        norms_before = [None, 0, 4, 8, 10]
        stats_before = [0, 4, 12, 20, 24]

        def chain(tiles):
            tiles = list(tiles)
            steps = []
            for i, t in enumerate(tiles):
                steps.append(("A", t))
                if i:
                    steps.append(("B", tiles[i - 1]))
            return steps + [("B", tiles[-1])]

        def act_fills(g, i):
            return 7 * g + sum(k != 4 for k in range(i + 1))

        def dve_fills(g, i):
            return 5 * g + sum(k in (1, 2, 3, 4, 5) for k in range(i + 1))

        mod_order = [(0, cb) for cb in range(6)] + [(0, cb) for jj in range(4) for cb in MERGE_MOD[jj]]
        mod_order += [(1, cb) for cb in range(6)] + [(1, cb) for jj in range(4) for cb in MERGE_MOD[jj]]
        mod_at = {b: n for n, b in enumerate(mod_order)}

        block = ctx.enter_context(nc.Block())

        @block.sync
        def _(sp):
            sp.dma_start(small[:, :], w["small"]).then_inc(consts_in, 16)
            sp.dma_start(const[:, :], w["const"]).then_inc(consts_in, 16)
            sp.dma_start(bmod[:, :], w["b_mod"].rearrange("l (c n) -> (l c) n", n=512)).then_inc(consts_in, 16)

            def load(n):
                if n >= SLOTS:
                    sp.wait_ge(slot_free, n - SLOTS + 1)
                for c0, shape, src in chunks[n][1]:
                    sp.dma_start(slot_view(n, c0, shape), src).then_inc(landed[n % SLOTS], 16)

            def load_ln(i, g, b):
                for a, v in ((0, g), (1, b)):
                    sp.dma_start(ln_rows[:, a, :], v.partition_broadcast(P)).then_inc(ln_in[i], 16)

            for n in range(4):
                load(n)
            for t in range(TT):
                src = w["ctx"][0] if t < 2 else w["x"][0]
                sp.dma_start(x_res[:, t, :], src[(t % 2) * P:(t % 2 + 1) * P, :]).then_inc(x_in[t], 16)
            for n in range(4, n_static):
                for l in range(DEPTH):
                    if n == index_of[("out", l, 0)]:
                        sp.wait_ge(pv_out[l], len(plans[l][2]))
                        load_ln(2 * l, w["ln1_g"][l], w["ln1_b"][l])
                        if l == 1:
                            sp.dma_start(route_c, w["route"]).then_inc(route_in, 16)
                            sp.dma_start(b_rout, w["b_router"][0].partition_broadcast(P)).then_inc(route_in, 16)
                if n == index_of[("fd", 0, 0)]:
                    sp.wait_ge(x_new, 4)
                    load_ln(1, w["ln2_g"][0], w["ln2_b"][0])
                load(n)

            def job(j, e):
                def chunk(c, src, shape):
                    sp.wait_ge(slot_free, j * JOB_CHUNKS + (n_static + c - SLOTS + 1))
                    n = n_static + c
                    sp.dma_start(slot_view(n, 0, shape), src).then_inc(landed[n % SLOTS], 16)

                gate = w["w_e_gate"].rearrange("a e (h k p) f -> (a e) h p k f", h=2, p=P)[bass.ds(e, 1)]
                up = w["w_e_up"].rearrange("a e (h k p) f -> (a e) h p k f", h=2, p=P)[bass.ds(e, 1)]
                down = w["w_e_down"].rearrange("a e (c h f p) n -> (a e) (c h) p f n", h=2, f=2, p=P)[bass.ds(e, 1)]
                c = 0
                for fc in range(NFC + 1):
                    if fc < NFC:
                        for v in (gate, up):
                            for h in range(2):
                                chunk(c, v[0, h, :, :, fc * 512:(fc + 1) * 512], (4, 512))
                                c += 1
                    if fc > 0:
                        for h in range(2):
                            chunk(c, down[0, 2 * (fc - 1) + h], (2, D))
                            c += 1

            sp.wait_ge(x_new, norms_before[4])
            load_ln(3, w["ln2_g"][1], w["ln2_b"][1])
            with sp.Fori(0, NE - 1) as j:
                job(j, j)
            sp.wait_ge(route_ready, 1)
            jobs = sp.value_load(n_jobs_i[0:1, 0:1], min_val=NE, max_val=JOBS)
            with sp.Fori(NE - 1, jobs) as j:
                job(j, sp.value_load(job_ei[0:1, bass.ds(j, 1)], min_val=0, max_val=NE - 1))
            for t in range(2):
                sp.wait_ge(x_new, norms_before[4] + t + 1)
                sp.dma_start(out[0, t * P:(t + 1) * P, :], x_res[:, 2 + t, :]).then_inc(out_done, 16)
            sp.wait_ge(out_done, 32)

        @block.tensor
        def _(pe):
            pending = [0]

            def mm(o, lhs, rhs, start, stop, sig=None, free=False, **kw):
                ins = pe.matmul(o, lhs, rhs, start=start, stop=stop, **kw)
                pending[0] += bool(free)
                if sig is not None:
                    ins.then_inc(sig, 1)
                elif pending[0]:
                    ins.then_inc(slot_free, 1)
                    pending[0] -= 1
                return ins

            def arrived(name):
                n = index_of[name]
                pe.wait_ge(landed[n % SLOTS], arrive[n])
                return n

            def mod_block(b):
                l, cb = b
                n = mod_at[b]
                if n >= 1:
                    pe.wait_ge(mod_copied, n)
                for h in range(2):
                    v = slot_view(arrived(("mod", l, cb, h)), 0, (4, 512))
                    for k in range(4):
                        mm(psum[32 * k:32 * k + 32, 4, :], c_act[:, 4 * h + k, :], v[:, k, :],
                           start=(h == 0), stop=(h == 1 and k > 0), free=(k == 3), skip_group_check=True)
                row = l * 12 + cb
                mm(psum[0:32, 4, :], ident[0:DEPTH * 12, row:row + 1].to_broadcast([DEPTH * 12, 32]),
                   bmod[:, :], start=False, stop=True, sig=mod_acc, skip_group_check=True)

            def mod_reduce(b):
                l, cb = b
                n = mod_at[b]
                pe.wait_ge(mod_copied, n + 1)
                if n >= 1:
                    pe.wait_ge(mod_done, n)
                pm = mod_pm[:, n % 2, :]
                if cb in (4, 5, 10, 11):
                    mm(psum[:, 5, :], sel[:, 0:1].to_broadcast([P, P]), pm, start=True, stop=True)
                    mm(psum[:, 6, :], sel[:, 1:2].to_broadcast([P, P]), pm, start=True, stop=True, sig=mod_sum)
                else:
                    for i in range(4):
                        mm(psum[:, 5, 2 * i:2 * i + 2], pm[:, i * P:(i + 1) * P], sel, start=True, stop=True,
                           sig=mod_sum if i == 3 else None)

            def turn_tiles(use):
                _, _, tiles = ln_uses[use]
                for i, t in enumerate(tiles):
                    n = tiles_before[use] + i
                    pe.wait_ge(xn_ready, n + 1)
                    for half in range(2):
                        if n >= 1:
                            pe.wait_ge((ht_act, ht_dve)[half], n)
                        for k in range(4):
                            ins = pe.transpose(psum[:, 6 + half, k * P:(k + 1) * P],
                                               xn[:, t % 2, (4 * half + k) * P:(4 * half + k + 1) * P], ident)
                        ins.then_inc(xn_turned[half], 1)

            def input_projection(l):
                pe.wait_ge(ht_act, tiles_before[2 * l + 1])
                pe.wait_ge(ht_dve, tiles_before[2 * l + 1])
                groups = [(0, 0, 0, 0), (0, P, 0, 0), (1, 0, 0, 1), (1, P, 64, 1),
                          (2, 0, 0, 0), (2, P, 0, 0), (3, 0, 0, 0), (3, P, 0, 0)]
                for i, (ch, c0, part0, full) in enumerate(groups):
                    name = ("in", l, ch)
                    shape = (KD, 160 if ch == 1 else 256)
                    v = slot_view(arrived(name), 0, shape)
                    m = ROPE if part0 else P
                    a = 0 if full else q0[l]
                    if i >= 4:
                        if i - 4 < 3:
                            pe.wait_ge(in_act[l], i - 3)
                        else:
                            pe.wait_ge(in_dve[l], 1)
                    for k in range(KD):
                        last = k == KD - 1
                        mm(psum[part0:part0 + m, i % 4, a:NTOK], v[:, k, c0:c0 + m], h_t[:, k, a:NTOK],
                           start=(k == 0), stop=last, sig=in_mm[l] if last else None,
                           free=last and i in (1, 3, 5, 7))

            def latent_norms(l):
                a = q0[l]
                pe.wait_ge(in_act[l], 3)
                for k in range(2):
                    mm(psum[:, 4, a:NTOK], one.to_broadcast([P, P]), squares[:, k, a:NTOK], start=(k == 0),
                       stop=(k == 1), sig=rms_mm[l] if k == 1 else None)
                mm(psum[:, 5, :], one.to_broadcast([P, P]), squares[:, 2, :], start=True, stop=True, sig=rms_mm[l])
                pe.wait_ge(in_dve[l], 1)
                mm(psum[64:96, 6, :], perm[64:96, 64:96], k_rope[64:96, :], start=True, stop=True, sig=kr_perm[l])

            def fourier(l):
                units = [(g, s) for g in range(FG) for s in ((0, 1) if l == 0 else (1,))]

                def second(n):
                    g, s = units[n]
                    pe.wait_ge(f1_act[l], n + 1)
                    if n >= 2:
                        pe.wait_ge(f2_dve[l], n - 1)
                    i = 0
                    for t in range(2):
                        for a in range(2):
                            mm(psum[:, 2 + n % 2, 0:SEQ], dft_1[:, n % 2, t, a * FC:(a + 1) * FC], dft_t[:, t, a, :],
                               start=(i == 0), stop=(i == 3), sig=f2_mm[l] if i == 3 else None)
                            i += 1

                pe.wait_ge(in_dve[l], 5)
                for n, (g, s) in enumerate(units):
                    if n >= 2:
                        pe.wait_ge(f1_act[l], n - 1)
                    for t in range(2):
                        mm(psum[:, n % 2, t * 256:(t + 1) * 256],
                           u_t[:, g, s * SEQ + t * P:s * SEQ + (t + 1) * P], dft_c,
                           start=True, stop=True, sig=f1_mm[l] if t == 1 else None)
                    if n >= 1:
                        second(n - 1)
                second(len(units) - 1)

            def attention(l):
                plan, tiles, units = plans[l]
                a = q0[l]
                pe.wait_ge(lat_done[l], 1)
                pe.wait_ge(f2_dve[l], FG * (2 if l == 0 else 1))

                def fill(g, i):
                    n = 8 * g + i
                    v = arrived(("heads", l, g))
                    uq = slot_view(v, 0, (2, 4 * QK))
                    uk = slot_view(v, 768, (256,))
                    uv = slot_view(v, 1024, (256,))
                    b = i % 2
                    if n >= 2:
                        before = (g, i - 2) if i >= 2 else (g - 1, i + 6)
                        pe.wait_ge(fill_act[l], act_fills(*before))
                        if dve_fills(*before):
                            pe.wait_ge(fill_dve[l], dve_fills(*before))
                    if i == 0:
                        for k in range(2):
                            mm(psum[:, b, a:NTOK], uq[:, k, 0:4 * ROPE], lat_q[:, k, a:NTOK], start=(k == 0),
                               stop=(k == 1), sig=fill_mm[l] if k == 1 else None)
                    elif i in (1, 2):
                        c0 = 4 * ROPE + (i - 1) * P
                        for k in range(2):
                            mm(psum[:, b, a:NTOK], uq[:, k, c0:c0 + P], lat_q[:, k, a:NTOK],
                               start=(k == 0), stop=(k == 1), sig=fill_mm[l] if k == 1 else None)
                    elif i in (3, 5):
                        c0 = 0 if i == 3 else P
                        mm(psum[:, b, :], uk[:, c0:c0 + P], lat_kv[:, :], start=True, stop=True, sig=fill_mm[l])
                    elif i == 4:
                        pe.wait_ge(fill_act[l], act_fills(g, 0))
                        mm(psum[:, b, a:NTOK], perm, q_rope[:, a:NTOK], start=True, stop=True, sig=fill_mm[l])
                    else:
                        for kt in range(2):
                            t = 2 * (i - 6) + kt
                            mm(psum[:, b, kt * 256:(kt + 1) * 256], lat_kv[:, t * P:(t + 1) * P], uv,
                               start=True, stop=True, sig=fill_mm[l] if kt == 1 else None,
                               free=(i == 7 and kt == 1))

                def score(c):
                    u, g, h, _, s, qt = tiles[c]
                    pe.wait_ge(fill_act[l], act_fills(g, 7))
                    pe.wait_ge(fill_dve[l], dve_fills(g, 7))
                    pe.wait_ge((kr_done, kr_copied)[g % 2][l], 1)
                    if c >= 2:
                        pe.wait_ge(s_exp[l], c - 1)
                    nk = CTX if s == 0 else NTOK
                    at_q = s * SEQ + qt * P
                    mm(psum[:, 2 + c % 2, 0:nk], q_t[0:QK, g % 2, h, at_q:at_q + P], k_t[0:QK, g % 2, h, 0:nk],
                       start=True, stop=True, sig=s_mm[l])

                def turn(c):
                    s = tiles[c][4]
                    pe.wait_ge(s_nrm[l], c + 1)
                    if c >= 2:
                        pe.wait_ge(t_out[l], c - 1)
                    nt = 2 if s == 0 else 4
                    for k in range(nt):
                        ins = pe.transpose(psum[:, 4 + c % 2, k * P:(k + 1) * P], reg_p[:, c % 3, k * P:(k + 1) * P],
                                           ident)
                    ins.then_inc(t_mm[l], 1)

                def pv(u):
                    g, pair, s = units[u]
                    pe.wait_ge(t_out[l], 4 * u + 4)
                    if u >= 2:
                        pe.wait_ge(pv_out[l], u - 1)
                    nt = 2 if s == 0 else 4
                    for k in range(nt):
                        for h in range(2):
                            c0 = (2 * pair + h) * VH
                            mm(psum[VH * h:VH * h + VH, 6 + u % 2, 0:SEQ], v_sb[:, g % 2, k, c0:c0 + VH],
                               p_t[:, u % 2, h, k, :], start=(k == 0), stop=(k == nt - 1),
                               sig=pv_mm[l] if k == nt - 1 and h == 1 else None, skip_group_check=True)

                for step in plan:
                    if step[0] == "fill":
                        fill(step[1], step[2])
                    elif step[0] == "score":
                        score(step[1])
                    elif step[0] == "turn":
                        turn(step[1])
                    elif step[0] == "pv":
                        pv(step[1])

            def merge(l):
                a = q0[l]
                units = plans[l][2]
                pe.wait_ge(pv_out[l], len(units))
                for jj in range(4):
                    fills = [(kind, i) for kind in ("ga", "gf", "ao", "fo") for i in range(2)]
                    for f, (kind, i) in enumerate(fills):
                        n = 8 * jj + f
                        if f >= 4:
                            pe.wait_ge(g_sig[l], 4 * jj + f - 3)
                        elif jj >= 1:
                            pe.wait_ge(g_mul[l], 4 * (jj - 1) + f + 1)
                        kn = FG if kind == "fo" else KD
                        v = slot_view(arrived((kind, l, jj)), 0, (kn, 256))
                        rhs = {"ga": h_t, "gf": h_t, "ao": attn_t, "fo": four_t}[kind]
                        for k in range(kn):
                            last = k == kn - 1
                            mm(psum[:, f % 4, a:NTOK], v[:, k, i * P:(i + 1) * P], rhs[:, k, a:NTOK],
                               start=(k == 0), stop=last, sig=g_mm[l] if last else None, free=last and i == 1)
                    for cb in MERGE_MOD[jj]:
                        mod_block((l, cb))
                        mod_reduce((l, cb))

            def output_projection(l):
                pe.wait_ge(m_done[l], KD)
                pe.wait_ge(g_mul[l], 16)
                for i, t in enumerate(range(t0[l], TT)):
                    if i >= 2:
                        pe.wait_ge(y_used[l], i - 1)
                    for kk in range(4):
                        v = slot_view(arrived(("out", l, kk)), 0, (2, D))
                        for k in range(2):
                            for dh in range(2):
                                kc = 2 * kk + k
                                last = kc == KD - 1
                                mm(psum[:, 2 * (i % 2) + dh, :], merged[:, kc, t * P:(t + 1) * P],
                                   v[:, k, dh * 512:(dh + 1) * 512], start=(kc == 0), stop=last,
                                   sig=y_mm[l] if last and dh == 1 else None,
                                   free=(t == TT - 1 and k == 1 and dh == 1), skip_group_check=True)

            def dense_mixer():
                pe.wait_ge(ht_act, tiles_before[2])
                pe.wait_ge(ht_dve, tiles_before[2])
                for fp in range(FT // 2):
                    for i in range(2):
                        f = 2 * fp + i
                        if f >= 2:
                            pe.wait_ge(fa_done, f - 1)
                        for m, kind in enumerate(("fg", "fu")):
                            v = slot_view(arrived((kind, fp)), 0, (KD, 256))
                            for k in range(KD):
                                last = k == KD - 1
                                mm(psum[:, 2 * m + f % 2, :], v[:, k, i * P:(i + 1) * P], h_t[:, k, :],
                                   start=(k == 0), stop=last, sig=fg_mm if last and m == 1 else None,
                                   free=last and i == 1)
                    if 2 <= fp < 8:
                        mod_block((1, fp - 2))
                        mod_reduce((1, fp - 2))
                for dh in range(2):
                    for fg in range(0, FT, 4):
                        n = min(4, FT - fg)
                        v = slot_view(arrived(("fd", dh, fg)), 0, (n, 512))
                        for f in range(fg, fg + n):
                            if dh == 0:
                                pe.wait_ge(fa_done, f + 1)
                            for t in range(TT):
                                if f == 0 and dh == 0 and t == 0:
                                    pe.wait_ge(mod_done, mod_at[(1, 5)] + 1)
                                mm(psum[:, (4 if dh == 0 else 0) + t, :], a_t[:, f, t * P:(t + 1) * P], v[:, f - fg, :],
                                   start=(f == 0), stop=(f == FT - 1), sig=fd_mm if f == FT - 1 else None,
                                   free=(f == fg + n - 1 and t == TT - 1))

            def router():
                pe.wait_ge(ht_act, tiles_before[4])
                pe.wait_ge(ht_dve, tiles_before[4])
                for t in range(2):
                    for k in range(KD):
                        mm(psum[:, t, 0:NE], h_t[:, k, CTX + t * P:CTX + (t + 1) * P], w_router[:, k, :],
                           start=(k == 0), stop=(k == KD - 1), sig=r_mm if k == KD - 1 else None)
                pe.wait_ge(r_taken, 1)
                mm(psum[:, 2, 0:NE], tri, taken[:, 0, :], start=True, stop=True)
                mm(psum[:, 3, 0:NE], one.to_broadcast([P, P]), taken[:, 0, :], start=True, stop=False)
                mm(psum[:, 3, 0:NE], tri, taken[:, 1, :], start=False, stop=True)
                mm(psum[:, 4, 0:NE], one.to_broadcast([P, P]), taken[:, 0, :], start=True, stop=False)
                mm(psum[:, 4, 0:NE], one.to_broadcast([P, P]), taken[:, 1, :], start=False, stop=True, sig=r_mm)

            def gather():
                for half, b in ((0, 1), (1, 3)):
                    for k in range(4):
                        d0 = (4 * half + k) * P
                        for t in range(2):
                            mm(psum[:, b, k * P:(k + 1) * P], xn[:, t, d0:d0 + P], sel_tok[:, t, :],
                               start=(t == 0), stop=(t == 1), sig=xg_mm if k == 3 and t == 1 else None)

            def scatter():
                n = 0
                for t in range(2):
                    for dh in range(2):
                        mm(psum[:, 4 + n, :], sel_slot[:, t, :], y_sb[:, dh * 512:(dh + 1) * 512],
                           start=True, stop=True, sig=sc_mm)
                        n += 1

            def experts():
                pe.wait_ge(route_ready, 1)
                jobs = pe.value_load(n_jobs_i[0:1, 0:1], min_val=NE, max_val=JOBS)
                pe.wait_ge(sel_ready, 1)
                gather()
                base = [arrive_total[s] for s in range(SLOTS)]
                with pe.Fori(0, jobs) as j:
                    c = [0]

                    def chunk(shape):
                        n = n_static + c[0]
                        turn = c[0] // SLOTS + 1
                        pe.wait_ge(landed[n % SLOTS], j * (16 * SLOT_TURNS) + (base[n % SLOTS] + 16 * turn))
                        c[0] += 1
                        return slot_view(n, 0, shape)

                    def gate_or_up(fc, b, sig):
                        for h in range(2):
                            v = chunk((4, 512))
                            for k in range(4):
                                last = h == 1 and k == 3
                                mm(psum[:, b + fc % 2, :], xg_t[:, 4 * h + k, :], v[:, k, :],
                                   start=(h == 0 and k == 0), stop=last, sig=sig if last else None, free=(k == 3))

                    def turn_a(fc):
                        pe.wait_ge(a_ok, j * NFC + (fc + 1))
                        for i in range(4):
                            ins = pe.transpose(psum[:, 4, i * P:(i + 1) * P], e_a[:, fc % 2, i * P:(i + 1) * P], ident)
                        ins.then_inc(at_mm, 1)

                    def down(fc):
                        pe.wait_ge(at_ok, j * NFC + (fc + 1))
                        for h in range(2):
                            v = chunk((2, D))
                            for f in range(2):
                                for dh in range(2):
                                    first = fc == 0 and h == 0 and f == 0
                                    last = fc == NFC - 1 and h == 1 and f == 1
                                    mm(psum[:, 6 + dh, :], e_at[:, fc % 2, 2 * h + f, :],
                                       v[:, f, dh * 512:(dh + 1) * 512], start=first, stop=last,
                                       sig=ye_mm if last and dh == 1 else None, free=(f == 1 and dh == 1),
                                       skip_group_check=True)

                    pe.wait_ge(xg_act, j + 1)
                    pe.wait_ge(xg_dve, j + 1)
                    for fc in range(NFC):
                        if fc >= 2:
                            pe.wait_ge(a_ok, j * NFC + (fc - 1))
                        gate_or_up(fc, 0, None)
                        if fc == 1:
                            pe.wait_ge(sc_ok, j * 4 + 4)
                        if fc >= 1:
                            turn_a(fc - 1)
                        gate_or_up(fc, 2, gu_mm)
                        if fc == 0:
                            pe.wait_ge(y_dve, j + 1)
                            pe.wait_ge(st_ok, j + 1)
                            scatter()
                        else:
                            down(fc - 1)
                        if fc == 2:
                            for t in range(2):
                                ins = pe.transpose(psum[:, 5, t * P:(t + 1) * P], sel_tok[:, t, :], ident)
                            ins.then_inc(st_mm, 1)
                    pe.wait_ge(sel_ready, j + 2)
                    gather()
                    turn_a(NFC - 1)
                    down(NFC - 1)
                    pe.wait_ge(st_ok, j + 2)
                    mm(psum[:, 5, 0:2], ident, ident[:, 0:2], start=True, stop=True)
                pe.wait_ge(y_dve, jobs + 1)
                scatter()

            arrive_total = per_slot
            pe.wait_ge(consts_in, 48)
            pe.wait_ge(c_ready, 1)
            mod_block((0, 0))
            for cb in range(1, 6):
                mod_reduce((0, cb - 1))
                mod_block((0, cb))
            mod_reduce((0, 5))
            pe.wait_ge(mod_done, 6)
            turn_tiles(0)
            for l in range(DEPTH):
                input_projection(l)
                latent_norms(l)
                fourier(l)
                attention(l)
                merge(l)
                output_projection(l)
                turn_tiles(2 * l + 1)
                if l == 0:
                    dense_mixer()
                    turn_tiles(2)
            router()
            experts()

        @block.scalar
        def _(act):
            own = [0]

            def link(ins):
                own[0] += 1
                ins.then_inc(act_own, 1)
                act.wait_ge(act_own, own[0])

            def mod_copy(b):
                n = mod_at[b]
                act.wait_ge(mod_acc, n + 1)
                if n >= 2:
                    act.wait_ge(mod_sum, n - 1)
                act.activation(mod_pm[:, n % 2, :], psum[:, 4, :], ACT.Copy).then_inc(mod_copied, 1)

            def std(n):
                act.wait_ge(var_ready, n + 1)
                act.activation(ln_std[:, n % 4:n % 4 + 1], ln_mv[:, n % 4, 1:2], ACT.Sqrt, bias=eps)\
                   .then_inc(std_ready, 1)

            def modulate(l, which, t, n):
                act.wait_ge(xn_turned[0], n + 1)
                s, m = t // 2, 2 * (which - 1)
                for k in range(4):
                    ins = act.activation(h_t[:, k, t * P:(t + 1) * P], psum[:, 6, k * P:(k + 1) * P], ACT.Identity,
                                         bias=modcol[:, l, m, k, s:s + 1], scale=modcol[:, l, m + 1, k, s:s + 1])
                ins.then_inc(ht_act, 1)

            def norm_chain(use):
                l, which, tiles = ln_uses[use]
                n = stats_before[use]
                for step, t in chain(tiles):
                    std(n)
                    n += 1
                    if step == "B":
                        modulate(l, which, t, tiles_before[use] + t - tiles[0])

            act.wait_ge(consts_in, 48)
            act.activation(c_sigm, small[:, S_C:S_C + 2 * KD], ACT.Sigmoid).then_inc(c_sig, 1)
            std(0)
            std(1)
            for cb in range(6):
                mod_copy((0, cb))
            act.wait_ge(mod_done, 6)
            for t in range(2, TT):
                std(t)
                modulate(0, 1, t - 2, t - 2)
            modulate(0, 1, 2, 2)
            modulate(0, 1, 3, 3)

            for l in range(DEPTH):
                a = q0[l]
                for i in range(3):
                    act.wait_ge(in_mm[l], i + 1)
                    if i < 2:
                        dst, gcol, c0 = lat_q[:, i, a:NTOK], S_GQ + 2 * l + i, a
                    else:
                        dst, gcol, c0 = lat_kv[:, :], S_GKV + l, 0
                    act.activation(dst, psum[:, i, c0:NTOK], ACT.Copy, scale=small[:, gcol:gcol + 1])
                    act.activation(squares[:, i, c0:NTOK], psum[:, i, c0:NTOK], ACT.Square).then_inc(in_act[l], 1)
                for i, (c0, n) in enumerate(((a, Q_LORA), (0, KV_LORA))):
                    act.wait_ge(rms_mm[l], i + 1)
                    act.activation(rms[:, i, c0:NTOK], psum[:, 4 + i, c0:NTOK], ACT.Sqrt, bias=eps, scale=1.0 / n)\
                       .then_inc(rms_act[l], 1)
                units = FG * (2 if l == 0 else 1)
                for n in range(units):
                    act.wait_ge(f1_mm[l], n + 1)
                    if n >= 2:
                        act.wait_ge(f2_mm[l], n - 1)
                    act.activation(dft_1[:, n % 2, :, :], psum[:, n % 2, :], ACT.Copy).then_inc(f1_act[l], 1)

                plan, tiles, att = plans[l]

                def fill(g, i):
                    n = 8 * g + i
                    if i == 4:
                        return
                    act.wait_ge(fill_mm[l], n + 1)
                    b = i % 2
                    if g >= 2 and i in (1, 6):
                        act.wait_ge(pv_mm[l], len(att) // 4 * (g - 1))
                    if i == 0:
                        if g >= 1:
                            act.wait_ge(fill_dve[l], dve_fills(g - 1, 4))
                        else:
                            act.wait_ge(kr_done[l], 1)
                            act.wait_ge(kr_copied[l], 1)
                        act.activation(q_rope[:, a:NTOK], psum[:, b, a:NTOK], ACT.Copy).then_inc(fill_act[l], 1)
                    elif i in (1, 2):
                        h = 2 * (i - 1)
                        act.activation(q_t[0:NOPE, g % 2, h, a:NTOK], psum[0:NOPE, b, a:NTOK], ACT.Copy)\
                           .then_inc(fill_act[l], 1)
                    elif i in (3, 5):
                        h = 0 if i == 3 else 2
                        act.activation(k_t[0:NOPE, g % 2, h, :], psum[0:NOPE, b, :], ACT.Copy).then_inc(fill_act[l], 1)
                    else:
                        act.activation(v_sb[:, g % 2, 2 * (i - 6):2 * (i - 5), :], psum[:, b, :], ACT.Copy)\
                           .then_inc(fill_act[l], 1)

                def exp(c):
                    s = tiles[c][4]
                    nk = CTX if s == 0 else NTOK
                    act.wait_ge(s_max[l], c + 1)
                    if c >= 3:
                        act.wait_ge(t_mm[l], c - 2)
                    act.activation(reg_p[:, c % 3, 0:nk], psum[:, 2 + c % 2, 0:nk], ACT.Exp,
                                   bias=s_neg[:, c % 4:c % 4 + 1], scale=SM_SCALE,
                                   accum_out=s_sum[:, c % 4:c % 4 + 1]).then_inc(s_exp[l], 1)

                def turned(c):
                    u, g, _, h, s, qt = tiles[c]
                    nt = 2 if s == 0 else 4
                    act.wait_ge(t_mm[l], c + 1)
                    if u >= 2:
                        act.wait_ge(pv_mm[l], u - 1)
                    act.activation(p_t[:, u % 2, h, 0:nt, qt * P:(qt + 1) * P],
                                   psum[:, 4 + c % 2, 0:nt * P].rearrange("p (k n) -> p k n", k=nt), ACT.Copy)\
                       .then_inc(t_out[l], 1)

                for step in plan:
                    if step[0] == "fill":
                        fill(step[1], step[2])
                    elif step[0] == "score":
                        exp(step[1])
                    elif step[0] == "turn":
                        turned(step[1])

                for jj in range(4):
                    for i in range(4):
                        act.wait_ge(g_mm[l], 8 * jj + i + 1)
                        if jj >= 1:
                            act.wait_ge(g_mul[l], 4 * (jj - 1) + i + 1)
                        act.activation(sig_b[:, i, a:NTOK], psum[:, i, a:NTOK], ACT.Sigmoid).then_inc(g_sig[l], 1)
                    for cb in MERGE_MOD[jj]:
                        mod_copy((l, cb))
                norm_chain(2 * l + 1)

                if l == 0:
                    for f in range(FT):
                        act.wait_ge(fg_mm, f + 1)
                        if f >= 2:
                            act.wait_ge(fa_done, f - 1)
                        act.activation(ff_b[:, f % 2, :], psum[:, f % 2, :], ACT.Sigmoid).then_inc(fg_sig, 1)
                        if f % 2 and 2 <= f // 2 < 8:
                            mod_copy((1, f // 2 - 2))
                    norm_chain(2)

            act.wait_ge(r_diff, 1)
            act.activation(pair_w[:, :, 1], pair_w[:, :, 0], ACT.Exp).then_inc(r_exp, 1)
            act.wait_ge(route_ready, 1)
            jobs = act.value_load(n_jobs_i[0:1, 0:1], min_val=NE, max_val=JOBS)

            def gathered(n):
                act.wait_ge(xg_mm, n)
                for k in range(4):
                    ins = act.activation(xg_t[:, k, :], psum[:, 1, k * P:(k + 1) * P], ACT.Identity,
                                         bias=modcol[:, 1, 2, k, 1:2], scale=modcol[:, 1, 3, k, 1:2])
                ins.then_inc(xg_act, 1)

            def turned_a(j, fc):
                act.wait_ge(at_mm, j * NFC + (fc + 1))
                act.activation(e_at[:, fc % 2, :, :].rearrange("p f n -> p (f n)"), psum[:, 4, :], ACT.Copy)\
                   .then_inc(at_ok, 1)

            gathered(2)
            with act.Fori(0, jobs) as j:
                for fc in range(NFC):
                    if fc >= 1:
                        turned_a(j, fc - 1)
                    act.wait_ge(gu_mm, j * NFC + (fc + 1))
                    if fc >= 2:
                        act.wait_ge(a_ok, j * NFC + (fc - 1))
                    act.activation(e_sig[:, fc % 2, :], psum[:, fc % 2, :], ACT.Sigmoid).then_inc(e_sig_ok, 1)
                gathered(j * 2 + 4)
                turned_a(j, NFC - 1)
            for t in range(2):
                std(stats_before[4] + t)

        @block.vector
        def _(dve):
            own = [0]

            def link(ins):
                own[0] += 1
                ins.then_inc(dve_own, 1)
                dve.wait_ge(dve_own, own[0])

            def mod_take(b):
                l, cb = b
                n = mod_at[b]
                dve.wait_ge(mod_sum, n + 1)
                if cb in (4, 5, 10, 11):
                    gate = gate1 if cb < 6 else gate2
                    c0 = (cb % 2) * 512
                    dve.tensor_copy(gate[:, 0, c0:c0 + 512], psum[:, 5, :])
                    dve.tensor_copy(gate[:, 1, c0:c0 + 512], psum[:, 6, :]).then_inc(mod_done, 1)
                else:
                    m = {0: 0, 2: 1, 6: 2, 8: 3}[cb - cb % 2]
                    dst = modcol[:, l, m, 4 * (cb % 2):4 * (cb % 2) + 4, :]
                    src = psum[:, 5, 0:8].rearrange("p (k s) -> p k s", s=2)
                    dve.tensor_scalar(dst, src, float(m % 2), None, ALU.add).then_inc(mod_done, 1)

            def normalise(n, src, dst, sig):
                dve.bn_stats(bn[:, 0, :], src[:, 0:512])
                link(dve.bn_stats(bn[:, 1, :], src[:, 512:1024]))
                dve.bn_aggr(ln_mv[:, n % 4, :], bn).then_inc(var_ready, 1)
                dve.wait_ge(std_ready, n + 1)
                link(dve.reciprocal(ln_rstd[:, n % 4:n % 4 + 1], ln_std[:, n % 4:n % 4 + 1]))
                dve.tensor_scalar(dst, src, ln_mv[:, n % 4, 0:1], ln_rstd[:, n % 4:n % 4 + 1],
                                  ALU.subtract, ALU.mult).then_inc(sig, 1)

            def modulate(l, which, t, n):
                dve.wait_ge(xn_turned[1], n + 1)
                s, m = t // 2, 2 * (which - 1)
                for k in range(4):
                    ins = dve.tensor_scalar(h_t[:, 4 + k, t * P:(t + 1) * P], psum[:, 7, k * P:(k + 1) * P],
                                            modcol[:, l, m + 1, 4 + k, s:s + 1], modcol[:, l, m, 4 + k, s:s + 1],
                                            ALU.mult, ALU.add)
                ins.then_inc(ht_dve, 1)

            def norm_b(use, t, n):
                _, _, tiles = ln_uses[use]
                at_b = tiles_before[use] + t - tiles[0]
                if use:
                    dve.wait_ge(x_new, norms_before[use] + t - tiles[0] + 1)
                if at_b >= 2:
                    dve.wait_ge(xn_turned[1], at_b - 1)
                normalise(n, x_res[:, t, :], xn[:, t % 2, :], xn_ready)

            def residual(t, dh, y, gate, sig):
                cols = slice(dh * 512, (dh + 1) * 512)
                ins = dve.tensor_tensor(reg_r[:, dh, :], y, gate[:, t // 2, cols], ALU.mult)
                if sig is None:
                    link(ins)
                else:
                    ins.then_inc(sig[0], 1)
                    dve.wait_ge(sig[0], sig[1])
                link(dve.scalar_tensor_tensor(out=x_res[:, t, cols], in0=x_res[:, t, cols], scalar=ALPHA,
                                              in1=reg_r[:, dh, :], op0=ALU.mult, op1=ALU.add))

            def norm_chain(use, add):
                l, which, tiles = ln_uses[use]
                n = stats_before[use]
                a = norms_before[use]
                turned = []
                for step, t in chain(tiles):
                    if step == "A":
                        add(t)
                        if t - tiles[0] >= 2:
                            dve.wait_ge(x_new, a + t - tiles[0] - 1)
                        normalise(n, x_res[:, t, :], z_sb[:, t % 2, :], z_scaled)
                    else:
                        norm_b(use, t, n)
                        if t > tiles[0]:
                            modulate(l, which, t - 1, tiles_before[use] + t - 1 - tiles[0])
                    n += 1
                modulate(l, which, tiles[-1], tiles_before[use] + len(tiles) - 1)

            link(dve.memset(c_act[:, :, :], 0.0))
            dve.wait_ge(c_sig, 1)
            dve.tensor_tensor(c_act[:, :, 0:2], c_raw, c_sigm.rearrange("p (k s) -> p k s", s=2), ALU.mult)\
               .then_inc(c_ready, 1)
            for t in range(2):
                dve.wait_ge(x_in[t], 16)
                norm_b(0, t, t)
            for cb in range(6):
                mod_take((0, cb))
            for t in range(2, TT):
                dve.wait_ge(x_in[t], 16)
                norm_b(0, t, t)
                modulate(0, 1, t - 2, t - 2)
            modulate(0, 1, 2, 2)
            modulate(0, 1, 3, 3)

            for l in range(DEPTH):
                a = q0[l]
                dve.wait_ge(in_mm[l], 4)
                dve.tensor_copy(k_rope[64:96, :], psum[64:96, 3, :]).then_inc(in_dve[l], 1)
                for i in range(4):
                    dve.wait_ge(in_mm[l], 5 + i)
                    dve.tensor_copy(u_t[:, i, a:NTOK], psum[:, i, a:NTOK]).then_inc(in_dve[l], 1)
                dve.wait_ge(rms_act[l], 2)
                dve.reciprocal(rms[:, 0, a:NTOK], rms[:, 0, a:NTOK])
                link(dve.reciprocal(rms[:, 1, :], rms[:, 1, :]))
                for k in range(2):
                    dve.tensor_tensor(lat_q[:, k, a:NTOK], lat_q[:, k, a:NTOK], rms[:, 0, a:NTOK], ALU.mult)
                dve.tensor_tensor(lat_kv[:, :], lat_kv[:, :], rms[:, 1, :], ALU.mult).then_inc(lat_done[l], 1)
                dve.wait_ge(kr_perm[l], 1)
                dve.tensor_tensor(rope_a[64:96, :], k_rope[64:96, :], cos[64:96, :], ALU.mult)
                link(dve.tensor_tensor(rope_b[64:96, :], psum[64:96, 6, :], sin[64:96, :], ALU.mult))
                dve.tensor_tensor(k_rope[64:96, :], rope_a[64:96, :], rope_b[64:96, :], ALU.add).then_inc(kr_sum[l], 1)
                dve.wait_ge(kr_sum[l], 1)
                for h in range(4):
                    ins = dve.tensor_copy(k_t[64:96, 0, h, :], k_rope[64:96, :])
                ins.then_inc(kr_done[l], 1)
                units = [(g, s) for g in range(FG) for s in ((0, 1) if l == 0 else (1,))]
                for n, (g, s) in enumerate(units):
                    dve.wait_ge(f2_mm[l], n + 1)
                    dve.tensor_copy(four_t[:, g, s * SEQ:(s + 1) * SEQ], psum[:, 2 + n % 2, 0:SEQ])\
                       .then_inc(f2_dve[l], 1)

                plan, tiles, att = plans[l]

                def fill(g, i):
                    if i not in (1, 2, 3, 4, 5):
                        return
                    dve.wait_ge(fill_mm[l], 8 * g + i + 1)
                    b = i % 2
                    if g >= 2 and i == 1:
                        dve.wait_ge(pv_mm[l], len(att) // 4 * (g - 1))
                    if i in (1, 2):
                        dve.tensor_copy(q_t[0:NOPE, g % 2, 2 * (i - 1) + 1, a:NTOK], psum[64:128, b, a:NTOK])\
                           .then_inc(fill_dve[l], 1)
                    elif i in (3, 5):
                        dve.tensor_copy(k_t[0:NOPE, g % 2, 1 if i == 3 else 3, :], psum[64:128, b, :])\
                           .then_inc(fill_dve[l], 1)
                    else:
                        link(dve.tensor_tensor(rope_b[:, a:NTOK], psum[:, b, a:NTOK], sin[:, a:NTOK], ALU.mult))
                        dve.wait_ge(rope_cos[l], g + 1)
                        for h in range(4):
                            rows = slice(32 * h, 32 * h + 32)
                            ins = dve.tensor_tensor(q_t[64:96, g % 2, h, a:NTOK], rope_a[rows, a:NTOK],
                                                    rope_b[rows, a:NTOK], ALU.add)
                        ins.then_inc(fill_dve[l], 1)

                def top_score(c):
                    nk = CTX if tiles[c][4] == 0 else NTOK
                    dve.wait_ge(s_mm[l], c + 1)
                    link(dve.reduce_max(s_top[:, c % 4:c % 4 + 1], psum[:, 2 + c % 2, 0:nk], AX.X))
                    dve.tensor_scalar(s_neg[:, c % 4:c % 4 + 1], s_top[:, c % 4:c % 4 + 1], -SM_SCALE, None,
                                      ALU.mult).then_inc(s_max[l], 1)

                def inverse(c):
                    dve.wait_ge(s_exp[l], c + 1)
                    dve.reciprocal(s_inv[:, c % 4:c % 4 + 1], s_sum[:, c % 4:c % 4 + 1]).then_inc(s_rec[l], 1)

                def values(u):
                    g, pair, s = att[u]
                    dve.wait_ge(pv_mm[l], u + 1)
                    dve.tensor_copy(attn_t[:, 2 * g + pair, s * SEQ:(s + 1) * SEQ], psum[:, 6 + u % 2, 0:SEQ])\
                       .then_inc(pv_out[l], 1)

                for step in plan:
                    if step[0] == "fill":
                        fill(step[1], step[2])
                    elif step[0] == "score":
                        top_score(step[1])
                    elif step[0] == "norm":
                        inverse(step[1])
                    elif step[0] == "take":
                        values(step[1])

                for jj in range(4):
                    if jj >= 1:
                        dve.wait_ge(m_done[l], 2 * jj)
                    for i in range(4):
                        dve.wait_ge(g_mm[l], 8 * jj + 4 + i + 1)
                        dve.wait_ge(g_sig[l], 4 * jj + i + 1)
                        dve.tensor_tensor(mrg_b[:, i, a:NTOK], psum[:, i, a:NTOK], sig_b[:, i, a:NTOK], ALU.mult)\
                           .then_inc(g_mul[l], 1)
                    for cb in MERGE_MOD[jj]:
                        mod_take((l, cb))

                def add_mixer(t):
                    i = t - t0[l]
                    dve.wait_ge(y_mm[l], i + 1)
                    residual(t, 0, psum[:, 2 * (i % 2), :], gate1, None)
                    residual(t, 1, psum[:, 2 * (i % 2) + 1, :], gate1, (y_used[l], i + 1))

                dve.wait_ge(ln_in[2 * l], 32)
                norm_chain(2 * l + 1, add_mixer)

                if l == 0:
                    for f in range(FT):
                        dve.wait_ge(fg_sig, f + 1)
                        link(dve.tensor_tensor(ff_b[:, 2 + f % 2, :], ff_b[:, f % 2, :], psum[:, f % 2, :], ALU.mult))
                        dve.tensor_tensor(a_t[:, f, :], ff_b[:, 2 + f % 2, :], psum[:, 2 + f % 2, :], ALU.mult)\
                           .then_inc(fa_done, 1)
                        if f % 2 and 2 <= f // 2 < 8:
                            mod_take((1, f // 2 - 2))
                    for t in range(TT):
                        dve.wait_ge(fd_mm, t + 1)
                        residual(t, 0, psum[:, 4 + t, :], gate2, None)

                    def add_dense(t):
                        dve.wait_ge(fd_mm, TT + t + 1)
                        residual(t, 1, psum[:, t, :], gate2, None)

                    norm_chain(2, add_dense)

            dve.wait_ge(route_in, 32)
            dve.wait_ge(r_mm, 2)
            for t in range(2):
                link(dve.tensor_tensor(logits[:, t, :], psum[:, t, 0:NE], b_rout, ALU.add))
                link(dve.max(top[:, t, :], logits[:, t, :]))
                link(dve.max_index(top_i[:, t, :].bitcast(U32), top[:, t, :], logits[:, t, :]))
                link(dve.tensor_copy(top_if[:, t, :], top_i[:, t, :].bitcast(U32)))
            dve.tensor_tensor(pair_w[:, :, 0], top[:, :, 1], top[:, :, 0], ALU.subtract).then_inc(r_diff, 1)
            dve.wait_ge(r_exp, 1)
            link(dve.tensor_scalar(pair_w[:, :, 3], pair_w[:, :, 1], 1.0, None, ALU.add))
            link(dve.reciprocal(pair_w[:, :, 2], pair_w[:, :, 3]))
            link(dve.tensor_tensor(pair_w[:, :, 3], pair_w[:, :, 2], pair_w[:, :, 1], ALU.mult))
            for t in range(2):
                for k in range(2):
                    link(dve.tensor_scalar(hot[:, t, k, :], e_num, top_if[:, t, k:k + 1], None, ALU.is_equal))
                link(dve.tensor_scalar(tmp8[:, t, :], hot[:, t, 1, :], pair_w[:, t, 3:4], None, ALU.mult))
                link(dve.scalar_tensor_tensor(out=comb[:, t, :], in0=hot[:, t, 0, :], scalar=pair_w[:, t, 2:3],
                                              in1=tmp8[:, t, :], op0=ALU.mult, op1=ALU.add))
            dve.tensor_tensor(taken[:, :, :], hot[:, :, 0, :], hot[:, :, 1, :], ALU.add).then_inc(r_taken, 1)
            dve.memset(job_at, -1.0)
            dve.memset(job_w, 0.0)
            link(dve.memset(job_e, 0.0))
            dve.tensor_copy(job_e[:, 0:NE], e_num)
            dve.memset(f_acc, 0.0)
            dve.memset(sel_slot, 0.0).then_inc(st_ok, 1)
            dve.memset(y_sb, 0.0).then_inc(y_dve, 1)
            link(dve.memset(rank, 0.0))
            dve.wait_ge(r_taken, 1)
            dve.wait_ge(r_mm, 3)
            for t in range(2):
                link(dve.scalar_tensor_tensor(out=place[:, t, :], in0=psum[:, 2 + t, 0:NE], scalar=1.0,
                                              in1=taken[:, t, :], op0=ALU.add, op1=ALU.mult))
            link(dve.tensor_scalar(place[:, :, :], place[:, :, :], -1.0, None, ALU.add))
            dve.tensor_copy(job_at[:, :, 0:NE], place[:, :, :])
            dve.tensor_copy(job_w[:, :, 1:NE + 1], comb[:, :, :])
            link(dve.tensor_scalar(over, psum[:, 4, 0:NE], float(P), None, ALU.is_gt))
            for e in range(1, NE):
                link(dve.tensor_tensor(rank[:, e:e + 1], rank[:, e - 1:e], over[:, e - 1:e], ALU.add))
            link(dve.tensor_tensor(n_jobs, rank[:, NE - 1:NE], over[:, NE - 1:NE], ALU.add))
            link(dve.tensor_scalar(n_jobs, n_jobs, float(NE), None, ALU.add))
            for r in range(3):
                link(dve.scalar_tensor_tensor(out=hit, in0=rank, scalar=float(r), in1=over, op0=ALU.is_equal,
                                              op1=ALU.mult))
                link(dve.tensor_tensor(tmp8[:, 0, :], hit, e_num, ALU.mult))
                link(dve.reduce_sum(job_e[:, NE + r:NE + r + 1], tmp8[:, 0, :], AX.X))
                for t in range(2):
                    link(dve.scalar_tensor_tensor(out=tmp8[:, 0, :], in0=place[:, t, :], scalar=-float(P), in1=hit,
                                                  op0=ALU.add, op1=ALU.mult))
                    link(dve.reduce_sum(job_at[:, t, NE + r:NE + r + 1], tmp8[:, 0, :], AX.X))
                    link(dve.tensor_tensor(tmp8[:, 1, :], comb[:, t, :], hit, ALU.mult))
                    link(dve.reduce_sum(job_w[:, t, NE + 1 + r:NE + 2 + r], tmp8[:, 1, :], AX.X))
            dve.tensor_copy(job_ei, job_e)
            dve.tensor_copy(n_jobs_i, n_jobs).then_inc(route_ready, 1)
            dve.wait_ge(route_ready, 1)
            jobs = dve.value_load(n_jobs_i[0:1, 0:1], min_val=NE, max_val=JOBS)

            def select(j):
                for t in range(2):
                    ins = dve.tensor_scalar(sel_tok[:, t, :], iota, job_at[:, t, bass.ds(j, 1)], None, ALU.is_equal)
                ins.then_inc(sel_ready, 1)

            def gathered(n):
                dve.wait_ge(xg_mm, n)
                for k in range(4):
                    ins = dve.tensor_scalar(xg_t[:, 4 + k, :], psum[:, 3, k * P:(k + 1) * P],
                                            modcol[:, 1, 3, 4 + k, 1:2], modcol[:, 1, 2, 4 + k, 1:2],
                                            ALU.mult, ALU.add)
                ins.then_inc(xg_dve, 1)

            def weigh(j):
                n = 0
                for t in range(2):
                    for dh in range(2):
                        dve.wait_ge(sc_mm, j * 4 + (n + 1))
                        acc = f_acc[:, t, dh * 512:(dh + 1) * 512]
                        dve.scalar_tensor_tensor(out=acc, in0=psum[:, 4 + n, :], scalar=job_w[:, t, bass.ds(j, 1)],
                                                 in1=acc, op0=ALU.mult, op1=ALU.add).then_inc(sc_ok, 1)
                        n += 1

            select(0)
            gathered(2)
            with dve.Fori(0, jobs) as j:
                for fc in range(NFC):
                    dve.wait_ge(e_sig_ok, j * NFC + (fc + 1))
                    dve.tensor_tensor(e_tmp, e_sig[:, fc % 2, :], psum[:, fc % 2, :], ALU.mult).then_inc(e_tmp_ok, 1)
                    dve.wait_ge(e_tmp_ok, j * NFC + (fc + 1))
                    if fc >= 2:
                        dve.wait_ge(at_mm, j * NFC + (fc - 1))
                    dve.tensor_tensor(e_a[:, fc % 2, :], e_tmp, psum[:, 2 + fc % 2, :], ALU.mult).then_inc(a_ok, 1)
                    if fc == 0:
                        weigh(j)
                    if fc == 2:
                        dve.wait_ge(st_mm, j + 1)
                        dve.tensor_copy(sel_slot.rearrange("p t n -> p (t n)"), psum[:, 5, 0:2 * P]).then_inc(st_ok, 1)
                    if fc == 3:
                        select(j + 1)
                gathered(j * 2 + 4)
                dve.wait_ge(ye_mm, j + 1)
                dve.tensor_copy(y_sb, psum[:, 6:8, :].rearrange("p b n -> p (b n)")).then_inc(y_dve, 1)
            weigh(jobs)
            dve.wait_ge(sc_ok, jobs * 4 + 4)
            for t in range(2):
                for dh in range(2):
                    residual(2 + t, dh, f_acc[:, t, dh * 512:(dh + 1) * 512], gate2, None)
                if t == 0:
                    dve.wait_ge(ln_in[3], 32)
                normalise(stats_before[4] + t, x_res[:, 2 + t, :], z_sb[:, t, :], z_scaled)

        @block.gpsimd
        def _(pool):
            def weights_of(use, t, i):
                n = norms_before[use] + i
                pool.wait_ge(z_scaled, n + 1)
                if i == 0:
                    pool.wait_ge(ln_in[use - 1], 32)
                pool.tensor_tensor(z_sb[:, t % 2, :], z_sb[:, t % 2, :], ln_rows[:, 0, :], ALU.mult)\
                    .then_inc(pool_own, 1)
                pool.wait_ge(pool_own, n + 1)
                pool.tensor_tensor(x_res[:, t, :], z_sb[:, t % 2, :], ln_rows[:, 1, :], ALU.add).then_inc(x_new, 1)

            for l in range(DEPTH):
                a = q0[l]
                pool.wait_ge(kr_sum[l], 1)
                for h in range(4):
                    ins = pool.tensor_copy(k_t[64:96, 1, h, :], k_rope[64:96, :])
                ins.then_inc(kr_copied[l], 1)
                plan, tiles, att = plans[l]
                for step in plan:
                    if step[0] == "fill" and step[2] == 4:
                        g = step[1]
                        pool.wait_ge(fill_act[l], act_fills(g, 0))
                        if g >= 1:
                            pool.wait_ge(fill_dve[l], dve_fills(g - 1, 4))
                        pool.tensor_tensor(rope_a[:, a:NTOK], q_rope[:, a:NTOK], cos[:, a:NTOK], ALU.mult)\
                            .then_inc(rope_cos[l], 1)
                    elif step[0] == "norm":
                        c = step[1]
                        nk = CTX if tiles[c][4] == 0 else NTOK
                        pool.wait_ge(s_rec[l], c + 1)
                        pool.tensor_scalar(reg_p[:, c % 3, 0:nk], reg_p[:, c % 3, 0:nk], s_inv[:, c % 4:c % 4 + 1],
                                           1.0, ALU.mult, ALU.mult).then_inc(s_nrm[l], 1)
                for jj in range(4):
                    pool.wait_ge(g_mul[l], 4 * jj + 4)
                    for i in range(2):
                        pool.tensor_tensor(merged[:, 2 * jj + i, a:NTOK], mrg_b[:, i, a:NTOK], mrg_b[:, 2 + i, a:NTOK],
                                           ALU.add).then_inc(m_done[l], 1)
                for use in ((1, 2), (3,))[l]:
                    for i, t in enumerate(ln_uses[use][2]):
                        weights_of(use, t, i)
            for t in range(2):
                weights_of(4, 2 + t, t)


def constants():
    c = np.zeros((P, C_END), np.float64)
    c[:, C_ID:C_ID + P] = np.eye(P)
    k = np.arange(FC)
    ang = 2 * np.pi * ((k[:, None] * k[None, :]) % FC) / FC
    c[:, C_DFTC:C_DFTC + FC] = np.cos(ang) / np.sqrt(FC)
    c[:, C_DFTC + FC:C_DFTC + 2 * FC] = np.sin(ang) / np.sqrt(FC)
    k = np.arange(SEQ)
    ang = 2 * np.pi * ((k[:, None] * k[None, :]) % SEQ) / SEQ
    both = np.stack([np.cos(ang), -np.sin(ang)], 1) / np.sqrt(SEQ)
    c[:, C_DFTT:C_DFTT + 4 * SEQ] = both.reshape(2, P, 2, SEQ).transpose(1, 0, 2, 3).reshape(P, -1)
    nf = ROPE // 4
    pos = np.stack([np.arange(SEQ) // 64, np.arange(SEQ) % 64]).astype(np.float32)
    inv = (1.0 / (np.float32(10000.0) ** (np.arange(nf, dtype=np.float32) / nf))).astype(np.float32)
    ang = (pos[:, None, :] * inv[None, :, None]).astype(np.float32).astype(np.float64)
    ang = np.tile(np.repeat(ang[:, None], 2, axis=1).reshape(ROPE, SEQ), (4, 1))
    c[:, C_COS:C_COS + CTX] = 1.0
    c[:, C_COS + CTX:C_COS + NTOK] = np.cos(ang)
    c[:, C_SIN + CTX:C_SIN + NTOK] = np.sin(ang)
    for m in range(P):
        first = m // nf % 2 == 0
        c[m + nf if first else m - nf, C_PERM + m] = -1.0 if first else 1.0
    for j in range(4):
        c[32 * j, C_SEL] = 1.0
        c[32 * j + 1, C_SEL + 1] = 1.0
    c[:, C_ONE] = 1.0
    c[:, C_EPS] = EPS
    r = np.zeros((P, R_END))
    r[:, R_IOTA:R_IOTA + P] = np.arange(P)[None]
    r[:, R_TRI:R_TRI + P] = np.triu(np.ones((P, P)), 1)
    r[:, R_E:R_E + NE] = np.arange(NE)[None]
    return c.astype(np.float32), r.astype(np.float32)


def small_inputs(c, c_ctx, g_q, g_kv, w_router):
    both = np.stack([c_ctx, c[0]], -1).reshape(KD, P, 2).transpose(1, 0, 2).reshape(P, -1)
    gq = g_q.reshape(DEPTH, 2, P).transpose(2, 0, 1).reshape(P, -1)
    gkv = g_kv.reshape(DEPTH, P).T
    router = w_router[0].reshape(KD, P, NE).transpose(1, 0, 2).reshape(P, -1)
    return np.ascontiguousarray(np.concatenate([both, gq, gkv, router], 1))


def query_weights(w_uq):
    v = w_uq.reshape(DEPTH, Q_LORA, 4, 4, QK)
    parts = [v[..., NOPE:].reshape(DEPTH, Q_LORA, 4, -1), v[..., :NOPE].reshape(DEPTH, Q_LORA, 4, -1)]
    return np.ascontiguousarray(np.concatenate(parts, -1).reshape(DEPTH, Q_LORA, -1))


_IN_DRAM = ["x", "ctx", "w_mod", "b_mod", "w_in", "w_uk", "w_uv", "w_ao", "w_fo", "w_out", "ln1_g", "ln1_b",
            "ln2_g", "ln2_b", "w_ff_gate", "w_ff_up", "w_ff_down", "b_router", "w_e_gate", "w_e_up", "w_e_down"]


def kernel(**inputs):
    import concourse.bacc as bacc
    from concourse.bass_utils import run_bass_kernel_spmd

    nc = bacc.Bacc("TRN2", target_bir_lowering=False, num_devices=1, dynamic_dma_scratch_size=1024)
    arrays = {n: np.ascontiguousarray(inputs[n]) for n in _IN_DRAM}
    arrays["const"], arrays["route"] = constants()
    arrays["small"] = small_inputs(*(np.asarray(inputs[n]) for n in ("c", "c_ctx", "g_q", "g_kv", "w_router")))
    arrays["w_uq"] = query_weights(np.asarray(inputs["w_uq"]))
    w = {n: nc.dram_tensor(f"in_{n}", a.shape, F32, kind="ExternalInput").ap() for n, a in arrays.items()}
    out = nc.dram_tensor("out_x", (1, SEQ, D), F32, kind="ExternalOutput").ap()
    build(nc, w, out)
    r = run_bass_kernel_spmd(nc, [{f"in_{n}": a for n, a in arrays.items()}], core_ids=[0])
    return r.results[0]["out_x"]
```

```python
from contextlib import ExitStack

import numpy as np

import concourse.bass as bass
from concourse import mybir

ALU = mybir.AluOpType
ACT = mybir.ActivationFunctionType
AX = mybir.AxisListType
F32 = mybir.dt.float32
F32R = mybir.dt.float32r
I32 = mybir.dt.int32
U32 = mybir.dt.uint32

P = 128
D = 1024
KD = D // P
SEQ = 256
CTX = 256
NTOK = SEQ + CTX
TT = NTOK // P
DEPTH = 2
HEADS = 16
NOPE = 64
ROPE = 32
QK = NOPE + ROPE
VH = 64
Q_LORA = 256
KV_LORA = 128
FG = 4
FC = 128
OFF_KV = Q_LORA
OFF_KR = OFF_KV + KV_LORA
OFF_F = OFF_KR + ROPE
OFF_G = OFF_F + FG * FC
D_FF = 2816
FT = D_FF // P
NE = 8
D_FE = 3584
SM_SCALE = float(QK) ** -0.5
ALPHA = float((2 * DEPTH) ** 0.25)
EPS = 1e-6

SLOTS = 4
SLOT = 2048
HIS = 3
SPLIT = ("out", "fg", "fu", "fd")
LO_DVE = SLOT * 3 // 4
NFC = D_FE // 512
JOB_CHUNKS = 6 * NFC
E_SLOTS = SLOTS + 2
assert JOB_CHUNKS % E_SLOTS == 0 and JOB_CHUNKS % HIS == 0
SLOT_TURNS = JOB_CHUNKS // E_SLOTS
JOBS = 16

C_ID = 0
C_DFTC = C_ID + P
C_DFTT = C_DFTC + 2 * FC
C_COS = C_DFTT + 4 * SEQ
C_SIN = C_COS + NTOK
C_PERM = C_SIN + NTOK
C_SEL = C_PERM + P
C_ONE = C_SEL + 2
C_EPS = C_ONE + 1
C_END = C_EPS + 1
S_C = 0
S_GQ = S_C + 2 * KD
S_GKV = S_GQ + 2 * DEPTH
S_ROUTER = S_GKV + DEPTH
S_END = S_ROUTER + KD * NE
R_IOTA = 0
R_TRI = R_IOTA + P
R_E = R_TRI + P
R_END = R_E + NE


def ring_chunks(w):
    chunks = []

    def mod(l, cb):
        v = w["w_mod"][l].rearrange("(h k p) n -> h p k n", h=2, p=P)
        for h in range(2):
            chunks.append((("mod", l, cb, h), [(0, (4, 512), v[h, :, :, cb * 512:(cb + 1) * 512])]))

    def rows(name, v, k, c0, n):
        chunks.append((name, [(0, (k, n), v.rearrange("(k p) n -> p k n", p=P)[:, :, c0:c0 + n])]))

    for cb in range(6):
        mod(0, cb)
    for l in range(DEPTH):
        w_in = w["w_in"][l]
        rows(("in", l, 0), w_in, KD, 0, Q_LORA)
        rows(("in", l, 1), w_in, KD, OFF_KV, KV_LORA + ROPE)
        rows(("in", l, 2), w_in, KD, OFF_F, 2 * FC)
        rows(("in", l, 3), w_in, KD, OFF_F + 2 * FC, 2 * FC)
        for g in range(4):
            uq = w["w_uq"][l].rearrange("(k p) n -> p k n", p=P)[:, :, g * 4 * QK:(g + 1) * 4 * QK]
            uk = w["w_uk"][l][:, g * 4 * NOPE:(g + 1) * 4 * NOPE]
            uv = w["w_uv"][l][:, g * 4 * VH:(g + 1) * 4 * VH]
            chunks.append((("heads", l, g), [(0, (2, 4 * QK), uq), (2 * 4 * QK, (256,), uk),
                                             (2 * 4 * QK + 256, (256,), uv)]))
        for jj in range(4):
            rows(("ga", l, jj), w_in, KD, OFF_G + jj * 256, 256)
            rows(("gf", l, jj), w_in, KD, OFF_G + D + jj * 256, 256)
            rows(("ao", l, jj), w["w_ao"][l], KD, jj * 256, 256)
            rows(("fo", l, jj), w["w_fo"][l], FG, jj * 256, 256)
            for cb in MERGE_MOD[jj]:
                mod(l, cb)
        v = w["w_out"][l].rearrange("(g k p) n -> g p k n", k=4, p=P)
        for dh in range(2):
            for kk in range(2):
                chunks.append((("out", l, dh, kk), [(0, (4, 512), v[kk, :, :, dh * 512:(dh + 1) * 512])]))
        if l == 0:
            for fp in range(FT // 2):
                rows(("fg", fp), w["w_ff_gate"][0], KD, fp * 256, 256)
                rows(("fu", fp), w["w_ff_up"][0], KD, fp * 256, 256)
                if 2 <= fp < 8:
                    mod(1, fp - 2)
            down = w["w_ff_down"][0].rearrange("(f p) n -> p f n", p=P)
            for dh in range(2):
                for fg, n in DOWN:
                    chunks.append((("fd", dh, fg), [(0, (n, 512), down[:, fg:fg + n, dh * 512:(dh + 1) * 512])]))
    return chunks


DOWN = [(0, FT % 4)] + [(f, 4) for f in range(FT % 4, FT, 4)]
assert FT % 4 and FT % 2 == 0
MERGE_MOD = ((6,), (7, 10), (8, 11), (9,))


def merged_plan(l):
    streams = (0, 1) if l == 0 else (1,)
    tiles, units = [], []
    for g in range(4):
        for pair in range(2):
            for s in streams:
                u = len(units)
                units.append((g, pair, s))
                tiles += [(u, g, 2 * pair + h, h, s, qt) for h in range(2) for qt in range(2)]
    per_group = len(tiles) // 4
    plan = [("fill", 0, i) for i in range(8)]
    for i in range(len(tiles) + 4):
        if i < len(tiles):
            plan.append(("score", i))
        if 1 <= i <= len(tiles):
            plan.append(("norm", i - 1))
        if 2 <= i < len(tiles) + 2:
            plan.append(("turn", i - 2))
        if i >= 6 and i % 4 == 2:
            plan.append(("pv", i // 4 - 1))
        if i >= 7 and i % 4 == 3:
            plan.append(("take", i // 4 - 1))
        g, at = divmod(i, per_group)
        if g < 3:
            step = per_group // 8
            if at % step == step - 1:
                plan.append(("fill", g + 1, at // step))
    return plan, tiles, units


def build(nc, w, out):
    ctx = ExitStack()
    with ctx:
        def sem(name):
            return ctx.enter_context(nc.semaphore(name))

        const = ctx.enter_context(nc.sbuf_tensor("const", [P, C_END], F32))
        small = ctx.enter_context(nc.sbuf_tensor("small", [P, S_END], F32))
        bmod = ctx.enter_context(nc.sbuf_tensor("bmod", [DEPTH * 12, 512], F32))
        x_res = ctx.enter_context(nc.sbuf_tensor("x_res", [P, TT, D], F32))
        w_hi = ctx.enter_context(nc.sbuf_tensor("w_hi", [P, HIS, SLOT], F32R))
        ring = ctx.enter_context(nc.sbuf_tensor("ring", [P, SLOTS, SLOT], F32))
        h_t = ctx.enter_context(nc.sbuf_tensor("h_t", [P, KD, NTOK], F32))
        at_h = nc.sbuf_base - 4 * KD * NTOK
        at_ring = at_h - 4 * SLOTS * SLOT
        assert (E_SLOTS - SLOTS) * SLOT <= KD * NTOK
        reg_q = ctx.enter_context(nc.sbuf_tensor("reg_q", [P, 12288], F32))
        at_q = nc.sbuf_base - 4 * 12288
        reg_v = ctx.enter_context(nc.sbuf_tensor("reg_v", [P, 2048], F32))
        reg_a = ctx.enter_context(nc.sbuf_tensor("reg_a", [P, 4096], F32))
        at_a = nc.sbuf_base - 4 * 4096
        reg_f = ctx.enter_context(nc.sbuf_tensor("reg_f", [P, 2048], F32))
        at_f = nc.sbuf_base - 4 * 2048
        lat_kv = ctx.enter_context(nc.sbuf_tensor("lat_kv", [P, NTOK], F32))
        at_lat = nc.sbuf_base - 4 * NTOK
        lat_q = ctx.enter_context(nc.sbuf_tensor("lat_q", [P, 2, NTOK], F32))
        reg_p = ctx.enter_context(nc.sbuf_tensor("reg_p", [P, 3, 512], F32))
        reg_r = ctx.enter_context(nc.sbuf_tensor("reg_r", [P, 3, NTOK], F32))
        gate1 = ctx.enter_context(nc.sbuf_tensor("gate1", [P, 2, D], F32))
        gate2 = ctx.enter_context(nc.sbuf_tensor("gate2", [P, 2, D], F32))
        c_act = ctx.enter_context(nc.sbuf_tensor("c_act", [P, KD, 32], F32))
        modcol = ctx.enter_context(nc.sbuf_tensor("modcol", [P, DEPTH, 4, KD, 2], F32))
        stat = ctx.enter_context(nc.sbuf_tensor("stat", [P, 80], F32))
        bn = stat[:, 0:12].rearrange("p (a b) -> p a b", a=2)
        ln_mv = stat[:, 12:20].rearrange("p (n a) -> p n a", a=2)
        ln_std = stat[:, 20:24]
        ln_rstd = stat[:, 24:28]
        s_top, s_neg, s_sum, s_inv = (stat[:, 28 + 4 * i:32 + 4 * i] for i in range(4))
        c_sigm = stat[:, 48:48 + 2 * KD]
        psum = ctx.enter_context(nc.psum_tensor("psum", [P, 8, 512], F32))

        ident = const[:, C_ID:C_ID + P]
        dft_c = const[:, C_DFTC:C_DFTC + 2 * FC]
        dft_t = const[:, C_DFTT:C_DFTT + 4 * SEQ].rearrange("p (t a n) -> p t a n", t=2, a=2)
        cos = const[:, C_COS:C_COS + NTOK]
        sin = const[:, C_SIN:C_SIN + NTOK]
        perm = const[:, C_PERM:C_PERM + P]
        sel = const[:, C_SEL:C_SEL + 2]
        one = const[:, C_ONE:C_ONE + 1]
        eps = const[:, C_EPS:C_EPS + 1]
        c_raw = small[:, S_C:S_C + 2 * KD].rearrange("p (k s) -> p k s", s=2)
        w_router = small[:, S_ROUTER:S_END].rearrange("p (k e) -> p k e", e=NE)

        q_t = reg_q[:, 0:4096].rearrange("p (b h n) -> p b h n", b=2, h=4)
        k_t = reg_q[:, 4096:8192].rearrange("p (b h n) -> p b h n", b=2, h=4)
        p_t = reg_q[:, 8192:12288].rearrange("p (b h k n) -> p b h k n", b=2, h=2, k=4)
        u_t = reg_q[:, 0:2048].rearrange("p (g n) -> p g n", g=FG)
        squares = reg_q[:, 8192:8192 + 3 * NTOK].rearrange("p (m n) -> p m n", m=3)
        rms = reg_q[:, 8192 + 3 * NTOK:8192 + 5 * NTOK].rearrange("p (m n) -> p m n", m=2)
        dft_1 = reg_q[:, 8192 + 5 * NTOK:8192 + 7 * NTOK].rearrange("p (b t n) -> p b t n", b=2, t=2)
        merged = reg_q[:, 0:4096].rearrange("p (k n) -> p k n", k=KD)
        sig_b = reg_q[:, 4096:4096 + 4 * NTOK].rearrange("p (m n) -> p m n", m=4)
        mrg_b = reg_q[:, 4096 + 4 * NTOK:4096 + 8 * NTOK].rearrange("p (m n) -> p m n", m=4)
        a_t = reg_q[:, 0:FT * NTOK].rearrange("p (f n) -> p f n", f=FT)
        v_sb = reg_v[:, :].rearrange("p (b k n) -> p b k n", b=2, k=4)
        ln_rows = reg_v[:, :].rearrange("p (a n) -> p a n", a=2)
        attn_t = reg_a[:, :].rearrange("p (k n) -> p k n", k=KD)
        z_sb = reg_a[:, 0:2048].rearrange("p (b n) -> p b n", b=2)
        xn = reg_a[:, 2048:4096].rearrange("p (b n) -> p b n", b=2)
        four_t = reg_f[:, :].rearrange("p (g n) -> p g n", g=FG)
        ff_b = reg_f[:, :].rearrange("p (m n) -> p m n", m=4)
        k_rope = reg_r[:, 0, :]
        q_rope = reg_r[:, 0, :]
        rope_a = reg_r[:, 1, :]
        rope_b = reg_r[:, 2, :]
        mod_pm = reg_p

        def over(name, shape, offset):
            return nc.alloc_sbuf_tensor_at(name, shape, F32R, offset=offset)

        w_lo = over("w_lo", [P, E_SLOTS, SLOT], at_ring)
        e_ring = nc.alloc_sbuf_tensor_at("e_ring", [P, E_SLOTS, SLOT], F32, offset=at_ring)
        h_hi = over("h_hi", [P, KD, NTOK], at_h)
        h_lo = over("h_lo", [P, KD, NTOK], at_a)
        a_hi = over("a_hi", [P, 2, 4, NTOK], at_h)
        a_lo = over("a_lo", [P, 2, 4, NTOK], at_a)
        m_hi = over("m_hi", [P, KD, NTOK], at_q + 4 * 8192)
        m_lo = over("m_lo", [P, KD, NTOK], at_q)
        y_hi = over("y_hi", [P, D], at_f)
        y_lo = over("y_lo", [P, D], at_f + 4 * D)
        sel_slot = over("sel_slot", [P, 2, P], at_lat)
        xg_hi = over("xg_hi", [P, KD, P], at_q + 4 * 4096)
        xg_lo = over("xg_lo", [P, KD, P], at_q + 4 * 5120)
        at_hi = over("at_hi", [P, 2, 4, P], at_q + 4 * 6144)
        at_lo = over("at_lo", [P, 2, 4, P], at_q + 4 * 7168)
        h_mod = lat_q
        z_of = [None, reg_q[:, 4096:6144].rearrange("p (b n) -> p b n", b=2),
                reg_f[:, :].rearrange("p (b n) -> p b n", b=2), z_sb, z_sb]
        xn_2 = nc.alloc_sbuf_tensor_at("xn_2", [P, 2, D], F32, offset=at_lat)
        xn_of = [xn, reg_q[:, 6144:8192].rearrange("p (b n) -> p b n", b=2), xn_2, xn]

        at = [0]

        def part(n):
            at[0] += n
            return reg_q[:, at[0] - n:at[0]]

        e_sig = part(1024).rearrange("p (b n) -> p b n", b=2)
        e_tmp = part(512)
        e_a = part(1024).rearrange("p (b n) -> p b n", b=2)
        xg_mod = part(D).rearrange("p (a n) -> p a n", a=2)
        assert at[0] <= 4096
        at[0] = 8192
        f_acc = part(2 * D).rearrange("p (t n) -> p t n", t=2)
        sel_tok = part(2 * P).rearrange("p (t n) -> p t n", t=2)
        route_c = part(R_END)
        iota = route_c[:, R_IOTA:R_IOTA + P]
        tri = route_c[:, R_TRI:R_TRI + P]
        e_num = route_c[:, R_E:R_E + NE]
        rt = part(1024)
        assert at[0] <= 12288
        rt_at = [0]

        def rpart(n):
            rt_at[0] += n
            return rt[:, rt_at[0] - n:rt_at[0]]

        b_rout = rpart(NE)
        logits = rpart(2 * NE).rearrange("p (t e) -> p t e", t=2)
        top = rpart(2 * 8).rearrange("p (t e) -> p t e", t=2)
        top_i = rpart(2 * 8).rearrange("p (t e) -> p t e", t=2)
        top_if = rpart(2 * 8).rearrange("p (t e) -> p t e", t=2)
        pair_w = rpart(2 * 4).rearrange("p (t e) -> p t e", t=2)
        hot = rpart(4 * NE).rearrange("p (t k e) -> p t k e", t=2, k=2)
        taken = rpart(2 * NE).rearrange("p (t e) -> p t e", t=2)
        comb = rpart(2 * NE).rearrange("p (t e) -> p t e", t=2)
        tmp8 = rpart(2 * NE).rearrange("p (t e) -> p t e", t=2)
        place = rpart(2 * NE).rearrange("p (t e) -> p t e", t=2)
        count = rpart(NE)
        full = rpart(NE)
        rank = rpart(NE)
        hit = rpart(NE)
        job_at = rpart(2 * (JOBS + 1)).rearrange("p (t j) -> p t j", t=2)
        job_w = rpart(2 * (JOBS + 1)).rearrange("p (t j) -> p t j", t=2)
        job_e = rpart(JOBS)
        job_ei = rpart(JOBS).bitcast(I32)
        n_jobs = rpart(1)
        n_jobs_i = rpart(1).bitcast(I32)

        landed = [sem(f"landed{i}") for i in range(E_SLOTS)]
        slot_free = sem("slot_free")
        hi_ok = sem("hi_ok")
        lo_dve, lo_pool = sem("lo_dve"), sem("lo_pool")
        w_used = sem("w_used")
        as_hi, as_lo = sem("as_hi"), sem("as_lo")
        consts_in = sem("consts_in")
        x_in = [sem(f"x_in{t}") for t in range(TT)]
        ln_in = [sem(f"ln_in{i}") for i in range(4)]
        route_in = sem("route_in")
        out_done = sem("out_done")
        c_sig = sem("c_sig")
        c_ready = sem("c_ready")
        mod_acc = sem("mod_acc")
        mod_copied = sem("mod_copied")
        mod_sum = sem("mod_sum")
        mod_done = sem("mod_done")
        dve_own = sem("dve_own")
        act_own = sem("act_own")
        pool_own = sem("pool_own")

        def layered(name):
            return [sem(f"{name}_{l}") for l in range(DEPTH)]

        var_ready, std_ready = sem("var_ready"), sem("std_ready")
        xn_ready = sem("xn_ready")
        xn_turned = [sem("xn_turned0"), sem("xn_turned1")]
        ht_act, ht_dve = sem("ht_act"), sem("ht_dve")
        z_scaled = sem("z_scaled")
        x_new = sem("x_new")
        in_mm, in_act, in_dve = layered("in_mm"), layered("in_act"), layered("in_dve")
        rms_mm, rms_act, lat_done = layered("rms_mm"), layered("rms_act"), layered("lat_done")
        kr_perm, kr_sum = layered("kr_perm"), layered("kr_sum")
        kr_done, kr_copied = layered("kr_done"), layered("kr_copied")
        f1_mm, f1_act, f2_mm, f2_dve = layered("f1_mm"), layered("f1_act"), layered("f2_mm"), layered("f2_dve")
        fill_mm, fill_act, fill_dve = layered("fill_mm"), layered("fill_act"), layered("fill_dve")
        rope_cos = layered("rope_cos")
        s_mm, s_max, s_exp, s_rec, s_nrm = (layered(n) for n in ("s_mm", "s_max", "s_exp", "s_rec", "s_nrm"))
        t_mm, t_out = layered("t_mm"), layered("t_out")
        pv_mm, pv_out = layered("pv_mm"), layered("pv_out")
        g_mm, g_sig, g_mul = layered("g_mm"), layered("g_sig"), layered("g_mul")
        m_done, mhi_ok, mlo_ok = layered("m_done"), layered("mhi_ok"), layered("mlo_ok")
        y_mm, y_used = layered("y_mm"), layered("y_used")
        fg_mm, fu_mm, fg_sig, fa_done = sem("fg_mm"), sem("fu_mm"), sem("fg_sig"), sem("fa_done")
        fd_mm, fd_used = sem("fd_mm"), sem("fd_used")
        r_mm, r_taken, route_ready = sem("r_mm"), sem("r_taken"), sem("route_ready")
        r_diff, r_exp = sem("r_diff"), sem("r_exp")
        sel_ready = sem("sel_ready")
        xg_mm, xg_act, xg_dve = sem("xg_mm"), sem("xg_act"), sem("xg_dve")
        gu_mm, e_sig_ok, a_ok = sem("gu_mm"), sem("e_sig_ok"), sem("a_ok")
        at_mm, at_ok, at_lo_ok = sem("at_mm"), sem("at_ok"), sem("at_lo_ok")
        st_mm, st_ok = sem("st_mm"), sem("st_ok")
        ye_mm, yhi_ok, y_dve = sem("ye_mm"), sem("yhi_ok"), sem("y_dve")
        sc_mm, sc_ok = sem("sc_mm"), sem("sc_ok")
        e_tmp_ok = sem("e_tmp_ok")
        xm_ok, xd_ok, ga_mm = sem("xm_ok"), sem("xd_ok"), sem("ga_mm")

        chunks = ring_chunks(w)
        n_static = len(chunks)
        index_of = {name: n for n, (name, _) in enumerate(chunks)}
        arrive = []
        per_slot = [0] * E_SLOTS
        for n, (_, dmas) in enumerate(chunks):
            per_slot[n % SLOTS] += 16 * len(dmas)
            arrive.append(per_slot[n % SLOTS])

        is_split = [name[0] in SPLIT for name, _ in chunks]
        splits_before = [sum(is_split[:n]) for n in range(n_static + 1)]
        n_split = splits_before[n_static]
        split_list = [n for n in range(n_static) if is_split[n]]

        q_ffn = splits_before[index_of[("fg", 0)]]
        q_end = splits_before[index_of[("in", 1, 0)]]

        def slot_view(n, c0, shape):
            size = int(np.prod(shape))
            v = ring[:, n % SLOTS, c0:c0 + size]
            return v.rearrange("p (k n) -> p k n", k=shape[0]) if len(shape) == 2 else v

        q0 = [0, CTX]
        t0 = [0, 2]
        nq = [NTOK, SEQ]
        plans = [merged_plan(l) for l in range(DEPTH)]

        ln_uses = [(0, 1, range(TT)), (0, 2, range(TT)), (1, 1, range(TT)), (1, 2, range(2, TT))]
        tiles_before = [0, 4, 8, 12, 14]
        norms_before = [None, 0, 4, 8, 10]
        stats_before = [0, 4, 12, 20, 24]

        def chain(tiles):
            tiles = list(tiles)
            steps = []
            for i, t in enumerate(tiles):
                steps.append(("A", t))
                if i:
                    steps.append(("B", tiles[i - 1]))
            return steps + [("B", tiles[-1])]

        def fd_buffer(dh, i):
            return (dh * len(DOWN) + i) % 2

        def act_fills(g, i):
            return 7 * g + sum(k != 4 for k in range(i + 1))

        def dve_fills(g, i):
            return 5 * g + sum(k in (1, 2, 3, 4, 5) for k in range(i + 1))

        mod_order = [(0, cb) for cb in range(6)] + [(0, cb) for jj in range(4) for cb in MERGE_MOD[jj]]
        mod_order += [(1, cb) for cb in range(6)] + [(1, cb) for jj in range(4) for cb in MERGE_MOD[jj]]
        mod_at = {b: n for n, b in enumerate(mod_order)}

        block = ctx.enter_context(nc.Block())

        @block.sync
        def _(sp):
            sp.dma_start(small[:, :], w["small"]).then_inc(consts_in, 16)
            sp.dma_start(const[:, :], w["const"]).then_inc(consts_in, 16)
            sp.dma_start(bmod[:, :], w["b_mod"].rearrange("l (c n) -> (l c) n", n=512)).then_inc(consts_in, 16)

            def load(n):
                last = n - SLOTS
                if last >= 0 and is_split[last]:
                    sp.wait_ge(w_used, splits_before[last] + 1)
                elif last >= 0:
                    sp.wait_ge(slot_free, last - splits_before[last] + 1)
                for c0, shape, src in chunks[n][1]:
                    sp.dma_start(slot_view(n, c0, shape), src).then_inc(landed[n % SLOTS], 16)

            def load_ln(i, g, b):
                for a, v in ((0, g), (1, b)):
                    sp.dma_start(ln_rows[:, a, :], v.partition_broadcast(P)).then_inc(ln_in[i], 16)

            for n in range(4):
                load(n)
            for t in range(TT):
                src = w["ctx"][0] if t < 2 else w["x"][0]
                sp.dma_start(x_res[:, t, :], src[(t % 2) * P:(t % 2 + 1) * P, :]).then_inc(x_in[t], 16)
            for n in range(4, n_static):
                for l in range(DEPTH):
                    if n == index_of[("out", l, 0, 0)]:
                        sp.wait_ge(pv_out[l], len(plans[l][2]))
                        load_ln(2 * l, w["ln1_g"][l], w["ln1_b"][l])
                if n == index_of[("fd", 0, 0)]:
                    sp.wait_ge(x_new, 4)
                    load_ln(1, w["ln2_g"][0], w["ln2_b"][0])
                load(n)

            def job(j, e):
                def chunk(c, src, shape):
                    sp.wait_ge(w_used, j * JOB_CHUNKS + (n_split + c - E_SLOTS + 1))
                    slot = c % E_SLOTS
                    view = e_ring[:, slot, :].rearrange("p (k n) -> p k n", k=shape[0])
                    sp.dma_start(view, src).then_inc(landed[slot], 16)

                gate = w["w_e_gate"].rearrange("a e (h k p) f -> (a e) h p k f", h=2, p=P)[bass.ds(e, 1)]
                up = w["w_e_up"].rearrange("a e (h k p) f -> (a e) h p k f", h=2, p=P)[bass.ds(e, 1)]
                down = w["w_e_down"].rearrange("a e (c h f p) n -> (a e) (c h) p f n", h=2, f=2, p=P)[bass.ds(e, 1)]
                c = 0
                for fc in range(NFC + 1):
                    if fc < NFC:
                        for v in (gate, up):
                            for h in range(2):
                                chunk(c, v[0, h, :, :, fc * 512:(fc + 1) * 512], (4, 512))
                                c += 1
                    if fc > 0:
                        for h in range(2):
                            chunk(c, down[0, 2 * (fc - 1) + h], (2, D))
                            c += 1

            sp.wait_ge(y_mm[1], 4)
            sp.dma_start(route_c, w["route"]).then_inc(route_in, 16)
            sp.dma_start(b_rout, w["b_router"][0].partition_broadcast(P)).then_inc(route_in, 16)
            sp.wait_ge(x_new, norms_before[4])
            load_ln(3, w["ln2_g"][1], w["ln2_b"][1])
            sp.wait_ge(slot_free, n_static - n_split)
            sp.wait_ge(w_used, n_split)
            sp.wait_ge(r_mm, 2)
            with sp.Fori(0, NE - 1) as j:
                job(j, j)
            sp.wait_ge(route_ready, 1)
            jobs = sp.value_load(n_jobs_i[0:1, 0:1], min_val=NE, max_val=JOBS)
            with sp.Fori(NE - 1, jobs) as j:
                job(j, sp.value_load(job_ei[0:1, bass.ds(j, 1)], min_val=0, max_val=NE - 1))
            for t in range(2):
                sp.wait_ge(x_new, norms_before[4] + t + 1)
                sp.dma_start(out[0, t * P:(t + 1) * P, :], x_res[:, 2 + t, :]).then_inc(out_done, 16)
            sp.wait_ge(out_done, 32)

        @block.tensor
        def _(pe):
            pending = []

            def mm(o, lhs, rhs, start, stop, sig=None, free=None, **kw):
                ins = pe.matmul(o, lhs, rhs, start=start, stop=stop, **kw)
                if free is not None:
                    pending.append(free)
                if sig is not None:
                    ins.then_inc(sig, 1)
                elif pending:
                    ins.then_inc(pending.pop(0), 1)
                return ins

            def mm3(o, lhs, rhs, start, stop, sig=None, free=None, **kw):
                mm(o, lhs[0], rhs[0], start, False, **kw)
                mm(o, lhs[0], rhs[1], False, False, **kw)
                mm(o, lhs[1], rhs[0], False, stop, sig=sig, free=free, **kw)

            def parts(q, slot, shape):
                size = int(np.prod(shape))
                return [v[:, i, 0:size].rearrange("p (k n) -> p k n", k=shape[0])
                        for v, i in ((w_hi, q % HIS), (w_lo, slot))]

            def split_chunk(name, shape):
                q = splits_before[index_of[name]]
                pe.wait_ge(lo_dve, q + 1)
                pe.wait_ge(lo_pool, q + 1)
                return parts(q, index_of[name] % SLOTS, shape)

            def arrived(name):
                n = index_of[name]
                pe.wait_ge(landed[n % SLOTS], arrive[n])
                return n

            def mod_block(b):
                l, cb = b
                n = mod_at[b]
                if n >= 1:
                    pe.wait_ge(mod_copied, n)
                for h in range(2):
                    v = slot_view(arrived(("mod", l, cb, h)), 0, (4, 512))
                    for k in range(4):
                        mm(psum[32 * k:32 * k + 32, 4, :], c_act[:, 4 * h + k, :], v[:, k, :],
                           start=(h == 0), stop=(h == 1 and k > 0), free=slot_free if k == 3 else None, skip_group_check=True)
                row = l * 12 + cb
                mm(psum[0:32, 4, :], ident[0:DEPTH * 12, row:row + 1].to_broadcast([DEPTH * 12, 32]),
                   bmod[:, :], start=False, stop=True, sig=mod_acc, skip_group_check=True)

            def mod_reduce(b):
                l, cb = b
                n = mod_at[b]
                pe.wait_ge(mod_copied, n + 1)
                if n >= 1:
                    pe.wait_ge(mod_done, n)
                pm = mod_pm[:, n % 2, :]
                if cb in (4, 5, 10, 11):
                    mm(psum[:, 5, :], sel[:, 0:1].to_broadcast([P, P]), pm, start=True, stop=True)
                    mm(psum[:, 6, :], sel[:, 1:2].to_broadcast([P, P]), pm, start=True, stop=True, sig=mod_sum)
                else:
                    for i in range(4):
                        mm(psum[:, 5, 2 * i:2 * i + 2], pm[:, i * P:(i + 1) * P], sel, start=True, stop=True,
                           sig=mod_sum if i == 3 else None)

            def turn_tiles(use):
                _, _, tiles = ln_uses[use]
                for i, t in enumerate(tiles):
                    n = tiles_before[use] + i
                    pe.wait_ge(xn_ready, n + 1)
                    for half in range(2):
                        if n >= 1:
                            reader = ht_act if half == 0 or (use == 1 and i >= 1) else ht_dve
                            pe.wait_ge(reader, n)
                        for k in range(4):
                            ins = pe.transpose(psum[:, 6 + half, k * P:(k + 1) * P],
                                               xn_of[use][:, t % 2, (4 * half + k) * P:(4 * half + k + 1) * P], ident)
                        ins.then_inc(xn_turned[half], 1)

            def input_projection(l):
                pe.wait_ge(ht_act, tiles_before[2 * l + 1])
                pe.wait_ge(ht_dve, tiles_before[2 * l + 1])
                groups = [(0, 0, 0, 0), (0, P, 0, 0), (1, 0, 0, 1), (1, P, 64, 1),
                          (2, 0, 0, 0), (2, P, 0, 0), (3, 0, 0, 0), (3, P, 0, 0)]
                for i, (ch, c0, part0, full) in enumerate(groups):
                    name = ("in", l, ch)
                    shape = (KD, 160 if ch == 1 else 256)
                    v = slot_view(arrived(name), 0, shape)
                    m = ROPE if part0 else P
                    a = 0 if full else q0[l]
                    if i >= 4:
                        if i - 4 < 3:
                            pe.wait_ge(in_act[l], i - 3)
                        else:
                            pe.wait_ge(in_dve[l], 1)
                    for k in range(KD):
                        last = k == KD - 1
                        mm(psum[part0:part0 + m, i % 4, a:NTOK], v[:, k, c0:c0 + m], h_t[:, k, a:NTOK],
                           start=(k == 0), stop=last, sig=in_mm[l] if last else None,
                           free=slot_free if last and i in (1, 3, 5, 7) else None)

            def latent_norms(l):
                a = q0[l]
                pe.wait_ge(in_act[l], 3)
                for k in range(2):
                    mm(psum[:, 4, a:NTOK], one.to_broadcast([P, P]), squares[:, k, a:NTOK], start=(k == 0),
                       stop=(k == 1), sig=rms_mm[l] if k == 1 else None)
                mm(psum[:, 5, :], one.to_broadcast([P, P]), squares[:, 2, :], start=True, stop=True, sig=rms_mm[l])
                pe.wait_ge(in_dve[l], 1)
                mm(psum[64:96, 6, :], perm[64:96, 64:96], k_rope[64:96, :], start=True, stop=True, sig=kr_perm[l])

            def fourier(l):
                units = [(g, s) for g in range(FG) for s in ((0, 1) if l == 0 else (1,))]

                def second(n):
                    g, s = units[n]
                    pe.wait_ge(f1_act[l], n + 1)
                    if n >= 2:
                        pe.wait_ge(f2_dve[l], n - 1)
                    i = 0
                    for t in range(2):
                        for a in range(2):
                            mm(psum[:, 2 + n % 2, 0:SEQ], dft_1[:, n % 2, t, a * FC:(a + 1) * FC], dft_t[:, t, a, :],
                               start=(i == 0), stop=(i == 3), sig=f2_mm[l] if i == 3 else None)
                            i += 1

                pe.wait_ge(in_dve[l], 5)
                for n, (g, s) in enumerate(units):
                    if n >= 2:
                        pe.wait_ge(f1_act[l], n - 1)
                    for t in range(2):
                        mm(psum[:, n % 2, t * 256:(t + 1) * 256],
                           u_t[:, g, s * SEQ + t * P:s * SEQ + (t + 1) * P], dft_c,
                           start=True, stop=True, sig=f1_mm[l] if t == 1 else None)
                    if n >= 1:
                        second(n - 1)
                second(len(units) - 1)

            def attention(l):
                plan, tiles, units = plans[l]
                a = q0[l]
                pe.wait_ge(lat_done[l], 1)
                pe.wait_ge(f2_dve[l], FG * (2 if l == 0 else 1))

                def fill(g, i):
                    n = 8 * g + i
                    v = arrived(("heads", l, g))
                    uq = slot_view(v, 0, (2, 4 * QK))
                    uk = slot_view(v, 768, (256,))
                    uv = slot_view(v, 1024, (256,))
                    b = i % 2
                    if n >= 2:
                        before = (g, i - 2) if i >= 2 else (g - 1, i + 6)
                        pe.wait_ge(fill_act[l], act_fills(*before))
                        if dve_fills(*before):
                            pe.wait_ge(fill_dve[l], dve_fills(*before))
                    if i == 0:
                        for k in range(2):
                            mm(psum[:, b, a:NTOK], uq[:, k, 0:4 * ROPE], lat_q[:, k, a:NTOK], start=(k == 0),
                               stop=(k == 1), sig=fill_mm[l] if k == 1 else None)
                    elif i in (1, 2):
                        c0 = 4 * ROPE + (i - 1) * P
                        for k in range(2):
                            mm(psum[:, b, a:NTOK], uq[:, k, c0:c0 + P], lat_q[:, k, a:NTOK],
                               start=(k == 0), stop=(k == 1), sig=fill_mm[l] if k == 1 else None)
                    elif i in (3, 5):
                        c0 = 0 if i == 3 else P
                        mm(psum[:, b, :], uk[:, c0:c0 + P], lat_kv[:, :], start=True, stop=True, sig=fill_mm[l])
                    elif i == 4:
                        pe.wait_ge(fill_act[l], act_fills(g, 0))
                        mm(psum[:, b, a:NTOK], perm, q_rope[:, a:NTOK], start=True, stop=True, sig=fill_mm[l])
                    else:
                        for kt in range(2):
                            t = 2 * (i - 6) + kt
                            mm(psum[:, b, kt * 256:(kt + 1) * 256], lat_kv[:, t * P:(t + 1) * P], uv,
                               start=True, stop=True, sig=fill_mm[l] if kt == 1 else None,
                               free=slot_free if i == 7 and kt == 1 else None)

                def score(c):
                    u, g, h, _, s, qt = tiles[c]
                    pe.wait_ge(fill_act[l], act_fills(g, 7))
                    pe.wait_ge(fill_dve[l], dve_fills(g, 7))
                    pe.wait_ge((kr_done, kr_copied)[g % 2][l], 1)
                    if c >= 2:
                        pe.wait_ge(s_exp[l], c - 1)
                    nk = CTX if s == 0 else NTOK
                    at_q = s * SEQ + qt * P
                    mm(psum[:, 2 + c % 2, 0:nk], q_t[0:QK, g % 2, h, at_q:at_q + P], k_t[0:QK, g % 2, h, 0:nk],
                       start=True, stop=True, sig=s_mm[l])

                def turn(c):
                    s = tiles[c][4]
                    pe.wait_ge(s_nrm[l], c + 1)
                    if c >= 2:
                        pe.wait_ge(t_out[l], c - 1)
                    nt = 2 if s == 0 else 4
                    for k in range(nt):
                        ins = pe.transpose(psum[:, 4 + c % 2, k * P:(k + 1) * P], reg_p[:, c % 3, k * P:(k + 1) * P],
                                           ident)
                    ins.then_inc(t_mm[l], 1)

                def pv(u):
                    g, pair, s = units[u]
                    pe.wait_ge(t_out[l], 4 * u + 4)
                    if u >= 2:
                        pe.wait_ge(pv_out[l], u - 1)
                    nt = 2 if s == 0 else 4
                    for k in range(nt):
                        for h in range(2):
                            c0 = (2 * pair + h) * VH
                            mm(psum[VH * h:VH * h + VH, 6 + u % 2, 0:SEQ], v_sb[:, g % 2, k, c0:c0 + VH],
                               p_t[:, u % 2, h, k, :], start=(k == 0), stop=(k == nt - 1),
                               sig=pv_mm[l] if k == nt - 1 and h == 1 else None, skip_group_check=True)

                for step in plan:
                    if step[0] == "fill":
                        fill(step[1], step[2])
                    elif step[0] == "score":
                        score(step[1])
                    elif step[0] == "turn":
                        turn(step[1])
                    elif step[0] == "pv":
                        pv(step[1])

            def merge(l):
                a = q0[l]
                units = plans[l][2]
                pe.wait_ge(pv_out[l], len(units))
                for jj in range(4):
                    fills = [(kind, i) for kind in ("ga", "gf", "ao", "fo") for i in range(2)]
                    for f, (kind, i) in enumerate(fills):
                        n = 8 * jj + f
                        if f >= 4:
                            pe.wait_ge(g_sig[l], 4 * jj + f - 3)
                        elif jj >= 1:
                            pe.wait_ge(g_mul[l], 4 * (jj - 1) + f + 1)
                        kn = FG if kind == "fo" else KD
                        v = slot_view(arrived((kind, l, jj)), 0, (kn, 256))
                        rhs = {"ga": h_t, "gf": h_t, "ao": attn_t, "fo": four_t}[kind]
                        for k in range(kn):
                            last = k == kn - 1
                            mm(psum[:, f % 4, a:NTOK], v[:, k, i * P:(i + 1) * P], rhs[:, k, a:NTOK],
                               start=(k == 0), stop=last, sig=g_mm[l] if last else None,
                                   free=slot_free if last and i == 1 else None)
                    for cb in MERGE_MOD[jj]:
                        mod_block((l, cb))
                        mod_reduce((l, cb))

            def output_projection(l):
                pe.wait_ge(mod_done, mod_at[(l, 9)] + 1)
                for dh in range(2):
                    for kk in range(2):
                        v = split_chunk(("out", l, dh, kk), (4, 512))
                        pe.wait_ge(mlo_ok[l], 2 * kk + 2)
                        if dh == 1:
                            pe.wait_ge(g_mul[l], 16)
                        for i, t in enumerate(range(t0[l], TT)):
                            cols = slice(t * P, (t + 1) * P)
                            for k in range(4):
                                last = kk == 1 and k == 3
                                kc = 4 * kk + k
                                mm3(psum[:, 4 - 4 * dh + i, :], (m_hi[:, kc, cols], m_lo[:, kc, cols]),
                                    [x[:, k, :] for x in v], start=(kk == 0 and k == 0), stop=last,
                                    sig=y_mm[l] if last else None, free=w_used if t == TT - 1 and k == 3 else None)

            def dense_mixer():
                pe.wait_ge(ht_act, tiles_before[2])
                pe.wait_ge(ht_dve, tiles_before[2])
                for fp in range(FT // 2):
                    for m, kind in enumerate(("fg", "fu")):
                        v = split_chunk((kind, fp), (KD, 256))
                        for i in range(2):
                            if fp >= 1:
                                pe.wait_ge(fa_done, 2 * fp - 1 + i)
                            for k in range(KD):
                                last = k == KD - 1
                                mm3(psum[:, 2 * m + i, :], [x[:, k, i * P:(i + 1) * P] for x in v],
                                    (h_hi[:, k, :], h_lo[:, k, :]), start=(k == 0), stop=last,
                                    sig=(fg_mm, fu_mm)[m] if last else None, free=w_used if last and i == 1 else None)
                        if m == 0 and 3 <= fp < 9:
                            mod_reduce((1, fp - 3))
                    if 2 <= fp < 8:
                        mod_block((1, fp - 2))
                for dh in range(2):
                    for i, (fg, n) in enumerate(DOWN):
                        v = split_chunk(("fd", dh, fg), (n, 512))
                        b = fd_buffer(dh, i)
                        order = [(f, t) for f in range(fg, fg + n) for t in range(TT)]
                        if i == len(DOWN) - 1:
                            order = [(f, t) for t in range(TT) for f in range(fg, fg + n)]
                        if i == 0 and dh == 0:
                            pe.wait_ge(mod_done, mod_at[(1, 5)] + 1)
                        for f, t in order:
                            pe.wait_ge(as_hi, dh * FT + f + 1)
                            pe.wait_ge(as_lo, dh * FT + f + 1)
                            cols = slice(t * P, (t + 1) * P)
                            mm3(psum[:, (4 if dh == 0 else 0) + t, :],
                                (a_hi[:, b, f - fg, cols], a_lo[:, b, f - fg, cols]), [x[:, f - fg, :] for x in v],
                                start=(f == 0), stop=(f == FT - 1), sig=fd_mm if f == FT - 1 else None,
                                free=w_used if (f, t) == order[-1] else None)

            def router():
                pe.wait_ge(ht_act, tiles_before[4])
                pe.wait_ge(ht_dve, tiles_before[4])
                for t in range(2):
                    for k in range(KD):
                        mm(psum[:, t, 0:NE], h_t[:, k, CTX + t * P:CTX + (t + 1) * P], w_router[:, k, :],
                           start=(k == 0), stop=(k == KD - 1), sig=r_mm if k == KD - 1 else None)
                pe.wait_ge(r_taken, 1)
                mm(psum[:, 2, 0:NE], tri, taken[:, 0, :], start=True, stop=True)
                mm(psum[:, 3, 0:NE], one.to_broadcast([P, P]), taken[:, 0, :], start=True, stop=False)
                mm(psum[:, 3, 0:NE], tri, taken[:, 1, :], start=False, stop=True)
                mm(psum[:, 4, 0:NE], one.to_broadcast([P, P]), taken[:, 0, :], start=True, stop=False)
                mm(psum[:, 4, 0:NE], one.to_broadcast([P, P]), taken[:, 1, :], start=False, stop=True, sig=r_mm)

            def gather():
                for half, b in ((0, 1), (1, 3)):
                    for k in range(4):
                        d0 = (4 * half + k) * P
                        for t in range(2):
                            mm(psum[:, b, k * P:(k + 1) * P], xn[:, t, d0:d0 + P], sel_tok[:, t, :],
                               start=(t == 0), stop=(t == 1), sig=xg_mm if k == 3 and t == 1 else None)

            def scatter():
                n = 0
                for t in range(2):
                    for dh in range(2):
                        for y in (y_hi, y_lo):
                            mm(psum[:, 4 + n, :], sel_slot[:, t, :], y[:, dh * 512:(dh + 1) * 512],
                               start=(y is y_hi), stop=(y is y_lo), sig=sc_mm if y is y_lo else None)
                        n += 1

            def experts():
                pe.wait_ge(route_ready, 1)
                jobs = pe.value_load(n_jobs_i[0:1, 0:1], min_val=NE, max_val=JOBS)
                pe.wait_ge(sel_ready, 1)
                gather()
                pe.wait_ge(st_ok, 1)
                for dh in range(2):
                    mm(psum[:, 6 + dh, :], f_acc[:, 0, 0:P], f_acc[:, 0, 0:512], start=True, stop=True,
                       sig=ye_mm if dh == 1 else None)
                with pe.Fori(0, jobs) as j:
                    c = [0]

                    def chunk_products(shape, products, done):
                        q = n_split + c[0]
                        hi, lo = parts(q, c[0] % E_SLOTS, shape)
                        c[0] += 1
                        pe.wait_ge(hi_ok, j * JOB_CHUNKS + (q + 1))
                        for o, x, at, start, _ in products:
                            mm(o, x[0], hi[at], start=start, stop=False, skip_group_check=True)
                            mm(o, x[1], hi[at], start=False, stop=False, skip_group_check=True)
                        pe.wait_ge(lo_dve, j * JOB_CHUNKS + (q + 1))
                        pe.wait_ge(lo_pool, j * JOB_CHUNKS + (q + 1))
                        for n, (o, x, at, _, stop) in enumerate(products):
                            last = n == len(products) - 1
                            mm(o, x[0], lo[at], start=False, stop=stop, sig=done if last else None,
                               free=w_used if last else None, skip_group_check=True)

                    def gate_or_up(fc, b, sig):
                        for h in range(2):
                            chunk_products((4, 512),
                                           [(psum[:, b + fc % 2, :], (xg_hi[:, 4 * h + k, :], xg_lo[:, 4 * h + k, :]),
                                             (slice(None), k), h == 0 and k == 0, h == 1 and k == 3)
                                            for k in range(4)], sig if h == 1 else None)

                    def turn_a(fc):
                        pe.wait_ge(a_ok, j * NFC + (fc + 1))
                        for i in range(4):
                            ins = pe.transpose(psum[:, 4, i * P:(i + 1) * P], e_a[:, fc % 2, i * P:(i + 1) * P], ident)
                        ins.then_inc(at_mm, 1)

                    def down(fc):
                        pe.wait_ge(at_ok, j * NFC + (fc + 1))
                        pe.wait_ge(at_lo_ok, j * NFC + (fc + 1))
                        for h in range(2):
                            products = []
                            for f in range(2):
                                for dh in range(2):
                                    products.append((psum[:, 6 + dh, :],
                                                     (at_hi[:, fc % 2, 2 * h + f, :], at_lo[:, fc % 2, 2 * h + f, :]),
                                                     (slice(None), f, slice(dh * 512, (dh + 1) * 512)),
                                                     fc == 0 and h == 0 and f == 0, fc == NFC - 1 and h == 1 and f == 1))
                            chunk_products((2, D), products, ye_mm if fc == NFC - 1 and h == 1 else None)

                    pe.wait_ge(xg_act, j + 1)
                    pe.wait_ge(xg_dve, j + 1)
                    for fc in range(NFC):
                        if fc >= 2:
                            pe.wait_ge(a_ok, j * NFC + (fc - 1))
                        gate_or_up(fc, 0, ga_mm)
                        if fc == 1:
                            pe.wait_ge(sc_ok, j * 4 + 4)
                        if fc >= 1:
                            turn_a(fc - 1)
                        gate_or_up(fc, 2, gu_mm)
                        if fc == 0:
                            pe.wait_ge(y_dve, j + 1)
                            pe.wait_ge(st_ok, j + 1)
                            scatter()
                        else:
                            down(fc - 1)
                        if fc == 2:
                            for t in range(2):
                                ins = pe.transpose(psum[:, 5, t * P:(t + 1) * P], sel_tok[:, t, :], ident)
                            ins.then_inc(st_mm, 1)
                    pe.wait_ge(sel_ready, j + 2)
                    turn_a(NFC - 1)
                    gather()
                    down(NFC - 1)
                    pe.wait_ge(st_ok, j + 2)
                    mm(psum[:, 5, 0:2], ident, ident[:, 0:2], start=True, stop=True)
                pe.wait_ge(y_dve, jobs + 1)
                scatter()

            pe.wait_ge(consts_in, 48)
            pe.wait_ge(c_ready, 1)
            mod_block((0, 0))
            for cb in range(1, 6):
                mod_reduce((0, cb - 1))
                mod_block((0, cb))
            mod_reduce((0, 5))
            pe.wait_ge(mod_done, 6)
            turn_tiles(0)
            for l in range(DEPTH):
                input_projection(l)
                latent_norms(l)
                fourier(l)
                attention(l)
                merge(l)
                output_projection(l)
                turn_tiles(2 * l + 1)
                if l == 0:
                    dense_mixer()
                    turn_tiles(2)
            router()
            experts()

        @block.scalar
        def _(act):
            own = [0]

            def link(ins):
                own[0] += 1
                ins.then_inc(act_own, 1)
                act.wait_ge(act_own, own[0])

            def mod_copy(b):
                n = mod_at[b]
                act.wait_ge(mod_acc, n + 1)
                if n >= 2:
                    act.wait_ge(mod_sum, n - 1)
                act.activation(mod_pm[:, n % 2, :], psum[:, 4, :], ACT.Copy).then_inc(mod_copied, 1)

            def std(n):
                act.wait_ge(var_ready, n + 1)
                act.activation(ln_std[:, n % 4:n % 4 + 1], ln_mv[:, n % 4, 1:2], ACT.Sqrt, bias=eps)\
                   .then_inc(std_ready, 1)

            def split_hi(q):
                n = split_list[q]
                act.wait_ge(landed[n % SLOTS], arrive[n])
                if q >= HIS:
                    act.wait_ge(w_used, q - HIS + 1)
                size = sum(int(np.prod(shape)) for _, shape, _ in chunks[n][1])
                act.activation(w_hi[:, q % HIS, 0:size], ring[:, n % SLOTS, 0:size], ACT.Copy).then_inc(hi_ok, 1)

            def modulate(l, which, t, n):
                act.wait_ge(xn_turned[0], n + 1)
                s, m = t // 2, 2 * (which - 1)
                if (l, which) == (0, 2):
                    act.wait_ge(xn_turned[1], n + 1)
                    if n > tiles_before[1]:
                        act.wait_ge(ht_dve, n)
                    for k in range(KD):
                        ins = act.activation(h_mod[:, k // 4, k % 4 * P:(k % 4 + 1) * P],
                                             psum[:, 6 + k // 4, k % 4 * P:(k % 4 + 1) * P],
                                             ACT.Identity, bias=modcol[:, l, m, k, s:s + 1],
                                             scale=modcol[:, l, m + 1, k, s:s + 1])
                    link(ins)
                    act.activation(h_hi[:, :, t * P:(t + 1) * P],
                                   h_mod[:, :, :].rearrange("p a (k n) -> p (a k) n", k=4), ACT.Copy)\
                       .then_inc(ht_act, 1)
                    return
                for k in range(4):
                    ins = act.activation(h_t[:, k, t * P:(t + 1) * P], psum[:, 6, k * P:(k + 1) * P], ACT.Identity,
                                         bias=modcol[:, l, m, k, s:s + 1], scale=modcol[:, l, m + 1, k, s:s + 1])
                ins.then_inc(ht_act, 1)

            def norm_chain(use):
                l, which, tiles = ln_uses[use]
                n = stats_before[use]
                for step, t in chain(tiles):
                    std(n)
                    n += 1
                    if step == "B":
                        modulate(l, which, t, tiles_before[use] + t - tiles[0])

            act.wait_ge(consts_in, 48)
            act.activation(c_sigm, small[:, S_C:S_C + 2 * KD], ACT.Sigmoid).then_inc(c_sig, 1)
            std(0)
            std(1)
            for cb in range(6):
                mod_copy((0, cb))
            act.wait_ge(mod_done, 6)
            for t in range(2, TT):
                std(t)
                modulate(0, 1, t - 2, t - 2)
            modulate(0, 1, 2, 2)
            modulate(0, 1, 3, 3)

            for l in range(DEPTH):
                a = q0[l]
                for i in range(3):
                    act.wait_ge(in_mm[l], i + 1)
                    if i < 2:
                        dst, gcol, c0 = lat_q[:, i, a:NTOK], S_GQ + 2 * l + i, a
                    else:
                        dst, gcol, c0 = lat_kv[:, :], S_GKV + l, 0
                    act.activation(dst, psum[:, i, c0:NTOK], ACT.Copy, scale=small[:, gcol:gcol + 1])
                    act.activation(squares[:, i, c0:NTOK], psum[:, i, c0:NTOK], ACT.Square).then_inc(in_act[l], 1)
                for i, (c0, n) in enumerate(((a, Q_LORA), (0, KV_LORA))):
                    act.wait_ge(rms_mm[l], i + 1)
                    act.activation(rms[:, i, c0:NTOK], psum[:, 4 + i, c0:NTOK], ACT.Sqrt, bias=eps, scale=1.0 / n)\
                       .then_inc(rms_act[l], 1)
                units = FG * (2 if l == 0 else 1)
                for n in range(units):
                    act.wait_ge(f1_mm[l], n + 1)
                    if n >= 2:
                        act.wait_ge(f2_mm[l], n - 1)
                    act.activation(dft_1[:, n % 2, :, :], psum[:, n % 2, :], ACT.Copy).then_inc(f1_act[l], 1)

                plan, tiles, att = plans[l]

                def fill(g, i):
                    n = 8 * g + i
                    if i == 4:
                        return
                    act.wait_ge(fill_mm[l], n + 1)
                    b = i % 2
                    if g >= 2 and i in (1, 6):
                        act.wait_ge(pv_mm[l], len(att) // 4 * (g - 1))
                    if i == 0:
                        if g >= 1:
                            act.wait_ge(fill_dve[l], dve_fills(g - 1, 4))
                        else:
                            act.wait_ge(kr_done[l], 1)
                            act.wait_ge(kr_copied[l], 1)
                        act.activation(q_rope[:, a:NTOK], psum[:, b, a:NTOK], ACT.Copy).then_inc(fill_act[l], 1)
                    elif i in (1, 2):
                        h = 2 * (i - 1)
                        act.activation(q_t[0:NOPE, g % 2, h, a:NTOK], psum[0:NOPE, b, a:NTOK], ACT.Copy)\
                           .then_inc(fill_act[l], 1)
                    elif i in (3, 5):
                        h = 0 if i == 3 else 2
                        act.activation(k_t[0:NOPE, g % 2, h, :], psum[0:NOPE, b, :], ACT.Copy).then_inc(fill_act[l], 1)
                    else:
                        act.activation(v_sb[:, g % 2, 2 * (i - 6):2 * (i - 5), :], psum[:, b, :], ACT.Copy)\
                           .then_inc(fill_act[l], 1)

                def exp(c):
                    s = tiles[c][4]
                    nk = CTX if s == 0 else NTOK
                    act.wait_ge(s_max[l], c + 1)
                    if c >= 3:
                        act.wait_ge(t_mm[l], c - 2)
                    act.activation(reg_p[:, c % 3, 0:nk], psum[:, 2 + c % 2, 0:nk], ACT.Exp,
                                   bias=s_neg[:, c % 4:c % 4 + 1], scale=SM_SCALE,
                                   accum_out=s_sum[:, c % 4:c % 4 + 1]).then_inc(s_exp[l], 1)

                def turned(c):
                    u, g, _, h, s, qt = tiles[c]
                    nt = 2 if s == 0 else 4
                    act.wait_ge(t_mm[l], c + 1)
                    if u >= 2:
                        act.wait_ge(pv_mm[l], u - 1)
                    act.activation(p_t[:, u % 2, h, 0:nt, qt * P:(qt + 1) * P],
                                   psum[:, 4 + c % 2, 0:nt * P].rearrange("p (k n) -> p k n", k=nt), ACT.Copy)\
                       .then_inc(t_out[l], 1)

                for step in plan:
                    if step[0] == "fill":
                        fill(step[1], step[2])
                    elif step[0] == "score":
                        exp(step[1])
                    elif step[0] == "turn":
                        turned(step[1])

                def merged_hi(jj):
                    act.wait_ge(m_done[l], 2 * jj + 2)
                    act.activation(m_hi[:, 2 * jj:2 * jj + 2, a:NTOK], merged[:, 2 * jj:2 * jj + 2, a:NTOK], ACT.Copy)\
                       .then_inc(mhi_ok[l], 1)

                q_out = splits_before[index_of[("out", l, 0, 0)]]
                for jj in range(4):
                    for i in range(4):
                        act.wait_ge(g_mm[l], 8 * jj + i + 1)
                        if jj >= 1:
                            act.wait_ge(g_mul[l], 4 * (jj - 1) + i + 1)
                        act.activation(sig_b[:, i, a:NTOK], psum[:, i, a:NTOK], ACT.Sigmoid).then_inc(g_sig[l], 1)
                    if jj == 3:
                        split_hi(q_out)
                    for cb in MERGE_MOD[jj]:
                        mod_copy((l, cb))
                    if jj >= 1:
                        merged_hi(jj - 1)
                split_hi(q_out + 1)
                merged_hi(3)
                split_hi(q_out + 2)
                split_hi(q_out + 3)
                if l == 0:
                    split_hi(q_ffn)
                    split_hi(q_ffn + 1)
                norm_chain(2 * l + 1)

                if l == 0:
                    split_hi(q_ffn + 2)
                    for fp in range(FT // 2):
                        for f in (2 * fp, 2 * fp + 1):
                            act.wait_ge(fg_mm, f + 1)
                            if f >= 2:
                                act.wait_ge(fa_done, f - 1)
                            act.activation(ff_b[:, f % 2, :], psum[:, f % 2, :], ACT.Sigmoid).then_inc(fg_sig, 1)
                        if 2 <= fp < 8:
                            mod_copy((1, fp - 2))
                        split_hi(q_ffn + 2 * fp + 3)
                        if 2 * fp + 4 < FT + HIS - 1:
                            split_hi(q_ffn + 2 * fp + 4)
                    q = q_ffn + FT
                    for dh in range(2):
                        for i, (fg, n) in enumerate(DOWN):
                            if dh or i:
                                act.wait_ge(w_used, q - 1)
                            else:
                                act.wait_ge(fu_mm, FT)
                            for f in range(fg, fg + n):
                                act.wait_ge(fa_done, f + 1)
                                act.activation(a_hi[:, fd_buffer(dh, i), f - fg, :], a_t[:, f, :], ACT.Copy)\
                                   .then_inc(as_hi, 1)
                            if q + 2 < q_end:
                                split_hi(q + 2)
                            q += 1
                    norm_chain(2)

            act.wait_ge(r_diff, 1)
            act.activation(pair_w[:, :, 1], pair_w[:, :, 0], ACT.Exp).then_inc(r_exp, 1)
            act.wait_ge(route_ready, 1)
            jobs = act.value_load(n_jobs_i[0:1, 0:1], min_val=NE, max_val=JOBS)

            def gathered(j):
                act.wait_ge(xg_mm, j * 2 + 2)
                for k in range(4):
                    ins = act.activation(xg_mod[:, 0, k * P:(k + 1) * P], psum[:, 1, k * P:(k + 1) * P], ACT.Identity,
                                         bias=modcol[:, 1, 2, k, 1:2], scale=modcol[:, 1, 3, k, 1:2])
                ins.then_inc(xm_ok, 1)
                act.wait_ge(xm_ok, j + 1)
                act.activation(xg_hi[:, 0:4, :].rearrange("p k n -> p (k n)"), xg_mod[:, 0, :], ACT.Copy)\
                   .then_inc(xg_act, 1)

            def outputs_hi(j):
                act.wait_ge(ye_mm, j + 1)
                act.activation(y_hi[:, :], psum[:, 6:8, :].rearrange("p b n -> p (b n)"), ACT.Copy).then_inc(yhi_ok, 1)

            gathered(0)
            with act.Fori(0, jobs) as j:
                def split_hi_of(c):
                    slot = c % E_SLOTS
                    q = n_split + c
                    act.wait_ge(landed[slot], j * (16 * SLOT_TURNS) + (per_slot[slot] + 16 * (c // E_SLOTS + 1)))
                    act.wait_ge(w_used, j * JOB_CHUNKS + (q - HIS + 1))
                    act.activation(w_hi[:, q % HIS, :], e_ring[:, slot, :], ACT.Copy).then_inc(hi_ok, 1)

                def turned_a(fc):
                    act.wait_ge(at_mm, j * NFC + (fc + 1))
                    act.activation(at_hi[:, fc % 2, :, :].rearrange("p f n -> p (f n)"), psum[:, 4, :], ACT.Copy)\
                       .then_inc(at_ok, 1)

                split_hi_of(0)
                split_hi_of(1)
                outputs_hi(j)
                c = 2
                for fc in range(NFC):
                    split_hi_of(c)
                    split_hi_of(c + 1)
                    c += 2
                    if fc >= 1:
                        turned_a(fc - 1)
                    act.wait_ge(ga_mm, j * NFC + (fc + 1))
                    if fc >= 2:
                        act.wait_ge(a_ok, j * NFC + (fc - 1))
                    act.activation(e_sig[:, fc % 2, :], psum[:, fc % 2, :], ACT.Sigmoid).then_inc(e_sig_ok, 1)
                    for _ in range(2 * (fc > 0) + 2):
                        split_hi_of(c)
                        c += 1
                turned_a(NFC - 1)
                gathered(j + 1)
            outputs_hi(jobs)
            for t in range(2):
                std(stats_before[4] + t)

        @block.vector
        def _(dve):
            own = [0]

            def link(ins):
                own[0] += 1
                ins.then_inc(dve_own, 1)
                dve.wait_ge(dve_own, own[0])

            def mod_take(b):
                l, cb = b
                n = mod_at[b]
                dve.wait_ge(mod_sum, n + 1)
                if cb in (4, 5, 10, 11):
                    gate = gate1 if cb < 6 else gate2
                    c0 = (cb % 2) * 512
                    dve.tensor_copy(gate[:, 0, c0:c0 + 512], psum[:, 5, :])
                    dve.tensor_copy(gate[:, 1, c0:c0 + 512], psum[:, 6, :]).then_inc(mod_done, 1)
                else:
                    m = {0: 0, 2: 1, 6: 2, 8: 3}[cb - cb % 2]
                    dst = modcol[:, l, m, 4 * (cb % 2):4 * (cb % 2) + 4, :]
                    src = psum[:, 5, 0:8].rearrange("p (k s) -> p k s", s=2)
                    dve.tensor_scalar(dst, src, float(m % 2), None, ALU.add).then_inc(mod_done, 1)

            def normalise(n, src, dst, sig):
                dve.bn_stats(bn[:, 0, :], src[:, 0:512])
                link(dve.bn_stats(bn[:, 1, :], src[:, 512:1024]))
                dve.bn_aggr(ln_mv[:, n % 4, :], bn).then_inc(var_ready, 1)
                dve.wait_ge(std_ready, n + 1)
                link(dve.reciprocal(ln_rstd[:, n % 4:n % 4 + 1], ln_std[:, n % 4:n % 4 + 1]))
                dve.tensor_scalar(dst, src, ln_mv[:, n % 4, 0:1], ln_rstd[:, n % 4:n % 4 + 1],
                                  ALU.subtract, ALU.mult).then_inc(sig, 1)

            def low(dst, src, hi):
                return dve.tensor_tensor(dst, src, hi.bitcast(F32), ALU.subtract)

            def split_lo(q):
                n = split_list[q]
                dve.wait_ge(hi_ok, q + 1)
                size = sum(int(np.prod(shape)) for _, shape, _ in chunks[n][1])
                m = size * 3 // 4
                low(w_lo[:, n % SLOTS, 0:m], ring[:, n % SLOTS, 0:m], w_hi[:, q % HIS, 0:m]).then_inc(lo_dve, 1)

            def modulate(l, which, t, n):
                dve.wait_ge(xn_turned[1], n + 1)
                s, m = t // 2, 2 * (which - 1)
                if (l, which) == (0, 2):
                    cols = slice(t * P, (t + 1) * P)
                    dve.wait_ge(ht_act, n + 1)
                    low(h_lo[:, :, cols], h_mod[:, :, :].rearrange("p a (k n) -> p (a k) n", k=4), h_hi[:, :, cols])\
                        .then_inc(ht_dve, 1)
                    return
                for k in range(4):
                    ins = dve.tensor_scalar(h_t[:, 4 + k, t * P:(t + 1) * P], psum[:, 7, k * P:(k + 1) * P],
                                            modcol[:, l, m + 1, 4 + k, s:s + 1], modcol[:, l, m, 4 + k, s:s + 1],
                                            ALU.mult, ALU.add)
                ins.then_inc(ht_dve, 1)

            def norm_b(use, t, n):
                _, _, tiles = ln_uses[use]
                at_b = tiles_before[use] + t - tiles[0]
                if use:
                    dve.wait_ge(x_new, norms_before[use] + t - tiles[0] + 1)
                if at_b >= 2:
                    dve.wait_ge(xn_turned[1], at_b - 1)
                normalise(n, x_res[:, t, :], xn_of[use][:, t % 2, :], xn_ready)

            def residual(t, dh, y, gate):
                cols = slice(dh * 512, (dh + 1) * 512)
                link(dve.tensor_tensor(reg_r[:, dh, :], y, gate[:, t // 2, cols], ALU.mult))
                link(dve.scalar_tensor_tensor(out=x_res[:, t, cols], in0=x_res[:, t, cols], scalar=ALPHA,
                                              in1=reg_r[:, dh, :], op0=ALU.mult, op1=ALU.add))

            def norm_chain(use, add):
                l, which, tiles = ln_uses[use]
                n = stats_before[use]
                a = norms_before[use]
                turned = []
                for step, t in chain(tiles):
                    if step == "A":
                        add(t)
                        if t - tiles[0] >= 2:
                            dve.wait_ge(x_new, a + t - tiles[0] - 1)
                        normalise(n, x_res[:, t, :], z_of[use][:, t % 2, :], z_scaled)
                    else:
                        norm_b(use, t, n)
                        if t > tiles[0]:
                            modulate(l, which, t - 1, tiles_before[use] + t - 1 - tiles[0])
                    n += 1
                modulate(l, which, tiles[-1], tiles_before[use] + len(tiles) - 1)

            link(dve.memset(c_act[:, :, :], 0.0))
            dve.wait_ge(c_sig, 1)
            dve.tensor_tensor(c_act[:, :, 0:2], c_raw, c_sigm.rearrange("p (k s) -> p k s", s=2), ALU.mult)\
               .then_inc(c_ready, 1)
            for t in range(2):
                dve.wait_ge(x_in[t], 16)
                norm_b(0, t, t)
            for cb in range(6):
                mod_take((0, cb))
            for t in range(2, TT):
                dve.wait_ge(x_in[t], 16)
                norm_b(0, t, t)
                modulate(0, 1, t - 2, t - 2)
            modulate(0, 1, 2, 2)
            modulate(0, 1, 3, 3)

            for l in range(DEPTH):
                a = q0[l]
                dve.wait_ge(in_mm[l], 4)
                dve.tensor_copy(k_rope[64:96, :], psum[64:96, 3, :]).then_inc(in_dve[l], 1)
                for i in range(4):
                    dve.wait_ge(in_mm[l], 5 + i)
                    dve.tensor_copy(u_t[:, i, a:NTOK], psum[:, i, a:NTOK]).then_inc(in_dve[l], 1)
                dve.wait_ge(rms_act[l], 2)
                dve.reciprocal(rms[:, 0, a:NTOK], rms[:, 0, a:NTOK])
                link(dve.reciprocal(rms[:, 1, :], rms[:, 1, :]))
                for k in range(2):
                    dve.tensor_tensor(lat_q[:, k, a:NTOK], lat_q[:, k, a:NTOK], rms[:, 0, a:NTOK], ALU.mult)
                dve.tensor_tensor(lat_kv[:, :], lat_kv[:, :], rms[:, 1, :], ALU.mult).then_inc(lat_done[l], 1)
                dve.wait_ge(kr_perm[l], 1)
                dve.tensor_tensor(rope_a[64:96, :], k_rope[64:96, :], cos[64:96, :], ALU.mult)
                link(dve.tensor_tensor(rope_b[64:96, :], psum[64:96, 6, :], sin[64:96, :], ALU.mult))
                dve.tensor_tensor(k_rope[64:96, :], rope_a[64:96, :], rope_b[64:96, :], ALU.add).then_inc(kr_sum[l], 1)
                dve.wait_ge(kr_sum[l], 1)
                for h in range(4):
                    ins = dve.tensor_copy(k_t[64:96, 0, h, :], k_rope[64:96, :])
                ins.then_inc(kr_done[l], 1)
                units = [(g, s) for g in range(FG) for s in ((0, 1) if l == 0 else (1,))]
                for n, (g, s) in enumerate(units):
                    dve.wait_ge(f2_mm[l], n + 1)
                    dve.tensor_copy(four_t[:, g, s * SEQ:(s + 1) * SEQ], psum[:, 2 + n % 2, 0:SEQ])\
                       .then_inc(f2_dve[l], 1)

                plan, tiles, att = plans[l]

                def fill(g, i):
                    if i not in (1, 2, 3, 4, 5):
                        return
                    dve.wait_ge(fill_mm[l], 8 * g + i + 1)
                    b = i % 2
                    if g >= 2 and i == 1:
                        dve.wait_ge(pv_mm[l], len(att) // 4 * (g - 1))
                    if i in (1, 2):
                        dve.tensor_copy(q_t[0:NOPE, g % 2, 2 * (i - 1) + 1, a:NTOK], psum[64:128, b, a:NTOK])\
                           .then_inc(fill_dve[l], 1)
                    elif i in (3, 5):
                        dve.tensor_copy(k_t[0:NOPE, g % 2, 1 if i == 3 else 3, :], psum[64:128, b, :])\
                           .then_inc(fill_dve[l], 1)
                    else:
                        link(dve.tensor_tensor(rope_b[:, a:NTOK], psum[:, b, a:NTOK], sin[:, a:NTOK], ALU.mult))
                        dve.wait_ge(rope_cos[l], g + 1)
                        for h in range(4):
                            rows = slice(32 * h, 32 * h + 32)
                            ins = dve.tensor_tensor(q_t[64:96, g % 2, h, a:NTOK], rope_a[rows, a:NTOK],
                                                    rope_b[rows, a:NTOK], ALU.add)
                        ins.then_inc(fill_dve[l], 1)

                def top_score(c):
                    nk = CTX if tiles[c][4] == 0 else NTOK
                    dve.wait_ge(s_mm[l], c + 1)
                    link(dve.reduce_max(s_top[:, c % 4:c % 4 + 1], psum[:, 2 + c % 2, 0:nk], AX.X))
                    dve.tensor_scalar(s_neg[:, c % 4:c % 4 + 1], s_top[:, c % 4:c % 4 + 1], -SM_SCALE, None,
                                      ALU.mult).then_inc(s_max[l], 1)

                def inverse(c):
                    dve.wait_ge(s_exp[l], c + 1)
                    dve.reciprocal(s_inv[:, c % 4:c % 4 + 1], s_sum[:, c % 4:c % 4 + 1]).then_inc(s_rec[l], 1)

                def values(u):
                    g, pair, s = att[u]
                    dve.wait_ge(pv_mm[l], u + 1)
                    dve.tensor_copy(attn_t[:, 2 * g + pair, s * SEQ:(s + 1) * SEQ], psum[:, 6 + u % 2, 0:SEQ])\
                       .then_inc(pv_out[l], 1)

                for step in plan:
                    if step[0] == "fill":
                        fill(step[1], step[2])
                    elif step[0] == "score":
                        top_score(step[1])
                    elif step[0] == "norm":
                        inverse(step[1])
                    elif step[0] == "take":
                        values(step[1])

                def merged_lo(jj):
                    dve.wait_ge(mhi_ok[l], jj + 1)
                    low(m_lo[:, 2 * jj:2 * jj + 2, a:NTOK], merged[:, 2 * jj:2 * jj + 2, a:NTOK],
                        m_hi[:, 2 * jj:2 * jj + 2, a:NTOK]).then_inc(mlo_ok[l], 1)

                q_out = splits_before[index_of[("out", l, 0, 0)]]
                for jj in range(4):
                    if jj >= 1:
                        dve.wait_ge(m_done[l], 2 * jj)
                    for i in range(4):
                        dve.wait_ge(g_mm[l], 8 * jj + 4 + i + 1)
                        dve.wait_ge(g_sig[l], 4 * jj + i + 1)
                        dve.tensor_tensor(mrg_b[:, i, a:NTOK], psum[:, i, a:NTOK], sig_b[:, i, a:NTOK], ALU.mult)\
                           .then_inc(g_mul[l], 1)
                    if jj == 3:
                        split_lo(q_out)
                    for cb in MERGE_MOD[jj]:
                        mod_take((l, cb))
                    if jj >= 1:
                        merged_lo(jj - 1)
                split_lo(q_out + 1)
                merged_lo(3)
                split_lo(q_out + 2)
                split_lo(q_out + 3)
                if l == 0:
                    split_lo(q_ffn)
                    split_lo(q_ffn + 1)
                for t in range(t0[l], TT):
                    dve.wait_ge(y_mm[l], t - t0[l] + 1)
                    residual(t, 0, psum[:, 4 + t - t0[l], :], gate1)

                def add_mixer(t):
                    dve.wait_ge(y_mm[l], TT - t0[l] + t - t0[l] + 1)
                    residual(t, 1, psum[:, t - t0[l], :], gate1)

                dve.wait_ge(ln_in[2 * l], 32)
                norm_chain(2 * l + 1, add_mixer)

                if l == 0:
                    split_lo(q_ffn + 2)
                    for fp in range(FT // 2):
                        if 3 <= fp < 9:
                            mod_take((1, fp - 3))
                        for f in (2 * fp, 2 * fp + 1):
                            dve.wait_ge(fg_sig, f + 1)
                            link(dve.tensor_tensor(ff_b[:, 2 + f % 2, :], ff_b[:, f % 2, :], psum[:, f % 2, :],
                                                   ALU.mult))
                            dve.wait_ge(fu_mm, f + 1)
                            dve.tensor_tensor(a_t[:, f, :], ff_b[:, 2 + f % 2, :], psum[:, 2 + f % 2, :], ALU.mult)\
                               .then_inc(fa_done, 1)
                        split_lo(q_ffn + 2 * fp + 3)
                        if 2 * fp + 4 < FT + HIS - 1:
                            split_lo(q_ffn + 2 * fp + 4)
                    q = q_ffn + FT
                    for dh in range(2):
                        for i, (fg, n) in enumerate(DOWN):
                            b = fd_buffer(dh, i)
                            for f in range(fg, fg + n):
                                dve.wait_ge(as_hi, dh * FT + f + 1)
                                low(a_lo[:, b, f - fg, :], a_t[:, f, :], a_hi[:, b, f - fg, :]).then_inc(as_lo, 1)
                            if q + 2 < q_end:
                                split_lo(q + 2)
                            q += 1
                            if dh == 1 and i == 0:
                                for t in range(TT):
                                    dve.wait_ge(fd_mm, t + 1)
                                    residual(t, 0, psum[:, 4 + t, :], gate2)

                    def add_dense(t):
                        dve.wait_ge(fd_mm, TT + t + 1)
                        residual(t, 1, psum[:, t, :], gate2)

                    norm_chain(2, add_dense)

            dve.wait_ge(route_in, 32)
            dve.wait_ge(r_mm, 2)
            for t in range(2):
                link(dve.tensor_tensor(logits[:, t, :], psum[:, t, 0:NE], b_rout, ALU.add))
                link(dve.max(top[:, t, :], logits[:, t, :]))
                link(dve.max_index(top_i[:, t, :].bitcast(U32), top[:, t, :], logits[:, t, :]))
                link(dve.tensor_copy(top_if[:, t, :], top_i[:, t, :].bitcast(U32)))
            dve.tensor_tensor(pair_w[:, :, 0], top[:, :, 1], top[:, :, 0], ALU.subtract).then_inc(r_diff, 1)
            dve.wait_ge(r_exp, 1)
            link(dve.tensor_scalar(pair_w[:, :, 3], pair_w[:, :, 1], 1.0, None, ALU.add))
            link(dve.reciprocal(pair_w[:, :, 2], pair_w[:, :, 3]))
            link(dve.tensor_tensor(pair_w[:, :, 3], pair_w[:, :, 2], pair_w[:, :, 1], ALU.mult))
            for t in range(2):
                for k in range(2):
                    link(dve.tensor_scalar(hot[:, t, k, :], e_num, top_if[:, t, k:k + 1], None, ALU.is_equal))
                link(dve.tensor_scalar(tmp8[:, t, :], hot[:, t, 1, :], pair_w[:, t, 3:4], None, ALU.mult))
                link(dve.scalar_tensor_tensor(out=comb[:, t, :], in0=hot[:, t, 0, :], scalar=pair_w[:, t, 2:3],
                                              in1=tmp8[:, t, :], op0=ALU.mult, op1=ALU.add))
            dve.tensor_tensor(taken[:, :, :], hot[:, :, 0, :], hot[:, :, 1, :], ALU.add).then_inc(r_taken, 1)
            dve.memset(job_at, -1.0)
            dve.memset(job_w, 0.0)
            link(dve.memset(job_e, 0.0))
            dve.tensor_copy(job_e[:, 0:NE], e_num)
            link(dve.memset(f_acc, 0.0))
            dve.tensor_copy(sel_slot[:, :, :], f_acc[:, :, 0:P]).then_inc(st_ok, 1)
            link(dve.memset(rank, 0.0))
            dve.wait_ge(r_taken, 1)
            dve.wait_ge(r_mm, 3)
            for t in range(2):
                link(dve.scalar_tensor_tensor(out=place[:, t, :], in0=psum[:, 2 + t, 0:NE], scalar=1.0,
                                              in1=taken[:, t, :], op0=ALU.add, op1=ALU.mult))
            link(dve.tensor_scalar(place[:, :, :], place[:, :, :], -1.0, None, ALU.add))
            dve.tensor_copy(job_at[:, :, 0:NE], place[:, :, :])
            dve.tensor_copy(job_w[:, :, 1:NE + 1], comb[:, :, :])
            link(dve.tensor_scalar(full, psum[:, 4, 0:NE], float(P), None, ALU.is_gt))
            for e in range(1, NE):
                link(dve.tensor_tensor(rank[:, e:e + 1], rank[:, e - 1:e], full[:, e - 1:e], ALU.add))
            link(dve.tensor_tensor(n_jobs, rank[:, NE - 1:NE], full[:, NE - 1:NE], ALU.add))
            link(dve.tensor_scalar(n_jobs, n_jobs, float(NE), None, ALU.add))
            for r in range(3):
                link(dve.scalar_tensor_tensor(out=hit, in0=rank, scalar=float(r), in1=full, op0=ALU.is_equal,
                                              op1=ALU.mult))
                link(dve.tensor_tensor(tmp8[:, 0, :], hit, e_num, ALU.mult))
                link(dve.reduce_sum(job_e[:, NE + r:NE + r + 1], tmp8[:, 0, :], AX.X))
                for t in range(2):
                    link(dve.scalar_tensor_tensor(out=tmp8[:, 0, :], in0=place[:, t, :], scalar=-float(P), in1=hit,
                                                  op0=ALU.add, op1=ALU.mult))
                    link(dve.reduce_sum(job_at[:, t, NE + r:NE + r + 1], tmp8[:, 0, :], AX.X))
                    link(dve.tensor_tensor(tmp8[:, 1, :], comb[:, t, :], hit, ALU.mult))
                    link(dve.reduce_sum(job_w[:, t, NE + 1 + r:NE + 2 + r], tmp8[:, 1, :], AX.X))
            dve.tensor_copy(job_ei, job_e)
            dve.tensor_copy(n_jobs_i, n_jobs).then_inc(route_ready, 1)
            dve.wait_ge(route_ready, 1)
            jobs = dve.value_load(n_jobs_i[0:1, 0:1], min_val=NE, max_val=JOBS)

            def select(j):
                for t in range(2):
                    ins = dve.tensor_scalar(sel_tok[:, t, :], iota, job_at[:, t, bass.ds(j, 1)], None, ALU.is_equal)
                ins.then_inc(sel_ready, 1)

            def gathered(j):
                dve.wait_ge(xg_mm, j * 2 + 2)
                for k in range(4):
                    ins = dve.tensor_scalar(xg_mod[:, 1, k * P:(k + 1) * P], psum[:, 3, k * P:(k + 1) * P],
                                            modcol[:, 1, 3, 4 + k, 1:2], modcol[:, 1, 2, 4 + k, 1:2],
                                            ALU.mult, ALU.add)
                ins.then_inc(xd_ok, 1)
                dve.wait_ge(xd_ok, j * 2 + 1)
                hi = [xg_hi[:, 4 * i:4 * i + 4, :].rearrange("p k n -> p (k n)") for i in range(2)]
                lo = [xg_lo[:, 4 * i:4 * i + 4, :].rearrange("p k n -> p (k n)") for i in range(2)]
                dve.tensor_copy(hi[1], xg_mod[:, 1, :]).then_inc(xd_ok, 1)
                dve.wait_ge(xd_ok, j * 2 + 2)
                low(lo[1], xg_mod[:, 1, :], hi[1])
                dve.wait_ge(xg_act, j + 1)
                low(lo[0], xg_mod[:, 0, :], hi[0]).then_inc(xg_dve, 1)

            def weigh(j):
                n = 0
                for t in range(2):
                    for dh in range(2):
                        dve.wait_ge(sc_mm, j * 4 + (n + 1))
                        acc = f_acc[:, t, dh * 512:(dh + 1) * 512]
                        dve.scalar_tensor_tensor(out=acc, in0=psum[:, 4 + n, :], scalar=job_w[:, t, bass.ds(j, 1)],
                                                 in1=acc, op0=ALU.mult, op1=ALU.add).then_inc(sc_ok, 1)
                        n += 1

            def outputs_lo(j):
                dve.wait_ge(yhi_ok, j + 1)
                low(y_lo[:, :], psum[:, 6:8, :].rearrange("p b n -> p (b n)"), y_hi[:, :]).then_inc(y_dve, 1)

            select(0)
            gathered(0)
            with dve.Fori(0, jobs) as j:
                def split_lo_of(c):
                    q = n_split + c
                    slot = c % E_SLOTS
                    dve.wait_ge(hi_ok, j * JOB_CHUNKS + (q + 1))
                    low(w_lo[:, slot, 0:LO_DVE], e_ring[:, slot, 0:LO_DVE], w_hi[:, q % HIS, 0:LO_DVE]).then_inc(lo_dve, 1)

                def turned_a(fc):
                    dve.wait_ge(at_ok, j * NFC + (fc + 1))
                    low(at_lo[:, fc % 2, :, :].rearrange("p f n -> p (f n)"), psum[:, 4, :],
                        at_hi[:, fc % 2, :, :].rearrange("p f n -> p (f n)")).then_inc(at_lo_ok, 1)

                split_lo_of(0)
                split_lo_of(1)
                outputs_lo(j)
                c = 2
                for fc in range(NFC):
                    split_lo_of(c)
                    split_lo_of(c + 1)
                    c += 2
                    if fc >= 1:
                        turned_a(fc - 1)
                    dve.wait_ge(e_sig_ok, j * NFC + (fc + 1))
                    dve.tensor_tensor(e_tmp, e_sig[:, fc % 2, :], psum[:, fc % 2, :], ALU.mult).then_inc(e_tmp_ok, 1)
                    if fc >= 1:
                        split_lo_of(c)
                        split_lo_of(c + 1)
                        c += 2
                    dve.wait_ge(e_tmp_ok, j * NFC + (fc + 1))
                    dve.wait_ge(gu_mm, j * NFC + (fc + 1))
                    if fc >= 2:
                        dve.wait_ge(at_mm, j * NFC + (fc - 1))
                    dve.tensor_tensor(e_a[:, fc % 2, :], e_tmp, psum[:, 2 + fc % 2, :], ALU.mult).then_inc(a_ok, 1)
                    if fc == 0:
                        weigh(j)
                    if fc == 2:
                        dve.wait_ge(st_mm, j + 1)
                        dve.tensor_copy(sel_slot[:, :, :].rearrange("p t n -> p (t n)"), psum[:, 5, 0:2 * P]).then_inc(st_ok, 1)
                    if fc == 3:
                        select(j + 1)
                    split_lo_of(c)
                    split_lo_of(c + 1)
                    c += 2
                turned_a(NFC - 1)
                gathered(j + 1)
            outputs_lo(jobs)
            weigh(jobs)
            dve.wait_ge(sc_ok, jobs * 4 + 4)
            for t in range(2):
                for dh in range(2):
                    residual(2 + t, dh, f_acc[:, t, dh * 512:(dh + 1) * 512], gate2)
                if t == 0:
                    dve.wait_ge(ln_in[3], 32)
                normalise(stats_before[4] + t, x_res[:, 2 + t, :], z_sb[:, t, :], z_scaled)

        @block.gpsimd
        def _(pool):
            def split_lo(q):
                n = split_list[q]
                pool.wait_ge(hi_ok, q + 1)
                size = sum(int(np.prod(shape)) for _, shape, _ in chunks[n][1])
                a = size * 3 // 4
                pool.tensor_tensor(w_lo[:, n % SLOTS, a:size], ring[:, n % SLOTS, a:size],
                                   w_hi[:, q % HIS, a:size].bitcast(F32), ALU.subtract).then_inc(lo_pool, 1)

            def weights_of(use, t, i):
                n = norms_before[use] + i
                pool.wait_ge(z_scaled, n + 1)
                if i == 0:
                    pool.wait_ge(ln_in[use - 1], 32)
                pool.tensor_tensor(z_of[use][:, t % 2, :], z_of[use][:, t % 2, :], ln_rows[:, 0, :], ALU.mult)\
                    .then_inc(pool_own, 1)
                pool.wait_ge(pool_own, n + 1)
                pool.tensor_tensor(x_res[:, t, :], z_of[use][:, t % 2, :], ln_rows[:, 1, :], ALU.add).then_inc(x_new, 1)

            for l in range(DEPTH):
                a = q0[l]
                pool.wait_ge(kr_sum[l], 1)
                for h in range(4):
                    ins = pool.tensor_copy(k_t[64:96, 1, h, :], k_rope[64:96, :])
                ins.then_inc(kr_copied[l], 1)
                plan, tiles, att = plans[l]
                for step in plan:
                    if step[0] == "fill" and step[2] == 4:
                        g = step[1]
                        pool.wait_ge(fill_act[l], act_fills(g, 0))
                        if g >= 1:
                            pool.wait_ge(fill_dve[l], dve_fills(g - 1, 4))
                        pool.tensor_tensor(rope_a[:, a:NTOK], q_rope[:, a:NTOK], cos[:, a:NTOK], ALU.mult)\
                            .then_inc(rope_cos[l], 1)
                    elif step[0] == "norm":
                        c = step[1]
                        nk = CTX if tiles[c][4] == 0 else NTOK
                        pool.wait_ge(s_rec[l], c + 1)
                        pool.tensor_scalar(reg_p[:, c % 3, 0:nk], reg_p[:, c % 3, 0:nk], s_inv[:, c % 4:c % 4 + 1],
                                           1.0, ALU.mult, ALU.mult).then_inc(s_nrm[l], 1)
                for jj in range(4):
                    pool.wait_ge(g_mul[l], 4 * jj + 4)
                    for i in range(2):
                        pool.tensor_tensor(merged[:, 2 * jj + i, a:NTOK], mrg_b[:, i, a:NTOK], mrg_b[:, 2 + i, a:NTOK],
                                           ALU.add).then_inc(m_done[l], 1)
                q_out = splits_before[index_of[("out", l, 0, 0)]]
                for q in range(q_out, q_out + 4):
                    split_lo(q)
                if l == 0:
                    split_lo(q_ffn)
                    split_lo(q_ffn + 1)
                    for t in range(TT):
                        weights_of(1, t, t)
                    for q in range(q_ffn + 2, q_end):
                        split_lo(q)
                    for t in range(TT):
                        weights_of(2, t, t)
                else:
                    for i in range(2):
                        weights_of(3, 2 + i, i)
            pool.wait_ge(route_ready, 1)
            jobs = pool.value_load(n_jobs_i[0:1, 0:1], min_val=NE, max_val=JOBS)
            with pool.Fori(0, jobs) as j:
                for c in range(JOB_CHUNKS):
                    q = n_split + c
                    slot = c % E_SLOTS
                    pool.wait_ge(hi_ok, j * JOB_CHUNKS + (q + 1))
                    pool.tensor_tensor(w_lo[:, slot, LO_DVE:SLOT], e_ring[:, slot, LO_DVE:SLOT],
                                       w_hi[:, q % HIS, LO_DVE:SLOT].bitcast(F32), ALU.subtract).then_inc(lo_pool, 1)
            for t in range(2):
                weights_of(4, 2 + t, t)


def constants():
    c = np.zeros((P, C_END), np.float64)
    c[:, C_ID:C_ID + P] = np.eye(P)
    k = np.arange(FC)
    ang = 2 * np.pi * ((k[:, None] * k[None, :]) % FC) / FC
    c[:, C_DFTC:C_DFTC + FC] = np.cos(ang) / np.sqrt(FC)
    c[:, C_DFTC + FC:C_DFTC + 2 * FC] = np.sin(ang) / np.sqrt(FC)
    k = np.arange(SEQ)
    ang = 2 * np.pi * ((k[:, None] * k[None, :]) % SEQ) / SEQ
    both = np.stack([np.cos(ang), -np.sin(ang)], 1) / np.sqrt(SEQ)
    c[:, C_DFTT:C_DFTT + 4 * SEQ] = both.reshape(2, P, 2, SEQ).transpose(1, 0, 2, 3).reshape(P, -1)
    nf = ROPE // 4
    pos = np.stack([np.arange(SEQ) // 64, np.arange(SEQ) % 64]).astype(np.float32)
    inv = (1.0 / (np.float32(10000.0) ** (np.arange(nf, dtype=np.float32) / nf))).astype(np.float32)
    ang = (pos[:, None, :] * inv[None, :, None]).astype(np.float32).astype(np.float64)
    ang = np.tile(np.repeat(ang[:, None], 2, axis=1).reshape(ROPE, SEQ), (4, 1))
    c[:, C_COS:C_COS + CTX] = 1.0
    c[:, C_COS + CTX:C_COS + NTOK] = np.cos(ang)
    c[:, C_SIN + CTX:C_SIN + NTOK] = np.sin(ang)
    for m in range(P):
        first = m // nf % 2 == 0
        c[m + nf if first else m - nf, C_PERM + m] = -1.0 if first else 1.0
    for j in range(4):
        c[32 * j, C_SEL] = 1.0
        c[32 * j + 1, C_SEL + 1] = 1.0
    c[:, C_ONE] = 1.0
    c[:, C_EPS] = EPS
    r = np.zeros((P, R_END))
    r[:, R_IOTA:R_IOTA + P] = np.arange(P)[None]
    r[:, R_TRI:R_TRI + P] = np.triu(np.ones((P, P)), 1)
    r[:, R_E:R_E + NE] = np.arange(NE)[None]
    return c.astype(np.float32), r.astype(np.float32)


def small_inputs(c, c_ctx, g_q, g_kv, w_router):
    both = np.stack([c_ctx, c[0]], -1).reshape(KD, P, 2).transpose(1, 0, 2).reshape(P, -1)
    gq = g_q.reshape(DEPTH, 2, P).transpose(2, 0, 1).reshape(P, -1)
    gkv = g_kv.reshape(DEPTH, P).T
    router = w_router[0].reshape(KD, P, NE).transpose(1, 0, 2).reshape(P, -1)
    return np.ascontiguousarray(np.concatenate([both, gq, gkv, router], 1))


def query_weights(w_uq):
    v = w_uq.reshape(DEPTH, Q_LORA, 4, 4, QK)
    parts = [v[..., NOPE:].reshape(DEPTH, Q_LORA, 4, -1), v[..., :NOPE].reshape(DEPTH, Q_LORA, 4, -1)]
    return np.ascontiguousarray(np.concatenate(parts, -1).reshape(DEPTH, Q_LORA, -1))


_IN_DRAM = ["x", "ctx", "w_mod", "b_mod", "w_in", "w_uk", "w_uv", "w_ao", "w_fo", "w_out", "ln1_g", "ln1_b",
            "ln2_g", "ln2_b", "w_ff_gate", "w_ff_up", "w_ff_down", "b_router", "w_e_gate", "w_e_up", "w_e_down"]


def kernel(**inputs):
    import concourse.bacc as bacc
    from concourse.bass_utils import run_bass_kernel_spmd

    nc = bacc.Bacc("TRN2", target_bir_lowering=False, num_devices=1, dynamic_dma_scratch_size=1024)
    arrays = {n: np.ascontiguousarray(inputs[n]) for n in _IN_DRAM}
    arrays["const"], arrays["route"] = constants()
    arrays["small"] = small_inputs(*(np.asarray(inputs[n]) for n in ("c", "c_ctx", "g_q", "g_kv", "w_router")))
    arrays["w_uq"] = query_weights(np.asarray(inputs["w_uq"]))
    w = {n: nc.dram_tensor(f"in_{n}", a.shape, F32, kind="ExternalInput").ap() for n, a in arrays.items()}
    out = nc.dram_tensor("out_x", (1, SEQ, D), F32, kind="ExternalOutput").ap()
    build(nc, w, out)
    r = run_bass_kernel_spmd(nc, [{f"in_{n}": a for n, a in arrays.items()}], core_ids=[0])
    return r.results[0]["out_x"]
```

```python
from contextlib import ExitStack

import numpy as np

import concourse.bass as bass
from concourse import mybir

ALU = mybir.AluOpType
ACT = mybir.ActivationFunctionType
AX = mybir.AxisListType
F32 = mybir.dt.float32
F32R = mybir.dt.float32r
I32 = mybir.dt.int32
U32 = mybir.dt.uint32

P = 128
D = 1024
KD = D // P
SEQ = 256
CTX = 256
NTOK = SEQ + CTX
TT = NTOK // P
DEPTH = 2
HEADS = 16
NOPE = 64
ROPE = 32
QK = NOPE + ROPE
VH = 64
Q_LORA = 256
KV_LORA = 128
FG = 4
FC = 128
OFF_KV = Q_LORA
OFF_KR = OFF_KV + KV_LORA
OFF_F = OFF_KR + ROPE
OFF_G = OFF_F + FG * FC
D_FF = 2816
FT = D_FF // P
NE = 8
D_FE = 3584
SM_SCALE = float(QK) ** -0.5
ALPHA = float((2 * DEPTH) ** 0.25)
EPS = 1e-6

SLOTS = 4
SLOT = 2048
HIS = 3
SPLIT = ("ga", "gf", "ao", "fo", "out", "fg", "fu", "fd")
LO_DVE = SLOT * 3 // 4
NFC = D_FE // 512
JOB_CHUNKS = 6 * NFC
E_SLOTS = SLOTS + 2
assert JOB_CHUNKS % E_SLOTS == 0 and JOB_CHUNKS % HIS == 0
SLOT_TURNS = JOB_CHUNKS // E_SLOTS
MIN_ONE = NE - 3

C_ID = 0
C_DFTC = C_ID + P
C_DFTT = C_DFTC + 2 * FC
C_COS = C_DFTT + 4 * SEQ
C_SIN = C_COS + NTOK
C_PERM = C_SIN + NTOK
C_SEL = C_PERM + P
C_ONE = C_SEL + 2
C_EPS = C_ONE + 1
C_END = C_EPS + 1
S_C = 0
S_GQ = S_C + 2 * KD
S_GKV = S_GQ + 2 * DEPTH
S_ROUTER = S_GKV + DEPTH
S_BMOD = S_ROUTER + KD * NE
S_END = S_BMOD + DEPTH * 6 * KD
R_IOTA = 0
R_TRI = R_IOTA + P
R_E = R_TRI + P
R_END = R_E + NE


def ring_chunks(w):
    chunks = []

    def mod(l, cb):
        v = w["w_mod"][l].rearrange("(h k p) n -> h p k n", h=2, p=P)
        for h in range(2):
            chunks.append((("mod", l, cb, h), [(0, (4, 512), v[h, :, :, cb * 512:(cb + 1) * 512])]))

    def rows(name, v, k, c0, n):
        chunks.append((name, [(0, (k, n), v.rearrange("(k p) n -> p k n", p=P)[:, :, c0:c0 + n])]))

    for cb in range(6):
        mod(0, cb)
    for l in range(DEPTH):
        w_in = w["w_in"][l]
        rows(("in", l, 0), w_in, KD, 0, Q_LORA)
        rows(("in", l, 1), w_in, KD, OFF_KV, KV_LORA + ROPE)
        rows(("in", l, 2), w_in, KD, OFF_F, 2 * FC)
        rows(("in", l, 3), w_in, KD, OFF_F + 2 * FC, 2 * FC)
        for g in range(4):
            uq = w["w_uq"][l].rearrange("(k p) n -> p k n", p=P)[:, :, g * 4 * QK:(g + 1) * 4 * QK]
            uk = w["w_uk"][l][:, g * 4 * NOPE:(g + 1) * 4 * NOPE]
            uv = w["w_uv"][l][:, g * 4 * VH:(g + 1) * 4 * VH]
            chunks.append((("heads", l, g), [(0, (2, 4 * QK), uq), (2 * 4 * QK, (256,), uk),
                                             (2 * 4 * QK + 256, (256,), uv)]))
        for u, (kind, jj) in enumerate(MERGE):
            src, k, c0 = {"ga": (w_in, KD, OFF_G), "gf": (w_in, KD, OFF_G + D), "ao": (w["w_ao"][l], KD, 0),
                          "fo": (w["w_fo"][l], FG, 0)}[kind]
            rows((kind, l, jj), src, k, c0 + jj * 256, 256)
            if u in MERGE_MOD:
                mod(l, MERGE_MOD[u])
        v = w["w_out"][l].rearrange("(g k p) n -> g p k n", k=4, p=P)
        for dh in range(2):
            for kk in range(2):
                chunks.append((("out", l, dh, kk), [(0, (4, 512), v[kk, :, :, dh * 512:(dh + 1) * 512])]))
        if l == 0:
            for fp in range(FT // 2):
                rows(("fg", fp), w["w_ff_gate"][0], KD, fp * 256, 256)
                rows(("fu", fp), w["w_ff_up"][0], KD, fp * 256, 256)
                if 2 <= fp < 8:
                    mod(1, fp - 2)
            down = w["w_ff_down"][0].rearrange("(f p) n -> p f n", p=P)
            for dh in range(2):
                for fg, n in DOWN:
                    chunks.append((("fd", dh, fg), [(0, (n, 512), down[:, fg:fg + n, dh * 512:(dh + 1) * 512])]))
    return chunks


DOWN = [(0, FT % 4)] + [(f, 4) for f in range(FT % 4, FT, 4)]
assert FT % 4 and FT % 2 == 0
MERGE = [(kind, jj) for kind in ("ga", "gf", "ao", "fo") for jj in range(4)]
GATE_BLOCKS = (4, 5, 10, 11)
MERGE_MOD = {2: 6, 4: 7, 6: 8, 8: 9, 10: 10, 12: 11}


def merged_plan(l):
    streams = (0, 1) if l == 0 else (1,)
    tiles, units = [], []
    for g in range(4):
        for pair in range(2):
            for s in streams:
                u = len(units)
                units.append((g, pair, s))
                tiles += [(u, g, 2 * pair + h, h, s, qt) for h in range(2) for qt in range(2)]
    per_group = len(tiles) // 4
    plan = [("fill", 0, i) for i in range(8)]
    for i in range(len(tiles) + 4):
        if i < len(tiles):
            plan.append(("score", i))
        if 1 <= i <= len(tiles):
            plan.append(("norm", i - 1))
        if 2 <= i < len(tiles) + 2:
            plan.append(("turn", i - 2))
        if i >= 6 and i % 4 == 2:
            plan.append(("pv", i // 4 - 1))
        if i >= 7 and i % 4 == 3:
            plan.append(("take", i // 4 - 1))
        g, at = divmod(i, per_group)
        if g < 3:
            step = per_group // 8
            if at % step == step - 1:
                plan.append(("fill", g + 1, at // step))
    return plan, tiles, units


def build(nc, w, out):
    ctx = ExitStack()
    with ctx:
        def sem(name):
            return ctx.enter_context(nc.semaphore(name))

        const = ctx.enter_context(nc.sbuf_tensor("const", [P, C_END], F32))
        small = ctx.enter_context(nc.sbuf_tensor("small", [P, S_END], F32))
        bmod = ctx.enter_context(nc.sbuf_tensor("bmod", [DEPTH * 12, 512], F32))
        x_res = ctx.enter_context(nc.sbuf_tensor("x_res", [P, TT, D], F32))
        w_hi = ctx.enter_context(nc.sbuf_tensor("w_hi", [P, HIS, SLOT], F32R))
        ring = ctx.enter_context(nc.sbuf_tensor("ring", [P, SLOTS, SLOT], F32))
        h_t = ctx.enter_context(nc.sbuf_tensor("h_t", [P, KD, NTOK], F32))
        at_h = nc.sbuf_base - 4 * KD * NTOK
        at_ring = at_h - 4 * SLOTS * SLOT
        assert (E_SLOTS - SLOTS) * SLOT <= KD * NTOK
        reg_q = ctx.enter_context(nc.sbuf_tensor("reg_q", [P, 12288], F32))
        at_q = nc.sbuf_base - 4 * 12288
        reg_v = ctx.enter_context(nc.sbuf_tensor("reg_v", [P, 2048], F32))
        at_v = nc.sbuf_base - 4 * 2048
        reg_a = ctx.enter_context(nc.sbuf_tensor("reg_a", [P, 4096], F32))
        at_a = nc.sbuf_base - 4 * 4096
        reg_f = ctx.enter_context(nc.sbuf_tensor("reg_f", [P, 2048], F32))
        at_f = nc.sbuf_base - 4 * 2048
        lat_kv = ctx.enter_context(nc.sbuf_tensor("lat_kv", [P, NTOK], F32))
        at_lat = nc.sbuf_base - 4 * NTOK
        lat_q = ctx.enter_context(nc.sbuf_tensor("lat_q", [P, 2, NTOK], F32))
        reg_p = ctx.enter_context(nc.sbuf_tensor("reg_p", [P, 3, 512], F32))
        at_p = nc.sbuf_base - 4 * 3 * 512
        reg_r = ctx.enter_context(nc.sbuf_tensor("reg_r", [P, 3, NTOK], F32))
        at_r = nc.sbuf_base - 4 * 3 * NTOK
        gate1 = ctx.enter_context(nc.sbuf_tensor("gate1", [P, 2, D], F32))
        gate2 = ctx.enter_context(nc.sbuf_tensor("gate2", [P, 2, D], F32))
        c_act = ctx.enter_context(nc.sbuf_tensor("c_act", [P, KD, 32], F32))
        modcol = ctx.enter_context(nc.sbuf_tensor("modcol", [P, DEPTH, 4, KD, 2], F32))
        stat = ctx.enter_context(nc.sbuf_tensor("stat", [P, 80], F32))
        bn = stat[:, 0:12].rearrange("p (a b) -> p a b", a=2)
        ln_mv = stat[:, 12:20].rearrange("p (n a) -> p n a", a=2)
        ln_std = stat[:, 20:24]
        ln_rstd = stat[:, 24:28]
        s_top, s_neg, s_sum, s_inv = (stat[:, 28 + 4 * i:32 + 4 * i] for i in range(4))
        c_sigm = stat[:, 48:48 + 2 * KD]
        psum = ctx.enter_context(nc.psum_tensor("psum", [P, 8, 512], F32))

        ident = const[:, C_ID:C_ID + P]
        dft_c = const[:, C_DFTC:C_DFTC + 2 * FC]
        dft_t = const[:, C_DFTT:C_DFTT + 4 * SEQ].rearrange("p (t a n) -> p t a n", t=2, a=2)
        cos = const[:, C_COS:C_COS + NTOK]
        sin = const[:, C_SIN:C_SIN + NTOK]
        perm = const[:, C_PERM:C_PERM + P]
        sel = const[:, C_SEL:C_SEL + 2]
        one = const[:, C_ONE:C_ONE + 1]
        eps = const[:, C_EPS:C_EPS + 1]
        b_cols = small[:, S_BMOD:S_END].rearrange("p (l c k) -> p l c k", l=DEPTH, k=4)
        c_raw = small[:, S_C:S_C + 2 * KD].rearrange("p (k s) -> p k s", s=2)
        w_router = small[:, S_ROUTER:S_BMOD].rearrange("p (k e) -> p k e", e=NE)

        q_t = reg_q[:, 0:4096].rearrange("p (b h n) -> p b h n", b=2, h=4)
        k_t = reg_q[:, 4096:8192].rearrange("p (b h n) -> p b h n", b=2, h=4)
        p_t = reg_q[:, 8192:12288].rearrange("p (b h k n) -> p b h k n", b=2, h=2, k=4)
        u_t = reg_q[:, 0:2048].rearrange("p (g n) -> p g n", g=FG)
        squares = reg_q[:, 8192:8192 + 3 * NTOK].rearrange("p (m n) -> p m n", m=3)
        rms = reg_q[:, 8192 + 3 * NTOK:8192 + 5 * NTOK].rearrange("p (m n) -> p m n", m=2)
        dft_1 = reg_q[:, 8192 + 5 * NTOK:8192 + 7 * NTOK].rearrange("p (b t n) -> p b t n", b=2, t=2)
        gates = reg_q[:, 4096:12288].rearrange("p (m n) -> p m n", m=2 * KD)
        merged = h_t
        a_t = reg_q[:, 0:FT * NTOK].rearrange("p (f n) -> p f n", f=FT)
        v_sb = reg_v[:, :].rearrange("p (b k n) -> p b k n", b=2, k=4)
        ln_rows = reg_v[:, :].rearrange("p (a n) -> p a n", a=2)
        attn_t = reg_a[:, :].rearrange("p (k n) -> p k n", k=KD)
        z_sb = reg_a[:, 0:2048].rearrange("p (b n) -> p b n", b=2)
        xn = reg_a[:, 2048:4096].rearrange("p (b n) -> p b n", b=2)
        four_t = reg_f[:, :].rearrange("p (g n) -> p g n", g=FG)
        ff_b = reg_f[:, :].rearrange("p (m n) -> p m n", m=4)
        k_rope = reg_r[:, 0, :]
        q_rope = reg_r[:, 0, :]
        rope_a = reg_r[:, 1, :]
        rope_b = reg_r[:, 2, :]
        mod_pm = reg_p

        def over(name, shape, offset):
            return nc.alloc_sbuf_tensor_at(name, shape, F32R, offset=offset)

        w_lo = over("w_lo", [P, E_SLOTS, SLOT], at_ring)
        e_ring = nc.alloc_sbuf_tensor_at("e_ring", [P, E_SLOTS, SLOT], F32, offset=at_ring)
        h_hi = over("h_hi", [P, KD, NTOK], at_h)
        h_lo = over("h_lo", [P, KD, NTOK], at_a)
        a_hi = over("a_hi", [P, 2, 4, NTOK], at_h)
        a_lo = over("a_lo", [P, 2, 4, NTOK], at_a)
        g_hi = over("g_hi", [P, KD, NTOK], at_q)
        g_lo = over("g_lo", [P, KD, NTOK], at_h)
        o_hi = [over("o_hi_v", [P, 4, NTOK], at_v), over("o_hi_r", [P, 3, NTOK], at_r),
                over("o_hi_l", [P, 1, NTOK], at_lat)]
        o_lo = over("o_lo", [P, KD, NTOK], at_a)
        O_PARTS = ((0, 4), (4, 7), (7, 8))
        f_hi = over("f_hi", [P, FG, NTOK], at_q)
        f_lo = over("f_lo", [P, FG, NTOK], at_f)
        m_hi = over("m_hi", [P, KD, NTOK], at_q + 4 * 4096)
        m_lo = over("m_lo", [P, KD, NTOK], at_h)
        xg_hi = over("xg_hi", [P, 2, KD, P], at_q + 4 * 4096)
        xg_lo = over("xg_lo", [P, 2, KD, P], at_a)
        at_hi = over("at_hi", [P, 2, 4, P], at_q + 4 * 6144)
        at_lo = over("at_lo", [P, 2, 4, P], at_q + 4 * 7168)
        y_hi = over("y_hi", [P, 2, D], at_f)
        y_lo = over("y_lo", [P, 2, D], at_p)
        sel_slot = over("sel_slot", [P, 2, 2, P], at_lat)
        sel_tok = lat_q[:, 0, :].rearrange("p (b t n) -> p b t n", b=2, t=2)
        xg_mod = gate1[:, :, :].rearrange("p h (b n) -> p h b n", b=2)
        h_mod = lat_q
        z_of = [None, reg_q[:, 8192:10240].rearrange("p (b n) -> p b n", b=2),
                reg_f[:, :].rearrange("p (b n) -> p b n", b=2), z_sb, z_sb]
        xn_2 = nc.alloc_sbuf_tensor_at("xn_2", [P, 2, D], F32, offset=at_lat)
        xn_of = [xn, reg_q[:, 10240:12288].rearrange("p (b n) -> p b n", b=2), xn_2, xn]

        at = [0]

        def part(n):
            at[0] += n
            return reg_q[:, at[0] - n:at[0]]

        e_sig = part(1024).rearrange("p (b n) -> p b n", b=2)
        e_tmp = part(1024).rearrange("p (b n) -> p b n", b=2)
        e_a = part(1024).rearrange("p (b n) -> p b n", b=2)
        assert at[0] <= 4096
        at[0] = 8192
        f_acc = part(2 * D).rearrange("p (t n) -> p t n", t=2)
        route_c = part(R_END)
        iota = route_c[:, R_IOTA:R_IOTA + P]
        tri = route_c[:, R_TRI:R_TRI + P]
        e_num = route_c[:, R_E:R_E + NE]
        rt = part(1024)
        assert at[0] <= 12288
        rt_at = [0]

        def rpart(n):
            rt_at[0] += n
            return rt[:, rt_at[0] - n:rt_at[0]]

        b_rout = rpart(NE)
        logits = rpart(2 * NE).rearrange("p (t e) -> p t e", t=2)
        top = rpart(2 * 8).rearrange("p (t e) -> p t e", t=2)
        top_i = rpart(2 * 8).rearrange("p (t e) -> p t e", t=2)
        top_if = rpart(2 * 8).rearrange("p (t e) -> p t e", t=2)
        pair_w = rpart(2 * 4).rearrange("p (t e) -> p t e", t=2)
        hot = rpart(4 * NE).rearrange("p (t k e) -> p t k e", t=2, k=2)
        taken = rpart(2 * NE).rearrange("p (t e) -> p t e", t=2)
        comb = rpart(2 * NE).rearrange("p (t e) -> p t e", t=2)
        tmp8 = rpart(2 * NE).rearrange("p (t e) -> p t e", t=2)
        place = rpart(2 * NE).rearrange("p (t e) -> p t e", t=2)
        full = rpart(NE)
        rank = rpart(NE)
        stand = rpart(NE)
        grid = rpart(2 * NE * NE).rearrange("p (a r e) -> p a r e", a=2, r=NE)
        job_at = rpart(4 * (NE + 1)).rearrange("p (b t j) -> p b t j", b=2, t=2)
        job_w = rpart(2 * (NE + 1)).rearrange("p (t j) -> p t j", t=2)
        job_e = rpart(NE)
        job_ei = rpart(NE).bitcast(I32)
        n_full = rpart(1)
        n_one = rpart(1)
        n_one_i = rpart(1).bitcast(I32)
        assert rt_at[0] <= 1024

        def blocks_at(nb, fc):
            return slice(0, 2) if nb == 2 else slice(fc % 2, fc % 2 + 1)

        landed = [sem(f"landed{i}") for i in range(E_SLOTS)]
        slot_free = sem("slot_free")
        hi_ok = sem("hi_ok")
        lo_dve, lo_pool = sem("lo_dve"), sem("lo_pool")
        w_used = sem("w_used")
        as_hi, as_lo = sem("as_hi"), sem("as_lo")
        consts_in = sem("consts_in")
        x_in = [sem(f"x_in{t}") for t in range(TT)]
        ln_in = [sem(f"ln_in{i}") for i in range(4)]
        route_in = sem("route_in")
        out_done = sem("out_done")
        c_sig = sem("c_sig")
        c_ready = sem("c_ready")
        mod_acc = sem("mod_acc")
        mod_copied = sem("mod_copied")
        mod_sum = sem("mod_sum")
        mod_done = sem("mod_done")
        dve_own = sem("dve_own")
        act_own = sem("act_own")
        pool_own = sem("pool_own")

        def layered(name):
            return [sem(f"{name}_{l}") for l in range(DEPTH)]

        var_ready, std_ready = sem("var_ready"), sem("std_ready")
        xn_ready = sem("xn_ready")
        xn_turned = [sem("xn_turned0"), sem("xn_turned1")]
        ht_act, ht_dve = sem("ht_act"), sem("ht_dve")
        z_scaled = sem("z_scaled")
        x_new = sem("x_new")
        in_mm, in_act, in_dve = layered("in_mm"), layered("in_act"), layered("in_dve")
        rms_mm, rms_act, lat_done = layered("rms_mm"), layered("rms_act"), layered("lat_done")
        kr_perm, kr_sum = layered("kr_perm"), layered("kr_sum")
        kr_done, kr_copied = layered("kr_done"), layered("kr_copied")
        f1_mm, f1_act, f2_mm, f2_dve = layered("f1_mm"), layered("f1_act"), layered("f2_mm"), layered("f2_dve")
        fill_mm, fill_act, fill_dve = layered("fill_mm"), layered("fill_act"), layered("fill_dve")
        rope_cos = layered("rope_cos")
        s_mm, s_max, s_exp, s_rec, s_nrm = (layered(n) for n in ("s_mm", "s_max", "s_exp", "s_rec", "s_nrm"))
        t_mm, t_out = layered("t_mm"), layered("t_out")
        pv_mm, pv_out = layered("pv_mm"), layered("pv_out")
        g_mm, g_sig, g_mul = layered("g_mm"), layered("g_sig"), layered("g_mul")
        ghi_ok, glo_ok = layered("ghi_ok"), layered("glo_ok")
        ohi_ok, olo_ok = layered("ohi_ok"), layered("olo_ok")
        fhi_ok, flo_ok = layered("fhi_ok"), layered("flo_ok")
        m_done, mhi_ok, mlo_ok = layered("m_done"), layered("mhi_ok"), layered("mlo_ok")
        y_mm = layered("y_mm")
        fg_mm, fu_mm, fg_sig, fa_done = sem("fg_mm"), sem("fu_mm"), sem("fg_sig"), sem("fa_done")
        fd_mm = sem("fd_mm")
        r_mm, r_taken, route_ready = sem("r_mm"), sem("r_taken"), sem("route_ready")
        r_diff, r_exp = sem("r_diff"), sem("r_exp")
        sel_ready = sem("sel_ready")
        xg_mm, xg_act, xg_dve = sem("xg_mm"), sem("xg_act"), sem("xg_dve")
        gu_mm, e_sig_ok, a_ok = sem("gu_mm"), sem("e_sig_ok"), sem("a_ok")
        at_mm, at_ok, at_lo_ok = sem("at_mm"), sem("at_ok"), sem("at_lo_ok")
        st_mm, st_ok = sem("st_mm"), sem("st_ok")
        y_zero, yhi_ok, y_dve = sem("y_zero"), sem("yhi_ok"), sem("y_dve")
        sc_mm, sc_ok = sem("sc_mm"), sem("sc_ok")
        e_tmp_ok = sem("e_tmp_ok")
        xm_ok, xd_ok, ga_mm = sem("xm_ok"), sem("xd_ok"), sem("ga_mm")

        chunks = ring_chunks(w)
        n_static = len(chunks)
        index_of = {name: n for n, (name, _) in enumerate(chunks)}
        arrive = []
        per_slot = [0] * E_SLOTS
        for n, (_, dmas) in enumerate(chunks):
            per_slot[n % SLOTS] += 16 * len(dmas)
            arrive.append(per_slot[n % SLOTS])

        is_split = [name[0] in SPLIT for name, _ in chunks]
        splits_before = [sum(is_split[:n]) for n in range(n_static + 1)]
        n_split = splits_before[n_static]
        split_list = [n for n in range(n_static) if is_split[n]]

        q_ffn = splits_before[index_of[("fg", 0)]]
        q_end = splits_before[index_of[("in", 1, 0)]]

        def slot_view(n, c0, shape):
            size = int(np.prod(shape))
            v = ring[:, n % SLOTS, c0:c0 + size]
            return v.rearrange("p (k n) -> p k n", k=shape[0]) if len(shape) == 2 else v

        q0 = [0, CTX]
        t0 = [0, 2]
        plans = [merged_plan(l) for l in range(DEPTH)]

        ln_uses = [(0, 1, range(TT)), (0, 2, range(TT)), (1, 1, range(TT)), (1, 2, range(2, TT))]
        tiles_before = [0, 4, 8, 12, 14]
        norms_before = [None, 0, 4, 8, 10]
        stats_before = [0, 4, 12, 20, 24]

        def chain(tiles):
            tiles = list(tiles)
            steps = []
            for i, t in enumerate(tiles):
                steps.append(("A", t))
                if i:
                    steps.append(("B", tiles[i - 1]))
            return steps + [("B", tiles[-1])]

        def fd_buffer(dh, i):
            return (dh * len(DOWN) + i) % 2

        def act_fills(g, i):
            return 7 * g + sum(k != 4 for k in range(i + 1))

        def dve_fills(g, i):
            return 5 * g + sum(k in (1, 2, 3, 4, 5) for k in range(i + 1))

        mod_order = [(l, cb) for l in range(DEPTH) for cb in range(12)]
        mod_at = {b: n for n, b in enumerate(mod_order)}

        block = ctx.enter_context(nc.Block())

        @block.sync
        def _(sp):
            sp.dma_start(small[:, :], w["small"]).then_inc(consts_in, 16)
            sp.dma_start(const[:, :], w["const"]).then_inc(consts_in, 16)
            sp.dma_start(bmod[:, :], w["b_mod"].rearrange("l (c n) -> (l c) n", n=512)).then_inc(consts_in, 16)

            def load(n):
                last = n - SLOTS
                if last >= 0 and is_split[last]:
                    sp.wait_ge(w_used, splits_before[last] + 1)
                elif last >= 0:
                    sp.wait_ge(slot_free, last - splits_before[last] + 1)
                for c0, shape, src in chunks[n][1]:
                    sp.dma_start(slot_view(n, c0, shape), src).then_inc(landed[n % SLOTS], 16)

            def load_ln(i, g, b):
                for a, v in ((0, g), (1, b)):
                    sp.dma_start(ln_rows[:, a, :], v.partition_broadcast(P)).then_inc(ln_in[i], 16)

            for n in range(4):
                load(n)
            for t in range(TT):
                src = w["ctx"][0] if t < 2 else w["x"][0]
                sp.dma_start(x_res[:, t, :], src[(t % 2) * P:(t % 2 + 1) * P, :]).then_inc(x_in[t], 16)
            for n in range(4, n_static):
                for l in range(DEPTH):
                    if n == index_of[("out", l, 0, 0)]:
                        sp.wait_ge(g_mm[l], 24)
                        load_ln(2 * l, w["ln1_g"][l], w["ln1_b"][l])
                if n == index_of[("fd", 0, 0)]:
                    sp.wait_ge(x_new, 4)
                    load_ln(1, w["ln2_g"][0], w["ln2_b"][0])
                load(n)

            def job(j, e):
                def chunk(c, src, shape):
                    sp.wait_ge(w_used, j * JOB_CHUNKS + (n_split + c - E_SLOTS + 1))
                    slot = c % E_SLOTS
                    view = e_ring[:, slot, :].rearrange("p (k n) -> p k n", k=shape[0])
                    sp.dma_start(view, src).then_inc(landed[slot], 16)

                gate = w["w_e_gate"].rearrange("a e (h k p) f -> (a e) h p k f", h=2, p=P)[bass.ds(e, 1)]
                up = w["w_e_up"].rearrange("a e (h k p) f -> (a e) h p k f", h=2, p=P)[bass.ds(e, 1)]
                down = w["w_e_down"].rearrange("a e (c h f p) n -> (a e) (c h) p f n", h=2, f=2, p=P)[bass.ds(e, 1)]
                c = 0
                for fc in range(NFC + 1):
                    if fc < NFC:
                        for v in (gate, up):
                            for h in range(2):
                                chunk(c, v[0, h, :, :, fc * 512:(fc + 1) * 512], (4, 512))
                                c += 1
                    if fc > 0:
                        for h in range(2):
                            chunk(c, down[0, 2 * (fc - 1) + h], (2, D))
                            c += 1

            sp.wait_ge(y_mm[1], 4)
            sp.dma_start(route_c, w["route"]).then_inc(route_in, 16)
            sp.dma_start(b_rout, w["b_router"][0].partition_broadcast(P)).then_inc(route_in, 16)
            sp.wait_ge(x_new, norms_before[4])
            load_ln(3, w["ln2_g"][1], w["ln2_b"][1])
            sp.wait_ge(slot_free, n_static - n_split)
            sp.wait_ge(w_used, n_split)
            sp.wait_ge(r_mm, 2)
            sp.wait_ge(route_ready, 1)
            with sp.Fori(0, NE) as j:
                job(j, sp.value_load(job_ei[0:1, bass.ds(j, 1)], min_val=0, max_val=NE - 1))
            for t in range(2):
                sp.wait_ge(x_new, norms_before[4] + t + 1)
                sp.dma_start(out[0, t * P:(t + 1) * P, :], x_res[:, 2 + t, :]).then_inc(out_done, 16)
            sp.wait_ge(out_done, 32)

        @block.tensor
        def _(pe):
            pending = []

            def mm(o, lhs, rhs, start, stop, sig=None, free=None, **kw):
                ins = pe.matmul(o, lhs, rhs, start=start, stop=stop, **kw)
                if free is not None:
                    pending.append(free)
                if sig is not None:
                    ins.then_inc(sig, 1)
                elif pending:
                    ins.then_inc(pending.pop(0), 1)
                return ins

            def mm3(o, lhs, rhs, start, stop, sig=None, free=None, **kw):
                mm(o, lhs[0], rhs[0], start, False, **kw)
                mm(o, lhs[0], rhs[1], False, False, **kw)
                mm(o, lhs[1], rhs[0], False, stop, sig=sig, free=free, **kw)

            def parts(q, slot, shape):
                size = int(np.prod(shape))
                return [v[:, i, 0:size].rearrange("p (k n) -> p k n", k=shape[0])
                        for v, i in ((w_hi, q % HIS), (w_lo, slot))]

            def split_chunk(name, shape):
                q = splits_before[index_of[name]]
                pe.wait_ge(lo_dve, q + 1)
                pe.wait_ge(lo_pool, q + 1)
                return parts(q, index_of[name] % SLOTS, shape)

            def arrived(name):
                n = index_of[name]
                pe.wait_ge(landed[n % SLOTS], arrive[n])
                return n

            def mod_block(b):
                l, cb = b
                n = mod_at[b]
                if n >= 1:
                    pe.wait_ge(mod_copied, n)
                for h in range(2):
                    v = slot_view(arrived(("mod", l, cb, h)), 0, (4, 512))
                    for k in range(4):
                        end = h == 1 and k == 3 and cb not in GATE_BLOCKS
                        mm(psum[32 * k:32 * k + 32, 4, :], c_act[:, 4 * h + k, :], v[:, k, :],
                           start=(h == 0), stop=(h == 1 and (k > 0 or cb not in GATE_BLOCKS)),
                           sig=mod_acc if end else None, free=slot_free if k == 3 else None, skip_group_check=True)
                if cb not in GATE_BLOCKS:
                    return
                row = l * 12 + cb
                mm(psum[0:32, 4, :], ident[0:DEPTH * 12, row:row + 1].to_broadcast([DEPTH * 12, 32]),
                   bmod[:, :], start=False, stop=True, sig=mod_acc, skip_group_check=True)

            def mod_reduce(b):
                l, cb = b
                n = mod_at[b]
                pe.wait_ge(mod_copied, n + 1)
                if n >= 1:
                    pe.wait_ge(mod_done, n)
                pm = mod_pm[:, n % 2, :]
                if cb in GATE_BLOCKS:
                    mm(psum[:, 5, :], sel[:, 0:1].to_broadcast([P, P]), pm, start=True, stop=True)
                    mm(psum[:, 6, :], sel[:, 1:2].to_broadcast([P, P]), pm, start=True, stop=True, sig=mod_sum)
                else:
                    for i in range(4):
                        mm(psum[:, 5, 2 * i:2 * i + 2], pm[:, i * P:(i + 1) * P], sel, start=True, stop=True,
                           sig=mod_sum if i == 3 else None)

            def turn_tiles(use):
                _, _, tiles = ln_uses[use]
                for i, t in enumerate(tiles):
                    n = tiles_before[use] + i
                    pe.wait_ge(xn_ready, n + 1)
                    for half in range(2):
                        if n >= 1:
                            reader = ht_act if half == 0 or (use == 1 and i >= 1) else ht_dve
                            pe.wait_ge(reader, n)
                        for k in range(4):
                            ins = pe.transpose(psum[:, 6 + half, k * P:(k + 1) * P],
                                               xn_of[use][:, t % 2, (4 * half + k) * P:(4 * half + k + 1) * P], ident)
                        ins.then_inc(xn_turned[half], 1)

            def input_projection(l):
                pe.wait_ge(ht_act, tiles_before[2 * l + 1])
                pe.wait_ge(ht_dve, tiles_before[2 * l + 1])
                groups = [(0, 0, 0, 0), (0, P, 0, 0), (1, 0, 0, 1), (1, P, 64, 1),
                          (2, 0, 0, 0), (2, P, 0, 0), (3, 0, 0, 0), (3, P, 0, 0)]
                for i, (ch, c0, part0, full) in enumerate(groups):
                    name = ("in", l, ch)
                    shape = (KD, 160 if ch == 1 else 256)
                    v = slot_view(arrived(name), 0, shape)
                    m = ROPE if part0 else P
                    a = 0 if full else q0[l]
                    if i >= 4:
                        if i - 4 < 3:
                            pe.wait_ge(in_act[l], i - 3)
                        else:
                            pe.wait_ge(in_dve[l], 1)
                    for k in range(KD):
                        last = k == KD - 1
                        mm(psum[part0:part0 + m, i % 4, a:NTOK], v[:, k, c0:c0 + m], h_t[:, k, a:NTOK],
                           start=(k == 0), stop=last, sig=in_mm[l] if last else None,
                           free=slot_free if last and i in (1, 3, 5, 7) else None)

            def latent_norms(l):
                a = q0[l]
                pe.wait_ge(in_act[l], 3)
                for k in range(2):
                    mm(psum[:, 4, a:NTOK], one.to_broadcast([P, P]), squares[:, k, a:NTOK], start=(k == 0),
                       stop=(k == 1), sig=rms_mm[l] if k == 1 else None)
                mm(psum[:, 5, :], one.to_broadcast([P, P]), squares[:, 2, :], start=True, stop=True, sig=rms_mm[l])
                pe.wait_ge(in_dve[l], 1)
                mm(psum[64:96, 6, :], perm[64:96, 64:96], k_rope[64:96, :], start=True, stop=True, sig=kr_perm[l])

            def fourier(l):
                units = [(g, s) for g in range(FG) for s in ((0, 1) if l == 0 else (1,))]

                def second(n):
                    g, s = units[n]
                    pe.wait_ge(f1_act[l], n + 1)
                    if n >= 2:
                        pe.wait_ge(f2_dve[l], n - 1)
                    i = 0
                    for t in range(2):
                        for a in range(2):
                            mm(psum[:, 2 + n % 2, 0:SEQ], dft_1[:, n % 2, t, a * FC:(a + 1) * FC], dft_t[:, t, a, :],
                               start=(i == 0), stop=(i == 3), sig=f2_mm[l] if i == 3 else None)
                            i += 1

                pe.wait_ge(in_dve[l], 5)
                for n, (g, s) in enumerate(units):
                    if n >= 2:
                        pe.wait_ge(f1_act[l], n - 1)
                    for t in range(2):
                        mm(psum[:, n % 2, t * 256:(t + 1) * 256],
                           u_t[:, g, s * SEQ + t * P:s * SEQ + (t + 1) * P], dft_c,
                           start=True, stop=True, sig=f1_mm[l] if t == 1 else None)
                    if n >= 1:
                        second(n - 1)
                second(len(units) - 1)

            def attention(l):
                plan, tiles, units = plans[l]
                a = q0[l]
                pe.wait_ge(lat_done[l], 1)
                pe.wait_ge(f2_dve[l], FG * (2 if l == 0 else 1))

                def fill(g, i):
                    n = 8 * g + i
                    v = arrived(("heads", l, g))
                    uq = slot_view(v, 0, (2, 4 * QK))
                    uk = slot_view(v, 768, (256,))
                    uv = slot_view(v, 1024, (256,))
                    b = i % 2
                    if n >= 2:
                        before = (g, i - 2) if i >= 2 else (g - 1, i + 6)
                        pe.wait_ge(fill_act[l], act_fills(*before))
                        if dve_fills(*before):
                            pe.wait_ge(fill_dve[l], dve_fills(*before))
                    if i == 0:
                        for k in range(2):
                            mm(psum[:, b, a:NTOK], uq[:, k, 0:4 * ROPE], lat_q[:, k, a:NTOK], start=(k == 0),
                               stop=(k == 1), sig=fill_mm[l] if k == 1 else None)
                    elif i in (1, 2):
                        c0 = 4 * ROPE + (i - 1) * P
                        for k in range(2):
                            mm(psum[:, b, a:NTOK], uq[:, k, c0:c0 + P], lat_q[:, k, a:NTOK],
                               start=(k == 0), stop=(k == 1), sig=fill_mm[l] if k == 1 else None)
                    elif i in (3, 5):
                        c0 = 0 if i == 3 else P
                        mm(psum[:, b, :], uk[:, c0:c0 + P], lat_kv[:, :], start=True, stop=True, sig=fill_mm[l])
                    elif i == 4:
                        pe.wait_ge(fill_act[l], act_fills(g, 0))
                        mm(psum[:, b, a:NTOK], perm, q_rope[:, a:NTOK], start=True, stop=True, sig=fill_mm[l])
                    else:
                        for kt in range(2):
                            t = 2 * (i - 6) + kt
                            mm(psum[:, b, kt * 256:(kt + 1) * 256], lat_kv[:, t * P:(t + 1) * P], uv,
                               start=True, stop=True, sig=fill_mm[l] if kt == 1 else None,
                               free=slot_free if i == 7 and kt == 1 else None)

                def score(c):
                    u, g, h, _, s, qt = tiles[c]
                    pe.wait_ge(fill_act[l], act_fills(g, 7))
                    pe.wait_ge(fill_dve[l], dve_fills(g, 7))
                    pe.wait_ge((kr_done, kr_copied)[g % 2][l], 1)
                    if c >= 2:
                        pe.wait_ge(s_exp[l], c - 1)
                    nk = CTX if s == 0 else NTOK
                    at_q = s * SEQ + qt * P
                    mm(psum[:, 2 + c % 2, 0:nk], q_t[0:QK, g % 2, h, at_q:at_q + P], k_t[0:QK, g % 2, h, 0:nk],
                       start=True, stop=True, sig=s_mm[l])

                def turn(c):
                    s = tiles[c][4]
                    pe.wait_ge(s_nrm[l], c + 1)
                    if c >= 2:
                        pe.wait_ge(t_out[l], c - 1)
                    nt = 2 if s == 0 else 4
                    for k in range(nt):
                        ins = pe.transpose(psum[:, 4 + c % 2, k * P:(k + 1) * P], reg_p[:, c % 3, k * P:(k + 1) * P],
                                           ident)
                    ins.then_inc(t_mm[l], 1)

                def pv(u):
                    g, pair, s = units[u]
                    pe.wait_ge(t_out[l], 4 * u + 4)
                    if u >= 2:
                        pe.wait_ge(pv_out[l], u - 1)
                    nt = 2 if s == 0 else 4
                    for k in range(nt):
                        for h in range(2):
                            c0 = (2 * pair + h) * VH
                            mm(psum[VH * h:VH * h + VH, 6 + u % 2, 0:SEQ], v_sb[:, g % 2, k, c0:c0 + VH],
                               p_t[:, u % 2, h, k, :], start=(k == 0), stop=(k == nt - 1),
                               sig=pv_mm[l] if k == nt - 1 and h == 1 else None, skip_group_check=True)

                for step in plan:
                    if step[0] == "fill":
                        fill(step[1], step[2])
                    elif step[0] == "score":
                        score(step[1])
                    elif step[0] == "turn":
                        turn(step[1])
                    elif step[0] == "pv":
                        pv(step[1])

            def merge(l):
                a = q0[l]
                units = plans[l][2]
                pe.wait_ge(pv_out[l], len(units))
                for u, (kind, jj) in enumerate(MERGE):
                    kn = FG if kind == "fo" else KD
                    v = split_chunk((kind, l, jj), (kn, 256))
                    if u == 8:
                        pe.wait_ge(olo_ok[l], len(O_PARTS))
                    if u == 12:
                        pe.wait_ge(flo_ok[l], 1)
                    for i in range(2):
                        n = 2 * u + i
                        if 4 <= n < 20:
                            pe.wait_ge(g_sig[l], n - 3)
                        elif n >= 20:
                            pe.wait_ge(g_mul[l], n - 19)
                        for k in range(kn):
                            if n == 0 and k % 2 == 0:
                                pe.wait_ge(glo_ok[l], k // 2 + 1)
                            if kind in ("ga", "gf"):
                                x = (g_hi[:, k, a:NTOK], g_lo[:, k, a:NTOK])
                            elif kind == "ao":
                                part = (k >= 4) + (k >= 7)
                                x = (o_hi[part][:, k - O_PARTS[part][0], a:NTOK], o_lo[:, k, a:NTOK])
                            else:
                                x = (f_hi[:, k, a:NTOK], f_lo[:, k, a:NTOK])
                            last = k == kn - 1
                            mm3(psum[:, n % 4, a:NTOK], [y[:, k, i * P:(i + 1) * P] for y in v], x,
                                start=(k == 0), stop=last, sig=g_mm[l] if last else None,
                                free=w_used if last and i == 1 else None)
                    if u - 1 in MERGE_MOD:
                        mod_reduce((l, MERGE_MOD[u - 1]))
                    if u in MERGE_MOD:
                        mod_block((l, MERGE_MOD[u]))

            def output_projection(l):
                pe.wait_ge(mod_done, mod_at[(l, 11)] + 1)
                for dh in range(2):
                    for kk in range(2):
                        v = split_chunk(("out", l, dh, kk), (4, 512))
                        pe.wait_ge(mlo_ok[l], 2 * kk + 2)
                        if dh == 1:
                            pe.wait_ge(g_mul[l], 16)
                        for i, t in enumerate(range(t0[l], TT)):
                            cols = slice(t * P, (t + 1) * P)
                            for k in range(4):
                                last = kk == 1 and k == 3
                                kc = 4 * kk + k
                                mm3(psum[:, 4 - 4 * dh + i, :], (m_hi[:, kc, cols], m_lo[:, kc, cols]),
                                    [x[:, k, :] for x in v], start=(kk == 0 and k == 0), stop=last,
                                    sig=y_mm[l] if last else None, free=w_used if t == TT - 1 and k == 3 else None)

            def dense_mixer():
                pe.wait_ge(ht_act, tiles_before[2])
                pe.wait_ge(ht_dve, tiles_before[2])
                for fp in range(FT // 2):
                    for m, kind in enumerate(("fg", "fu")):
                        v = split_chunk((kind, fp), (KD, 256))
                        for i in range(2):
                            if fp >= 1:
                                pe.wait_ge(fa_done, 2 * fp - 1 + i)
                            for k in range(KD):
                                last = k == KD - 1
                                mm3(psum[:, 2 * m + i, :], [x[:, k, i * P:(i + 1) * P] for x in v],
                                    (h_hi[:, k, :], h_lo[:, k, :]), start=(k == 0), stop=last,
                                    sig=(fg_mm, fu_mm)[m] if last else None, free=w_used if last and i == 1 else None)
                        if m == 0 and 3 <= fp < 9:
                            mod_reduce((1, fp - 3))
                    if 2 <= fp < 8:
                        mod_block((1, fp - 2))
                for dh in range(2):
                    for i, (fg, n) in enumerate(DOWN):
                        v = split_chunk(("fd", dh, fg), (n, 512))
                        b = fd_buffer(dh, i)
                        order = [(f, t) for f in range(fg, fg + n) for t in range(TT)]
                        if i == len(DOWN) - 1:
                            order = [(f, t) for t in range(TT) for f in range(fg, fg + n)]
                        if i == 0 and dh == 0:
                            pe.wait_ge(mod_done, mod_at[(1, 5)] + 1)
                        for f, t in order:
                            pe.wait_ge(as_hi, dh * FT + f + 1)
                            pe.wait_ge(as_lo, dh * FT + f + 1)
                            cols = slice(t * P, (t + 1) * P)
                            mm3(psum[:, (4 if dh == 0 else 0) + t, :],
                                (a_hi[:, b, f - fg, cols], a_lo[:, b, f - fg, cols]), [x[:, f - fg, :] for x in v],
                                start=(f == 0), stop=(f == FT - 1), sig=fd_mm if f == FT - 1 else None,
                                free=w_used if (f, t) == order[-1] else None)

            def router():
                pe.wait_ge(ht_act, tiles_before[4])
                pe.wait_ge(ht_dve, tiles_before[4])
                for t in range(2):
                    for k in range(KD):
                        mm(psum[:, t, 0:NE], h_t[:, k, CTX + t * P:CTX + (t + 1) * P], w_router[:, k, :],
                           start=(k == 0), stop=(k == KD - 1), sig=r_mm if k == KD - 1 else None)
                pe.wait_ge(r_taken, 1)
                mm(psum[:, 2, 0:NE], tri, taken[:, 0, :], start=True, stop=True)
                mm(psum[:, 3, 0:NE], one.to_broadcast([P, P]), taken[:, 0, :], start=True, stop=False)
                mm(psum[:, 3, 0:NE], tri, taken[:, 1, :], start=False, stop=True)
                mm(psum[:, 4, 0:NE], one.to_broadcast([P, P]), taken[:, 0, :], start=True, stop=False)
                mm(psum[:, 4, 0:NE], one.to_broadcast([P, P]), taken[:, 1, :], start=False, stop=True, sig=r_mm)

            def gather(nb, half):
                for b in range(nb):
                    bank = 2 * half + (b if nb == 2 else 1)
                    for k in range(4):
                        d0 = (4 * half + k) * P
                        for t in range(2):
                            end = b == nb - 1 and half == 1 and k == 3 and t == 1
                            mm(psum[:, bank, k * P:(k + 1) * P], xn[:, t, d0:d0 + P], sel_tok[:, b, t, :],
                               start=(t == 0), stop=(t == 1), sig=xg_mm if end else None)

            def scatter(nb):
                n = 0
                for t in range(2):
                    for dh in range(2):
                        parts_of_y = [(b, y) for b in range(nb) for y in (y_hi, y_lo)]
                        for i, (b, y) in enumerate(parts_of_y):
                            last = i == len(parts_of_y) - 1
                            mm(psum[:, 4 + n, :], sel_slot[:, b, t, :], y[:, 1 - b, dh * 512:(dh + 1) * 512],
                               start=(i == 0), stop=last, sig=sc_mm if last else None)
                        n += 1

            def experts(nb, first, end):
                y_banks = [(6, 7), (4, 5)]
                with pe.Fori(first, end) as j:
                    c = [0]

                    def chunk_products(shape, products, done):
                        q = n_split + c[0]
                        hi, lo = parts(q, c[0] % E_SLOTS, shape)
                        c[0] += 1
                        pe.wait_ge(hi_ok, j * JOB_CHUNKS + (q + 1))
                        for o, x, at, start, _ in products:
                            mm(o, x[0], hi[at], start=start, stop=False, skip_group_check=True)
                            mm(o, x[1], hi[at], start=False, stop=False, skip_group_check=True)
                        pe.wait_ge(lo_dve, j * JOB_CHUNKS + (q + 1))
                        pe.wait_ge(lo_pool, j * JOB_CHUNKS + (q + 1))
                        for n, (o, x, at, _, stop) in enumerate(products):
                            last = n == len(products) - 1
                            mm(o, x[0], lo[at], start=False, stop=stop, sig=done if last else None,
                               free=w_used if last else None, skip_group_check=True)

                    def gate_or_up(fc, bank, sig):
                        for h in range(2):
                            products = []
                            for k in range(4):
                                for b in range(nb):
                                    o = psum[:, bank + (b if nb == 2 else fc % 2), :]
                                    products.append((o, (xg_hi[:, b, 4 * h + k, :], xg_lo[:, b, 4 * h + k, :]),
                                                     (slice(None), k), h == 0 and k == 0, h == 1 and k == 3))
                            chunk_products((4, 512), products, sig if h == 1 else None)

                    def turn_a(fc):
                        pe.wait_ge(a_ok, j * NFC + (fc + 1))
                        for b in range(nb):
                            for i in range(4):
                                ins = pe.transpose(psum[:, 4 if nb == 1 else 2 + b, i * P:(i + 1) * P],
                                                   e_a[:, b if nb == 2 else fc % 2, i * P:(i + 1) * P], ident)
                        ins.then_inc(at_mm, 1)

                    def down(fc):
                        pe.wait_ge(at_ok, j * NFC + (fc + 1))
                        pe.wait_ge(at_lo_ok, j * NFC + (fc + 1))
                        for h in range(2):
                            products = []
                            for f in range(2):
                                for b in range(nb):
                                    i = b if nb == 2 else fc % 2
                                    x = (at_hi[:, i, 2 * h + f, :], at_lo[:, i, 2 * h + f, :])
                                    for dh in range(2):
                                        products.append((psum[:, y_banks[b][dh], :], x,
                                                         (slice(None), f, slice(dh * 512, (dh + 1) * 512)),
                                                         fc == 0 and h == 0 and f == 0,
                                                         fc == NFC - 1 and h == 1 and f == 1))
                            chunk_products((2, D), products, None)

                    pe.wait_ge(xg_act, j + 1)
                    pe.wait_ge(xg_dve, j + 1)
                    for fc in range(NFC):
                        if nb == 2 and fc >= 1:
                            turn_a(fc - 1)
                        if nb == 1 and fc >= 2:
                            pe.wait_ge(a_ok, j * NFC + (fc - 1))
                        gate_or_up(fc, 0, ga_mm)
                        if fc == 1:
                            pe.wait_ge(sc_ok, j * 4 + 4)
                            for b in range(nb):
                                for t in range(2):
                                    ins = pe.transpose(psum[:, 6 - nb, (2 * b + t) * P:(2 * b + t + 1) * P],
                                                       sel_tok[:, b, t, :], ident)
                            ins.then_inc(st_mm, 1)
                        if nb == 1 and fc >= 1:
                            turn_a(fc - 1)
                        if nb == 2 and fc >= 1:
                            pe.wait_ge(at_lo_ok, j * NFC + fc)
                        gate_or_up(fc, 2, gu_mm)
                        if fc == 0:
                            pe.wait_ge(y_dve, j + 1)
                            pe.wait_ge(st_ok, j + 1)
                            scatter(nb)
                        else:
                            if nb == 2 and fc == 1:
                                pe.wait_ge(st_ok, j + 2)
                            down(fc - 1)
                    pe.wait_ge(sel_ready, j + 2)
                    turn_a(NFC - 1)
                    gather(nb, 0)
                    if nb == 2:
                        pe.wait_ge(at_lo_ok, j * NFC + NFC)
                    gather(nb, 1)
                    down(NFC - 1)

            pe.wait_ge(consts_in, 48)
            pe.wait_ge(c_ready, 1)
            mod_block((0, 0))
            for cb in range(1, 6):
                mod_reduce((0, cb - 1))
                mod_block((0, cb))
            mod_reduce((0, 5))
            pe.wait_ge(mod_done, 6)
            turn_tiles(0)
            for l in range(DEPTH):
                input_projection(l)
                latent_norms(l)
                fourier(l)
                attention(l)
                merge(l)
                output_projection(l)
                turn_tiles(2 * l + 1)
                if l == 0:
                    dense_mixer()
                    turn_tiles(2)
            router()
            pe.wait_ge(route_ready, 1)
            ones = pe.value_load(n_one_i[0:1, 0:1], min_val=MIN_ONE, max_val=NE - 1)
            pe.wait_ge(sel_ready, 1)
            gather(2, 0)
            gather(2, 1)
            experts(1, 0, ones)
            experts(2, ones, NE)
            pe.wait_ge(y_dve, NE + 1)
            pe.wait_ge(st_ok, NE + 1)
            scatter(2)

        @block.scalar
        def _(act):
            own = [0]

            def link(ins):
                own[0] += 1
                ins.then_inc(act_own, 1)
                act.wait_ge(act_own, own[0])

            def mod_copy(b):
                n = mod_at[b]
                act.wait_ge(mod_acc, n + 1)
                if n >= 2:
                    act.wait_ge(mod_sum, n - 1)
                act.activation(mod_pm[:, n % 2, :], psum[:, 4, :], ACT.Copy).then_inc(mod_copied, 1)

            def std(n):
                act.wait_ge(var_ready, n + 1)
                act.activation(ln_std[:, n % 4:n % 4 + 1], ln_mv[:, n % 4, 1:2], ACT.Sqrt, bias=eps)\
                   .then_inc(std_ready, 1)

            def split_hi(q):
                n = split_list[q]
                act.wait_ge(landed[n % SLOTS], arrive[n])
                if q >= HIS:
                    act.wait_ge(w_used, q - HIS + 1)
                size = sum(int(np.prod(shape)) for _, shape, _ in chunks[n][1])
                act.activation(w_hi[:, q % HIS, 0:size], ring[:, n % SLOTS, 0:size], ACT.Copy).then_inc(hi_ok, 1)

            def modulate(l, which, t, n, between=None):
                act.wait_ge(xn_turned[0], n + 1)
                s, m = t // 2, 2 * (which - 1)
                if (l, which) == (0, 2):
                    act.wait_ge(xn_turned[1], n + 1)
                    if n > tiles_before[1]:
                        act.wait_ge(ht_dve, n)
                    for k in range(KD):
                        if k == 4 and between is not None:
                            between()
                        ins = act.activation(h_mod[:, k // 4, k % 4 * P:(k % 4 + 1) * P],
                                             psum[:, 6 + k // 4, k % 4 * P:(k % 4 + 1) * P],
                                             ACT.Identity, bias=modcol[:, l, m, k, s:s + 1],
                                             scale=modcol[:, l, m + 1, k, s:s + 1])
                    link(ins)
                    act.activation(h_hi[:, :, t * P:(t + 1) * P],
                                   h_mod[:, :, :].rearrange("p a (k n) -> p (a k) n", k=4), ACT.Copy)\
                       .then_inc(ht_act, 1)
                    return
                for k in range(4):
                    ins = act.activation(h_t[:, k, t * P:(t + 1) * P], psum[:, 6, k * P:(k + 1) * P], ACT.Identity,
                                         bias=modcol[:, l, m, k, s:s + 1], scale=modcol[:, l, m + 1, k, s:s + 1])
                ins.then_inc(ht_act, 1)

            def norm_chain(use):
                l, which, tiles = ln_uses[use]
                n = stats_before[use]
                steps = chain(tiles)
                early = None
                for i, (step, t) in enumerate(steps):
                    if early != i:
                        std(n)
                    n += 1
                    if step == "B":
                        between = None
                        if use == 1 and i + 1 < len(steps) and steps[i + 1][0] == "A":
                            early = i + 1
                            between = lambda n=n: std(n)
                        modulate(l, which, t, tiles_before[use] + t - tiles[0], between)

            act.wait_ge(consts_in, 48)
            act.activation(c_sigm, small[:, S_C:S_C + 2 * KD], ACT.Sigmoid).then_inc(c_sig, 1)
            std(0)
            std(1)
            for cb in range(6):
                mod_copy((0, cb))
            act.wait_ge(mod_done, 6)
            for t in range(2, TT):
                std(t)
                modulate(0, 1, t - 2, t - 2)
            modulate(0, 1, 2, 2)
            modulate(0, 1, 3, 3)

            for l in range(DEPTH):
                a = q0[l]
                for i in range(3):
                    act.wait_ge(in_mm[l], i + 1)
                    if i < 2:
                        dst, gcol, c0 = lat_q[:, i, a:NTOK], S_GQ + 2 * l + i, a
                    else:
                        dst, gcol, c0 = lat_kv[:, :], S_GKV + l, 0
                    act.activation(dst, psum[:, i, c0:NTOK], ACT.Copy, scale=small[:, gcol:gcol + 1])
                    act.activation(squares[:, i, c0:NTOK], psum[:, i, c0:NTOK], ACT.Square).then_inc(in_act[l], 1)
                for i, (c0, n) in enumerate(((a, Q_LORA), (0, KV_LORA))):
                    act.wait_ge(rms_mm[l], i + 1)
                    act.activation(rms[:, i, c0:NTOK], psum[:, 4 + i, c0:NTOK], ACT.Sqrt, bias=eps, scale=1.0 / n)\
                       .then_inc(rms_act[l], 1)
                units = FG * (2 if l == 0 else 1)
                for n in range(units):
                    act.wait_ge(f1_mm[l], n + 1)
                    if n >= 2:
                        act.wait_ge(f2_mm[l], n - 1)
                    act.activation(dft_1[:, n % 2, :, :], psum[:, n % 2, :], ACT.Copy).then_inc(f1_act[l], 1)

                plan, tiles, att = plans[l]
                q_m = splits_before[index_of[("ga", l, 0)]]

                def fill(g, i):
                    n = 8 * g + i
                    if i == 4:
                        return
                    act.wait_ge(fill_mm[l], n + 1)
                    b = i % 2
                    if g >= 2 and i in (1, 6):
                        act.wait_ge(pv_mm[l], len(att) // 4 * (g - 1))
                    if i == 0:
                        if g >= 1:
                            act.wait_ge(fill_dve[l], dve_fills(g - 1, 4))
                        else:
                            act.wait_ge(kr_done[l], 1)
                            act.wait_ge(kr_copied[l], 1)
                        act.activation(q_rope[:, a:NTOK], psum[:, b, a:NTOK], ACT.Copy).then_inc(fill_act[l], 1)
                    elif i in (1, 2):
                        h = 2 * (i - 1)
                        act.activation(q_t[0:NOPE, g % 2, h, a:NTOK], psum[0:NOPE, b, a:NTOK], ACT.Copy)\
                           .then_inc(fill_act[l], 1)
                    elif i in (3, 5):
                        h = 0 if i == 3 else 2
                        act.activation(k_t[0:NOPE, g % 2, h, :], psum[0:NOPE, b, :], ACT.Copy).then_inc(fill_act[l], 1)
                    else:
                        act.activation(v_sb[:, g % 2, 2 * (i - 6):2 * (i - 5), :], psum[:, b, :], ACT.Copy)\
                           .then_inc(fill_act[l], 1)

                def exp(c):
                    s = tiles[c][4]
                    nk = CTX if s == 0 else NTOK
                    act.wait_ge(s_max[l], c + 1)
                    if c >= 3:
                        act.wait_ge(t_mm[l], c - 2)
                    act.activation(reg_p[:, c % 3, 0:nk], psum[:, 2 + c % 2, 0:nk], ACT.Exp,
                                   bias=s_neg[:, c % 4:c % 4 + 1], scale=SM_SCALE,
                                   accum_out=s_sum[:, c % 4:c % 4 + 1]).then_inc(s_exp[l], 1)

                def turned(c):
                    u, g, _, h, s, qt = tiles[c]
                    nt = 2 if s == 0 else 4
                    act.wait_ge(t_mm[l], c + 1)
                    if u >= 2:
                        act.wait_ge(pv_mm[l], u - 1)
                    act.activation(p_t[:, u % 2, h, 0:nt, qt * P:(qt + 1) * P],
                                   psum[:, 4 + c % 2, 0:nt * P].rearrange("p (k n) -> p k n", k=nt), ACT.Copy)\
                       .then_inc(t_out[l], 1)

                for step in plan:
                    if step[0] == "fill":
                        fill(step[1], step[2])
                    elif step[0] == "score":
                        exp(step[1])
                    elif step[0] == "turn":
                        turned(step[1])
                        if len(tiles) - step[1] in (12, 8, 4):
                            split_hi(q_m + 3 - (len(tiles) - step[1]) // 4)

                def merged_hi(jj):
                    act.wait_ge(m_done[l], 2 * jj + 2)
                    act.activation(m_hi[:, 2 * jj:2 * jj + 2, a:NTOK], merged[:, 2 * jj:2 * jj + 2, a:NTOK], ACT.Copy)\
                       .then_inc(mhi_ok[l], 1)

                act.wait_ge(s_mm[l], len(tiles))
                for k in range(0, KD, 2):
                    act.activation(g_hi[:, k:k + 2, a:NTOK], h_t[:, k:k + 2, a:NTOK], ACT.Copy).then_inc(ghi_ok[l], 1)
                act.wait_ge(pv_out[l], len(att))
                q_out = q_m + len(MERGE)
                for u, (kind, jj) in enumerate(MERGE):
                    if u < 8:
                        for n in (2 * u, 2 * u + 1):
                            act.wait_ge(g_mm[l], n + 1)
                            act.activation(gates[:, n, a:NTOK], psum[:, n % 4, a:NTOK], ACT.Sigmoid)\
                               .then_inc(g_sig[l], 1)
                    if u in MERGE_MOD:
                        mod_copy((l, MERGE_MOD[u]))
                    if u < len(O_PARTS):
                        k0, k1 = O_PARTS[u]
                        act.activation(o_hi[u][:, :, a:NTOK], attn_t[:, k0:k1, a:NTOK], ACT.Copy).then_inc(ohi_ok[l], 1)
                    if u == 8:
                        act.wait_ge(g_mm[l], 16)
                        act.activation(f_hi[:, :, a:NTOK], four_t[:, :, a:NTOK], ACT.Copy).then_inc(fhi_ok[l], 1)
                    if u >= 13:
                        merged_hi(u - 13)
                    if u == 15:
                        merged_hi(3)
                    split_hi(q_m + u + HIS)
                split_hi(q_out + 3)
                if l == 0:
                    split_hi(q_ffn)
                    split_hi(q_ffn + 1)
                norm_chain(2 * l + 1)

                if l == 0:
                    split_hi(q_ffn + 2)
                    for fp in range(FT // 2):
                        for f in (2 * fp, 2 * fp + 1):
                            act.wait_ge(fg_mm, f + 1)
                            if f >= 2:
                                act.wait_ge(fa_done, f - 1)
                            act.activation(ff_b[:, f % 2, :], psum[:, f % 2, :], ACT.Sigmoid).then_inc(fg_sig, 1)
                        if 2 <= fp < 8:
                            mod_copy((1, fp - 2))
                        split_hi(q_ffn + 2 * fp + 3)
                        if 2 * fp + 4 < FT + HIS - 1:
                            split_hi(q_ffn + 2 * fp + 4)
                    q = q_ffn + FT
                    for dh in range(2):
                        for i, (fg, n) in enumerate(DOWN):
                            if dh or i:
                                act.wait_ge(w_used, q - 1)
                            else:
                                act.wait_ge(fu_mm, FT)
                            for f in range(fg, fg + n):
                                act.wait_ge(fa_done, f + 1)
                                act.activation(a_hi[:, fd_buffer(dh, i), f - fg, :], a_t[:, f, :], ACT.Copy)\
                                   .then_inc(as_hi, 1)
                            if q + 2 < q_end:
                                split_hi(q + 2)
                            q += 1
                    norm_chain(2)

            act.wait_ge(r_diff, 1)
            act.activation(pair_w[:, :, 1], pair_w[:, :, 0], ACT.Exp).then_inc(r_exp, 1)
            act.wait_ge(route_ready, 1)
            ones = act.value_load(n_one_i[0:1, 0:1], min_val=MIN_ONE, max_val=NE - 1)

            def gathered(nb, j):
                act.wait_ge(xg_mm, j + 1)
                src = psum[:, 1:2, :] if nb == 1 else psum[:, 0:2, :]
                for k in range(4):
                    cols = slice(k * P, (k + 1) * P)
                    ins = act.activation(xg_mod[:, 0, 0:nb, cols], src[:, :, cols], ACT.Identity,
                                         bias=modcol[:, 1, 2, k, 1:2], scale=modcol[:, 1, 3, k, 1:2])
                ins.then_inc(xm_ok, 1)
                act.wait_ge(xm_ok, j + 1)
                act.activation(xg_hi[:, 0:nb, 0:4, :].rearrange("p b k n -> p b (k n)"), xg_mod[:, 0, 0:nb, :],
                               ACT.Copy).then_inc(xg_act, 1)

            def outputs_hi(nb, j):
                act.wait_ge(w_used, j * JOB_CHUNKS + n_split)
                act.wait_ge(y_zero, nb)
                act.activation(y_hi[:, 2 - nb:2, :].rearrange("p b n -> p (b n)"),
                               psum[:, 8 - 2 * nb:8, :].rearrange("p b n -> p (b n)"), ACT.Copy).then_inc(yhi_ok, 1)

            def experts(nb, first, end):
                with act.Fori(first, end) as j:
                    def split_hi_of(c):
                        slot = c % E_SLOTS
                        q = n_split + c
                        act.wait_ge(landed[slot], j * (16 * SLOT_TURNS) + (per_slot[slot] + 16 * (c // E_SLOTS + 1)))
                        act.wait_ge(w_used, j * JOB_CHUNKS + (q - HIS + 1))
                        act.activation(w_hi[:, q % HIS, :], e_ring[:, slot, :], ACT.Copy).then_inc(hi_ok, 1)

                    def turned_a(fc):
                        act.wait_ge(at_mm, j * NFC + (fc + 1))
                        i = blocks_at(nb, fc)
                        src = psum[:, 4:5, :] if nb == 1 else psum[:, 2:4, :]
                        act.activation(at_hi[:, i, :, :].rearrange("p b f n -> p b (f n)"), src, ACT.Copy)\
                           .then_inc(at_ok, 1)

                    split_hi_of(0)
                    split_hi_of(1)
                    outputs_hi(nb, j)
                    c = 2
                    for fc in range(NFC):
                        if nb == 2 and fc >= 1:
                            turned_a(fc - 1)
                        split_hi_of(c)
                        split_hi_of(c + 1)
                        c += 2
                        if nb == 1 and fc >= 1:
                            turned_a(fc - 1)
                        act.wait_ge(ga_mm, j * NFC + (fc + 1))
                        if fc >= 3 - nb:
                            act.wait_ge(a_ok, j * NFC + (fc - (2 - nb)))
                        i = blocks_at(nb, fc)
                        act.activation(e_sig[:, i, :], psum[:, i, :], ACT.Sigmoid).then_inc(e_sig_ok, 1)
                        for _ in range(2 * (fc > 0) + 2):
                            split_hi_of(c)
                            c += 1
                    turned_a(NFC - 1)
                    gathered(nb, j + 1)

            gathered(2, 0)
            experts(1, 0, ones)
            experts(2, ones, NE)
            outputs_hi(2, NE)
            for t in range(2):
                std(stats_before[4] + t)

        @block.vector
        def _(dve):
            own = [0]

            def link(ins):
                own[0] += 1
                ins.then_inc(dve_own, 1)
                dve.wait_ge(dve_own, own[0])

            def mod_take(b):
                l, cb = b
                n = mod_at[b]
                dve.wait_ge(mod_sum, n + 1)
                if cb in GATE_BLOCKS:
                    gate = gate1 if cb < 6 else gate2
                    c0 = (cb % 2) * 512
                    dve.tensor_copy(gate[:, 0, c0:c0 + 512], psum[:, 5, :])
                    dve.tensor_copy(gate[:, 1, c0:c0 + 512], psum[:, 6, :]).then_inc(mod_done, 1)
                else:
                    m = {0: 0, 2: 1, 6: 2, 8: 3}[cb - cb % 2]
                    dst = modcol[:, l, m, 4 * (cb % 2):4 * (cb % 2) + 4, :]
                    src = psum[:, 5, 0:8].rearrange("p (k s) -> p k s", s=2)
                    bias = b_cols[:, l, cb, :].unsqueeze(2).to_broadcast([P, 4, 2])
                    if m % 2 == 0:
                        dve.tensor_tensor(dst, src, bias, ALU.add).then_inc(mod_done, 1)
                    else:
                        link(dve.tensor_tensor(dst, src, bias, ALU.add))
                        dve.tensor_scalar(dst, dst, 1.0, None, ALU.add).then_inc(mod_done, 1)

            def normalise(n, src, dst, sig):
                dve.bn_stats(bn[:, 0, :], src[:, 0:512])
                link(dve.bn_stats(bn[:, 1, :], src[:, 512:1024]))
                dve.bn_aggr(ln_mv[:, n % 4, :], bn).then_inc(var_ready, 1)
                dve.wait_ge(std_ready, n + 1)
                link(dve.reciprocal(ln_rstd[:, n % 4:n % 4 + 1], ln_std[:, n % 4:n % 4 + 1]))
                dve.tensor_scalar(dst, src, ln_mv[:, n % 4, 0:1], ln_rstd[:, n % 4:n % 4 + 1],
                                  ALU.subtract, ALU.mult).then_inc(sig, 1)

            def low(dst, src, hi):
                return dve.tensor_tensor(dst, src, hi.bitcast(F32), ALU.subtract)

            def split_lo(q):
                n = split_list[q]
                dve.wait_ge(hi_ok, q + 1)
                size = sum(int(np.prod(shape)) for _, shape, _ in chunks[n][1])
                m = size * 3 // 4
                low(w_lo[:, n % SLOTS, 0:m], ring[:, n % SLOTS, 0:m], w_hi[:, q % HIS, 0:m]).then_inc(lo_dve, 1)

            def modulate(l, which, t, n):
                dve.wait_ge(xn_turned[1], n + 1)
                s, m = t // 2, 2 * (which - 1)
                if (l, which) == (0, 2):
                    cols = slice(t * P, (t + 1) * P)
                    dve.wait_ge(ht_act, n + 1)
                    low(h_lo[:, :, cols], h_mod[:, :, :].rearrange("p a (k n) -> p (a k) n", k=4), h_hi[:, :, cols])\
                        .then_inc(ht_dve, 1)
                    return
                for k in range(4):
                    ins = dve.tensor_scalar(h_t[:, 4 + k, t * P:(t + 1) * P], psum[:, 7, k * P:(k + 1) * P],
                                            modcol[:, l, m + 1, 4 + k, s:s + 1], modcol[:, l, m, 4 + k, s:s + 1],
                                            ALU.mult, ALU.add)
                ins.then_inc(ht_dve, 1)

            def norm_b(use, t, n):
                _, _, tiles = ln_uses[use]
                at_b = tiles_before[use] + t - tiles[0]
                if use:
                    dve.wait_ge(x_new, norms_before[use] + t - tiles[0] + 1)
                if at_b >= 2:
                    dve.wait_ge(xn_turned[1], at_b - 1)
                normalise(n, x_res[:, t, :], xn_of[use][:, t % 2, :], xn_ready)

            def residual(t, dh, y, gate):
                cols = slice(dh * 512, (dh + 1) * 512)
                link(dve.tensor_tensor(reg_r[:, dh, :], y, gate[:, t // 2, cols], ALU.mult))
                link(dve.scalar_tensor_tensor(out=x_res[:, t, cols], in0=x_res[:, t, cols], scalar=ALPHA,
                                              in1=reg_r[:, dh, :], op0=ALU.mult, op1=ALU.add))

            def norm_chain(use, add):
                l, which, tiles = ln_uses[use]
                n = stats_before[use]
                a = norms_before[use]
                turned = []
                for step, t in chain(tiles):
                    if step == "A":
                        add(t)
                        if t - tiles[0] >= 2:
                            dve.wait_ge(x_new, a + t - tiles[0] - 1)
                        normalise(n, x_res[:, t, :], z_of[use][:, t % 2, :], z_scaled)
                    else:
                        norm_b(use, t, n)
                        if t > tiles[0]:
                            modulate(l, which, t - 1, tiles_before[use] + t - 1 - tiles[0])
                    n += 1
                modulate(l, which, tiles[-1], tiles_before[use] + len(tiles) - 1)

            link(dve.memset(c_act[:, :, :], 0.0))
            dve.wait_ge(c_sig, 1)
            dve.tensor_tensor(c_act[:, :, 0:2], c_raw, c_sigm.rearrange("p (k s) -> p k s", s=2), ALU.mult)\
               .then_inc(c_ready, 1)
            for t in range(2):
                dve.wait_ge(x_in[t], 16)
                norm_b(0, t, t)
            for cb in range(6):
                mod_take((0, cb))
            for t in range(2, TT):
                dve.wait_ge(x_in[t], 16)
                norm_b(0, t, t)
                modulate(0, 1, t - 2, t - 2)
            modulate(0, 1, 2, 2)
            modulate(0, 1, 3, 3)

            for l in range(DEPTH):
                a = q0[l]
                dve.wait_ge(in_mm[l], 4)
                dve.tensor_copy(k_rope[64:96, :], psum[64:96, 3, :]).then_inc(in_dve[l], 1)
                for i in range(4):
                    dve.wait_ge(in_mm[l], 5 + i)
                    dve.tensor_copy(u_t[:, i, a:NTOK], psum[:, i, a:NTOK]).then_inc(in_dve[l], 1)
                dve.wait_ge(rms_act[l], 2)
                dve.reciprocal(rms[:, 0, a:NTOK], rms[:, 0, a:NTOK])
                link(dve.reciprocal(rms[:, 1, :], rms[:, 1, :]))
                for k in range(2):
                    dve.tensor_tensor(lat_q[:, k, a:NTOK], lat_q[:, k, a:NTOK], rms[:, 0, a:NTOK], ALU.mult)
                dve.tensor_tensor(lat_kv[:, :], lat_kv[:, :], rms[:, 1, :], ALU.mult).then_inc(lat_done[l], 1)
                dve.wait_ge(kr_perm[l], 1)
                dve.tensor_tensor(rope_a[64:96, :], k_rope[64:96, :], cos[64:96, :], ALU.mult)
                link(dve.tensor_tensor(rope_b[64:96, :], psum[64:96, 6, :], sin[64:96, :], ALU.mult))
                dve.tensor_tensor(k_rope[64:96, :], rope_a[64:96, :], rope_b[64:96, :], ALU.add).then_inc(kr_sum[l], 1)
                dve.wait_ge(kr_sum[l], 1)
                for h in range(4):
                    ins = dve.tensor_copy(k_t[64:96, 0, h, :], k_rope[64:96, :])
                ins.then_inc(kr_done[l], 1)
                units = [(g, s) for g in range(FG) for s in ((0, 1) if l == 0 else (1,))]
                for n, (g, s) in enumerate(units):
                    dve.wait_ge(f2_mm[l], n + 1)
                    dve.tensor_copy(four_t[:, g, s * SEQ:(s + 1) * SEQ], psum[:, 2 + n % 2, 0:SEQ])\
                       .then_inc(f2_dve[l], 1)

                plan, tiles, att = plans[l]
                q_m = splits_before[index_of[("ga", l, 0)]]

                def fill(g, i):
                    if i not in (1, 2, 3, 4, 5):
                        return
                    dve.wait_ge(fill_mm[l], 8 * g + i + 1)
                    b = i % 2
                    if g >= 2 and i == 1:
                        dve.wait_ge(pv_mm[l], len(att) // 4 * (g - 1))
                    if i in (1, 2):
                        dve.tensor_copy(q_t[0:NOPE, g % 2, 2 * (i - 1) + 1, a:NTOK], psum[64:128, b, a:NTOK])\
                           .then_inc(fill_dve[l], 1)
                    elif i in (3, 5):
                        dve.tensor_copy(k_t[0:NOPE, g % 2, 1 if i == 3 else 3, :], psum[64:128, b, :])\
                           .then_inc(fill_dve[l], 1)
                    else:
                        link(dve.tensor_tensor(rope_b[:, a:NTOK], psum[:, b, a:NTOK], sin[:, a:NTOK], ALU.mult))
                        dve.wait_ge(rope_cos[l], g + 1)
                        for h in range(4):
                            rows = slice(32 * h, 32 * h + 32)
                            ins = dve.tensor_tensor(q_t[64:96, g % 2, h, a:NTOK], rope_a[rows, a:NTOK],
                                                    rope_b[rows, a:NTOK], ALU.add)
                        ins.then_inc(fill_dve[l], 1)

                def top_score(c):
                    nk = CTX if tiles[c][4] == 0 else NTOK
                    dve.wait_ge(s_mm[l], c + 1)
                    link(dve.reduce_max(s_top[:, c % 4:c % 4 + 1], psum[:, 2 + c % 2, 0:nk], AX.X))
                    dve.tensor_scalar(s_neg[:, c % 4:c % 4 + 1], s_top[:, c % 4:c % 4 + 1], -SM_SCALE, None,
                                      ALU.mult).then_inc(s_max[l], 1)

                def inverse(c):
                    dve.wait_ge(s_exp[l], c + 1)
                    dve.reciprocal(s_inv[:, c % 4:c % 4 + 1], s_sum[:, c % 4:c % 4 + 1]).then_inc(s_rec[l], 1)

                def values(u):
                    g, pair, s = att[u]
                    dve.wait_ge(pv_mm[l], u + 1)
                    dve.tensor_copy(attn_t[:, 2 * g + pair, s * SEQ:(s + 1) * SEQ], psum[:, 6 + u % 2, 0:SEQ])\
                       .then_inc(pv_out[l], 1)

                for step in plan:
                    if step[0] == "fill":
                        fill(step[1], step[2])
                    elif step[0] == "score":
                        top_score(step[1])
                    elif step[0] == "norm":
                        inverse(step[1])
                        if len(tiles) - step[1] in (9, 5, 1):
                            split_lo(q_m + 2 - (len(tiles) - step[1]) // 4)
                    elif step[0] == "take":
                        values(step[1])

                def merged_lo(jj):
                    dve.wait_ge(mhi_ok[l], jj + 1)
                    low(m_lo[:, 2 * jj:2 * jj + 2, a:NTOK], merged[:, 2 * jj:2 * jj + 2, a:NTOK],
                        m_hi[:, 2 * jj:2 * jj + 2, a:NTOK]).then_inc(mlo_ok[l], 1)

                for k in range(0, KD, 2):
                    dve.wait_ge(ghi_ok[l], k // 2 + 1)
                    low(g_lo[:, k:k + 2, a:NTOK], h_t[:, k:k + 2, a:NTOK], g_hi[:, k:k + 2, a:NTOK])\
                        .then_inc(glo_ok[l], 1)
                q_out = q_m + len(MERGE)
                for u, (kind, jj) in enumerate(MERGE):
                    if u == 8:
                        dve.wait_ge(g_sig[l], 16)
                    if u >= 8:
                        for n in (2 * u, 2 * u + 1):
                            dve.wait_ge(g_mm[l], n + 1)
                            dve.tensor_tensor(gates[:, n - 16, a:NTOK], psum[:, n % 4, a:NTOK], gates[:, n - 16, a:NTOK],
                                              ALU.mult).then_inc(g_mul[l], 1)
                    if u - 1 in MERGE_MOD:
                        mod_take((l, MERGE_MOD[u - 1]))
                    if u < len(O_PARTS):
                        k0, k1 = O_PARTS[u]
                        dve.wait_ge(ohi_ok[l], u + 1)
                        low(o_lo[:, k0:k1, a:NTOK], attn_t[:, k0:k1, a:NTOK], o_hi[u][:, :, a:NTOK])\
                            .then_inc(olo_ok[l], 1)
                    if u == 8:
                        dve.wait_ge(fhi_ok[l], 1)
                        low(f_lo[:, :, a:NTOK], four_t[:, :, a:NTOK], f_hi[:, :, a:NTOK]).then_inc(flo_ok[l], 1)
                    if u >= 13:
                        merged_lo(u - 13)
                    if u == 15:
                        merged_lo(3)
                    split_lo(q_m + u + HIS)
                split_lo(q_out + 3)
                if l == 0:
                    split_lo(q_ffn)
                    split_lo(q_ffn + 1)
                for t in range(t0[l], TT):
                    dve.wait_ge(y_mm[l], t - t0[l] + 1)
                    residual(t, 0, psum[:, 4 + t - t0[l], :], gate1)

                def add_mixer(t):
                    dve.wait_ge(y_mm[l], TT - t0[l] + t - t0[l] + 1)
                    residual(t, 1, psum[:, t - t0[l], :], gate1)

                dve.wait_ge(ln_in[2 * l], 32)
                norm_chain(2 * l + 1, add_mixer)

                if l == 0:
                    split_lo(q_ffn + 2)
                    for fp in range(FT // 2):
                        if 3 <= fp < 9:
                            mod_take((1, fp - 3))
                        for f in (2 * fp, 2 * fp + 1):
                            dve.wait_ge(fg_sig, f + 1)
                            link(dve.tensor_tensor(ff_b[:, 2 + f % 2, :], ff_b[:, f % 2, :], psum[:, f % 2, :],
                                                   ALU.mult))
                            dve.wait_ge(fu_mm, f + 1)
                            dve.tensor_tensor(a_t[:, f, :], ff_b[:, 2 + f % 2, :], psum[:, 2 + f % 2, :], ALU.mult)\
                               .then_inc(fa_done, 1)
                        split_lo(q_ffn + 2 * fp + 3)
                        if 2 * fp + 4 < FT + HIS - 1:
                            split_lo(q_ffn + 2 * fp + 4)
                    q = q_ffn + FT
                    for dh in range(2):
                        for i, (fg, n) in enumerate(DOWN):
                            b = fd_buffer(dh, i)
                            for f in range(fg, fg + n):
                                dve.wait_ge(as_hi, dh * FT + f + 1)
                                low(a_lo[:, b, f - fg, :], a_t[:, f, :], a_hi[:, b, f - fg, :]).then_inc(as_lo, 1)
                            if q + 2 < q_end:
                                split_lo(q + 2)
                            q += 1
                            if dh == 1 and i == 2:
                                for t in range(TT):
                                    dve.wait_ge(fd_mm, t + 1)
                                    residual(t, 0, psum[:, 4 + t, :], gate2)

                    def add_dense(t):
                        dve.wait_ge(fd_mm, TT + t + 1)
                        residual(t, 1, psum[:, t, :], gate2)

                    norm_chain(2, add_dense)

            dve.wait_ge(route_in, 32)
            dve.wait_ge(r_mm, 2)
            for t in range(2):
                link(dve.tensor_tensor(logits[:, t, :], psum[:, t, 0:NE], b_rout, ALU.add))
                link(dve.max(top[:, t, :], logits[:, t, :]))
                link(dve.max_index(top_i[:, t, :].bitcast(U32), top[:, t, :], logits[:, t, :]))
                link(dve.tensor_copy(top_if[:, t, :], top_i[:, t, :].bitcast(U32)))
            dve.tensor_tensor(pair_w[:, :, 0], top[:, :, 1], top[:, :, 0], ALU.subtract).then_inc(r_diff, 1)
            dve.wait_ge(r_exp, 1)
            link(dve.tensor_scalar(pair_w[:, :, 3], pair_w[:, :, 1], 1.0, None, ALU.add))
            link(dve.reciprocal(pair_w[:, :, 2], pair_w[:, :, 3]))
            link(dve.tensor_tensor(pair_w[:, :, 3], pair_w[:, :, 2], pair_w[:, :, 1], ALU.mult))
            for t in range(2):
                for k in range(2):
                    link(dve.tensor_scalar(hot[:, t, k, :], e_num, top_if[:, t, k:k + 1], None, ALU.is_equal))
                link(dve.tensor_scalar(tmp8[:, t, :], hot[:, t, 1, :], pair_w[:, t, 3:4], None, ALU.mult))
                link(dve.scalar_tensor_tensor(out=comb[:, t, :], in0=hot[:, t, 0, :], scalar=pair_w[:, t, 2:3],
                                              in1=tmp8[:, t, :], op0=ALU.mult, op1=ALU.add))
            dve.tensor_tensor(taken[:, :, :], hot[:, :, 0, :], hot[:, :, 1, :], ALU.add).then_inc(r_taken, 1)
            dve.memset(job_at[:, :, :, NE:NE + 1], -1.0)
            dve.memset(job_w[:, :, 0:1], 0.0)
            link(dve.memset(f_acc, 0.0))
            dve.wait_ge(r_taken, 1)
            dve.wait_ge(r_mm, 3)
            for t in range(2):
                dve.scalar_tensor_tensor(out=place[:, t, :], in0=psum[:, 2 + t, 0:NE], scalar=1.0,
                                         in1=taken[:, t, :], op0=ALU.add, op1=ALU.mult)
            link(dve.tensor_scalar(full, psum[:, 4, 0:NE], float(P), None, ALU.is_gt))

            def across(v):
                return v.unsqueeze(1).to_broadcast([P, NE, NE])

            def along(v):
                return v.unsqueeze(2).to_broadcast([P, NE, NE])

            pairs = grid[:, 0, :, :]
            product = grid[:, 1, :, :]
            link(dve.tensor_tensor(pairs, along(e_num), across(e_num), ALU.is_gt))
            link(dve.tensor_tensor(product, pairs, across(full), ALU.mult))
            link(dve.reduce_sum(rank, product, AX.X))
            link(dve.tensor_tensor(n_full, rank[:, NE - 1:NE], full[:, NE - 1:NE], ALU.add))
            dve.tensor_scalar(n_one, n_full, -1.0, float(NE), ALU.mult, ALU.add)
            link(dve.tensor_tensor(stand, e_num, rank, ALU.subtract))
            link(dve.tensor_tensor(rank, rank, stand, ALU.subtract))
            link(dve.scalar_tensor_tensor(out=rank, in0=rank, scalar=n_one, in1=full, op0=ALU.add, op1=ALU.mult))
            link(dve.tensor_tensor(stand, stand, rank, ALU.add))
            link(dve.tensor_tensor(pairs, along(e_num), across(stand), ALU.is_equal))

            link(dve.tensor_tensor(product, pairs, across(e_num), ALU.mult))
            link(dve.reduce_sum(job_e, product, AX.X))
            dve.tensor_copy(job_ei, job_e)
            link(dve.tensor_scalar(n_one, n_one, float(NE - 1), None, ALU.min))
            dve.tensor_copy(n_one_i, n_one).then_inc(route_ready, 1)
            for t in range(2):
                link(dve.tensor_tensor(product, pairs, across(place[:, t, :]), ALU.mult))
                link(dve.reduce_sum(job_at[:, 0, t, 0:NE], product, AX.X))
            dve.tensor_scalar(job_at[:, 1, :, 0:NE], job_at[:, 0, :, 0:NE], -float(P + 1), None, ALU.add)
            link(dve.tensor_scalar(job_at[:, 0, :, 0:NE], job_at[:, 0, :, 0:NE], -1.0, None, ALU.add))
            dve.wait_ge(route_ready, 1)
            ones = dve.value_load(n_one_i[0:1, 0:1], min_val=MIN_ONE, max_val=NE - 1)

            def select(b, j):
                for t in range(2):
                    ins = dve.tensor_scalar(sel_tok[:, b, t, :], iota, job_at[:, b, t, bass.ds(j, 1)], None,
                                            ALU.is_equal)
                return ins

            def gathered(nb, j):
                dve.wait_ge(xg_mm, j + 1)
                src = psum[:, 3:4, :] if nb == 1 else psum[:, 2:4, :]
                for k in range(4):
                    cols = slice(k * P, (k + 1) * P)
                    ins = dve.tensor_scalar(xg_mod[:, 1, 0:nb, cols], src[:, :, cols],
                                            modcol[:, 1, 3, 4 + k, 1:2], modcol[:, 1, 2, 4 + k, 1:2],
                                            ALU.mult, ALU.add)
                ins.then_inc(xd_ok, 1)
                dve.wait_ge(xd_ok, j * 2 + 1)
                hi = [xg_hi[:, 0:nb, 4 * i:4 * i + 4, :].rearrange("p b k n -> p b (k n)") for i in range(2)]
                lo = [xg_lo[:, 0:nb, 4 * i:4 * i + 4, :].rearrange("p b k n -> p b (k n)") for i in range(2)]
                dve.tensor_copy(hi[1], xg_mod[:, 1, 0:nb, :]).then_inc(xd_ok, 1)
                dve.wait_ge(xd_ok, j * 2 + 2)
                low(lo[1], xg_mod[:, 1, 0:nb, :], hi[1])
                dve.wait_ge(xg_act, j + 1)
                low(lo[0], xg_mod[:, 0, 0:nb, :], hi[0]).then_inc(xg_dve, 1)

            def weigh(j):
                n = 0
                for t in range(2):
                    for dh in range(2):
                        dve.wait_ge(sc_mm, j * 4 + (n + 1))
                        acc = f_acc[:, t, dh * 512:(dh + 1) * 512]
                        dve.scalar_tensor_tensor(out=acc, in0=psum[:, 4 + n, :], scalar=job_w[:, t, bass.ds(j, 1)],
                                                 in1=acc, op0=ALU.mult, op1=ALU.add).then_inc(sc_ok, 1)
                        n += 1

            def outputs_lo(nb, j):
                dve.wait_ge(yhi_ok, j + 1)
                low(y_lo[:, 2 - nb:2, :].rearrange("p b n -> p (b n)"),
                    psum[:, 8 - 2 * nb:8, :].rearrange("p b n -> p (b n)"),
                    y_hi[:, 2 - nb:2, :].rearrange("p b n -> p (b n)")).then_inc(y_dve, 1)

            def experts(nb, first, end):
                with dve.Fori(first, end) as j:
                    def split_lo_of(c):
                        q = n_split + c
                        slot = c % E_SLOTS
                        dve.wait_ge(hi_ok, j * JOB_CHUNKS + (q + 1))
                        low(w_lo[:, slot, 0:LO_DVE], e_ring[:, slot, 0:LO_DVE], w_hi[:, q % HIS, 0:LO_DVE])\
                            .then_inc(lo_dve, 1)

                    def turned_a(fc):
                        dve.wait_ge(at_ok, j * NFC + (fc + 1))
                        i = blocks_at(nb, fc)
                        src = psum[:, 4:5, :] if nb == 1 else psum[:, 2:4, :]
                        low(at_lo[:, i, :, :].rearrange("p b f n -> p b (f n)"), src,
                            at_hi[:, i, :, :].rearrange("p b f n -> p b (f n)")).then_inc(at_lo_ok, 1)

                    split_lo_of(0)
                    split_lo_of(1)
                    outputs_lo(nb, j)
                    c = 2
                    for fc in range(NFC):
                        i = blocks_at(nb, fc)
                        if nb == 2 and fc >= 1:
                            turned_a(fc - 1)
                        split_lo_of(c)
                        split_lo_of(c + 1)
                        c += 2
                        if nb == 1 and fc >= 1:
                            turned_a(fc - 1)
                        if fc == 1:
                            dve.wait_ge(st_mm, j + 1)
                            dve.tensor_copy(sel_slot[:, 0:nb, :, :].rearrange("p b t n -> p (b t n)"),
                                            psum[:, 6 - nb, 0:nb * 2 * P]).then_inc(st_ok, 1)
                        dve.wait_ge(e_sig_ok, j * NFC + (fc + 1))
                        dve.tensor_tensor(e_tmp[:, i, :], e_sig[:, i, :], psum[:, i, :], ALU.mult).then_inc(e_tmp_ok, 1)
                        if fc >= 1:
                            split_lo_of(c)
                            split_lo_of(c + 1)
                            c += 2
                        dve.wait_ge(e_tmp_ok, j * NFC + (fc + 1))
                        dve.wait_ge(gu_mm, j * NFC + (fc + 1))
                        if fc >= 3 - nb:
                            dve.wait_ge(at_mm, j * NFC + (fc - (2 - nb)))
                        up = psum[:, 2 + i.start:2 + i.stop, :]
                        dve.tensor_tensor(e_a[:, i, :], e_tmp[:, i, :], up, ALU.mult).then_inc(a_ok, 1)
                        if fc == 0:
                            weigh(j)
                        if fc == 3:
                            for b in range(nb):
                                ins = select(b, j + 1)
                            ins.then_inc(sel_ready, 1)
                        split_lo_of(c)
                        split_lo_of(c + 1)
                        c += 2
                    turned_a(NFC - 1)
                    gathered(nb, j + 1)

            select(0, 0)
            select(1, ones).then_inc(sel_ready, 1)
            dve.memset(psum[:, 6:8, :], 0.0).then_inc(y_zero, 1)
            for b in range(2):
                ins = dve.tensor_copy(sel_slot[:, b, :, :].rearrange("p t n -> p (t n)"), f_acc[:, 0, 0:2 * P])
            ins.then_inc(st_ok, 1)
            for t in range(2):
                link(dve.tensor_tensor(product, pairs, across(comb[:, t, :]), ALU.mult))
                link(dve.reduce_sum(job_w[:, t, 1:NE + 1], product, AX.X))
            gathered(2, 0)
            experts(1, 0, ones)
            dve.memset(psum[:, 4:6, :], 0.0).then_inc(y_zero, 1)
            experts(2, ones, NE)
            outputs_lo(2, NE)
            weigh(NE)
            dve.wait_ge(sc_ok, NE * 4 + 4)
            for t in range(2):
                for dh in range(2):
                    residual(2 + t, dh, f_acc[:, t, dh * 512:(dh + 1) * 512], gate2)
                if t == 0:
                    dve.wait_ge(ln_in[3], 32)
                normalise(stats_before[4] + t, x_res[:, 2 + t, :], z_sb[:, t, :], z_scaled)

        @block.gpsimd
        def _(pool):
            def split_lo(q):
                n = split_list[q]
                pool.wait_ge(hi_ok, q + 1)
                size = sum(int(np.prod(shape)) for _, shape, _ in chunks[n][1])
                a = size * 3 // 4
                pool.tensor_tensor(w_lo[:, n % SLOTS, a:size], ring[:, n % SLOTS, a:size],
                                   w_hi[:, q % HIS, a:size].bitcast(F32), ALU.subtract).then_inc(lo_pool, 1)

            def weights_of(use, t, i):
                n = norms_before[use] + i
                pool.wait_ge(z_scaled, n + 1)
                if i == 0:
                    pool.wait_ge(ln_in[use - 1], 32)
                pool.tensor_tensor(z_of[use][:, t % 2, :], z_of[use][:, t % 2, :], ln_rows[:, 0, :], ALU.mult)\
                    .then_inc(pool_own, 1)
                pool.wait_ge(pool_own, n + 1)
                pool.tensor_tensor(x_res[:, t, :], z_of[use][:, t % 2, :], ln_rows[:, 1, :], ALU.add).then_inc(x_new, 1)

            for l in range(DEPTH):
                a = q0[l]
                pool.wait_ge(kr_sum[l], 1)
                for h in range(4):
                    ins = pool.tensor_copy(k_t[64:96, 1, h, :], k_rope[64:96, :])
                ins.then_inc(kr_copied[l], 1)
                plan, tiles, att = plans[l]
                q_m = splits_before[index_of[("ga", l, 0)]]
                for step in plan:
                    if step[0] == "fill" and step[2] == 4:
                        g = step[1]
                        pool.wait_ge(fill_act[l], act_fills(g, 0))
                        if g >= 1:
                            pool.wait_ge(fill_dve[l], dve_fills(g - 1, 4))
                        pool.tensor_tensor(rope_a[:, a:NTOK], q_rope[:, a:NTOK], cos[:, a:NTOK], ALU.mult)\
                            .then_inc(rope_cos[l], 1)
                    elif step[0] == "norm":
                        c = step[1]
                        nk = CTX if tiles[c][4] == 0 else NTOK
                        pool.wait_ge(s_rec[l], c + 1)
                        pool.tensor_scalar(reg_p[:, c % 3, 0:nk], reg_p[:, c % 3, 0:nk], s_inv[:, c % 4:c % 4 + 1],
                                           1.0, ALU.mult, ALU.mult).then_inc(s_nrm[l], 1)
                        if len(tiles) - c in (9, 5, 1):
                            split_lo(q_m + 2 - (len(tiles) - c) // 4)
                for u, (kind, jj) in enumerate(MERGE):
                    if kind == "fo":
                        pool.wait_ge(g_mul[l], 8 + 2 * jj + 2)
                        for m in (2 * jj, 2 * jj + 1):
                            pool.tensor_tensor(merged[:, m, a:NTOK], gates[:, m, a:NTOK], gates[:, KD + m, a:NTOK],
                                               ALU.add).then_inc(m_done[l], 1)
                    split_lo(q_m + u + HIS)
                split_lo(q_m + len(MERGE) + 3)
                if l == 0:
                    split_lo(q_ffn)
                    split_lo(q_ffn + 1)
                    for t in range(TT):
                        weights_of(1, t, t)
                    for q in range(q_ffn + 2, q_end):
                        split_lo(q)
                    for t in range(TT):
                        weights_of(2, t, t)
                else:
                    for i in range(2):
                        weights_of(3, 2 + i, i)
            pool.wait_ge(route_ready, 1)
            with pool.Fori(0, NE) as j:
                for c in range(JOB_CHUNKS):
                    q = n_split + c
                    slot = c % E_SLOTS
                    pool.wait_ge(hi_ok, j * JOB_CHUNKS + (q + 1))
                    pool.tensor_tensor(w_lo[:, slot, LO_DVE:SLOT], e_ring[:, slot, LO_DVE:SLOT],
                                       w_hi[:, q % HIS, LO_DVE:SLOT].bitcast(F32), ALU.subtract).then_inc(lo_pool, 1)
            for t in range(2):
                weights_of(4, 2 + t, t)


def constants():
    c = np.zeros((P, C_END), np.float64)
    c[:, C_ID:C_ID + P] = np.eye(P)
    k = np.arange(FC)
    ang = 2 * np.pi * ((k[:, None] * k[None, :]) % FC) / FC
    c[:, C_DFTC:C_DFTC + FC] = np.cos(ang) / np.sqrt(FC)
    c[:, C_DFTC + FC:C_DFTC + 2 * FC] = np.sin(ang) / np.sqrt(FC)
    k = np.arange(SEQ)
    ang = 2 * np.pi * ((k[:, None] * k[None, :]) % SEQ) / SEQ
    both = np.stack([np.cos(ang), -np.sin(ang)], 1) / np.sqrt(SEQ)
    c[:, C_DFTT:C_DFTT + 4 * SEQ] = both.reshape(2, P, 2, SEQ).transpose(1, 0, 2, 3).reshape(P, -1)
    nf = ROPE // 4
    pos = np.stack([np.arange(SEQ) // 64, np.arange(SEQ) % 64]).astype(np.float32)
    inv = (1.0 / (np.float32(10000.0) ** (np.arange(nf, dtype=np.float32) / nf))).astype(np.float32)
    ang = (pos[:, None, :] * inv[None, :, None]).astype(np.float32).astype(np.float64)
    ang = np.tile(np.repeat(ang[:, None], 2, axis=1).reshape(ROPE, SEQ), (4, 1))
    c[:, C_COS:C_COS + CTX] = 1.0
    c[:, C_COS + CTX:C_COS + NTOK] = np.cos(ang)
    c[:, C_SIN + CTX:C_SIN + NTOK] = np.sin(ang)
    for m in range(P):
        first = m // nf % 2 == 0
        c[m + nf if first else m - nf, C_PERM + m] = -1.0 if first else 1.0
    for j in range(4):
        c[32 * j, C_SEL] = 1.0
        c[32 * j + 1, C_SEL + 1] = 1.0
    c[:, C_ONE] = 1.0
    c[:, C_EPS] = EPS
    r = np.zeros((P, R_END))
    r[:, R_IOTA:R_IOTA + P] = np.arange(P)[None]
    r[:, R_TRI:R_TRI + P] = np.triu(np.ones((P, P)), 1)
    r[:, R_E:R_E + NE] = np.arange(NE)[None]
    return c.astype(np.float32), r.astype(np.float32)


def small_inputs(c, c_ctx, g_q, g_kv, w_router, b_mod):
    both = np.stack([c_ctx, c[0]], -1).reshape(KD, P, 2).transpose(1, 0, 2).reshape(P, -1)
    gq = g_q.reshape(DEPTH, 2, P).transpose(2, 0, 1).reshape(P, -1)
    gkv = g_kv.reshape(DEPTH, P).T
    router = w_router[0].reshape(KD, P, NE).transpose(1, 0, 2).reshape(P, -1)
    bias = b_mod.reshape(DEPTH * 12 * 4, P).T
    return np.ascontiguousarray(np.concatenate([both, gq, gkv, router, bias], 1))


def query_weights(w_uq):
    v = w_uq.reshape(DEPTH, Q_LORA, 4, 4, QK)
    parts = [v[..., NOPE:].reshape(DEPTH, Q_LORA, 4, -1), v[..., :NOPE].reshape(DEPTH, Q_LORA, 4, -1)]
    return np.ascontiguousarray(np.concatenate(parts, -1).reshape(DEPTH, Q_LORA, -1))


_IN_DRAM = ["x", "ctx", "w_mod", "b_mod", "w_in", "w_uk", "w_uv", "w_ao", "w_fo", "w_out", "ln1_g", "ln1_b",
            "ln2_g", "ln2_b", "w_ff_gate", "w_ff_up", "w_ff_down", "b_router", "w_e_gate", "w_e_up", "w_e_down"]


def kernel(**inputs):
    import concourse.bacc as bacc
    from concourse.bass_utils import run_bass_kernel_spmd

    nc = bacc.Bacc("TRN2", target_bir_lowering=False, num_devices=1, dynamic_dma_scratch_size=1024)
    arrays = {n: np.ascontiguousarray(inputs[n]) for n in _IN_DRAM}
    arrays["const"], arrays["route"] = constants()
    arrays["small"] = small_inputs(*(np.asarray(inputs[n]) for n in ("c", "c_ctx", "g_q", "g_kv", "w_router", "b_mod")))
    arrays["w_uq"] = query_weights(np.asarray(inputs["w_uq"]))
    w = {n: nc.dram_tensor(f"in_{n}", a.shape, F32, kind="ExternalInput").ap() for n, a in arrays.items()}
    out = nc.dram_tensor("out_x", (1, SEQ, D), F32, kind="ExternalOutput").ap()
    build(nc, w, out)
    r = run_bass_kernel_spmd(nc, [{f"in_{n}": a for n, a in arrays.items()}], core_ids=[0])
    return r.results[0]["out_x"]
```
